# Optimizing a Trainium2 kernel written in Bass

```python
import math
import jax, jax.numpy as jnp
from jax import lax
import numpy as np

D_MODEL = 1024
BATCH = 1
SEQ = 512
DEPTH = 1

CONV_DIM = D_MODEL
CONV_KERNEL = 31
SSM_EXPAND = 2
SSM_DIM = SSM_EXPAND * D_MODEL
SSM_HEAD_DIM = 64
SSM_HEADS = SSM_DIM // SSM_HEAD_DIM
SSM_GROUPS = 4
SSM_STATE = 128
SSM_CONV = 4
SSM_CHUNK = 128
SSM_BC = 2 * SSM_GROUPS * SSM_STATE
FFN_DIM = 2816
FFN_CONV = 3
DN_ALPHA = (2 * DEPTH) ** 0.25
DN_BETA = (8 * DEPTH) ** -0.25
LN_EPS = 1e-5
RMS_EPS = 1e-5
IN_SIZES = (2 * CONV_DIM, SSM_DIM, SSM_DIM + SSM_BC, SSM_HEADS, D_MODEL, D_MODEL)
IN_DIM = sum(IN_SIZES)


def layer_norm(x, g, b):
    xf = x.astype(jnp.float32)
    mu = jnp.mean(xf, axis=-1, keepdims=True)
    var = jnp.mean(jnp.square(xf - mu), axis=-1, keepdims=True)
    return ((xf - mu) * lax.rsqrt(var + LN_EPS) * g.astype(jnp.float32)
            + b.astype(jnp.float32)).astype(x.dtype)

def causal_dwconv(x, w, b):
    k = w.shape[0]
    y = lax.conv_general_dilated(
        x, w[:, None, :].astype(x.dtype), window_strides=(1,),
        padding=[(k - 1, 0)], dimension_numbers=("NWC", "WIO", "NWC"),
        feature_group_count=x.shape[-1])
    return y + b.astype(x.dtype)

def split_in(u):
    idx = [int(v) for v in np.cumsum(IN_SIZES)[:-1]]
    return jnp.split(u, idx, axis=-1)

def conformer_branch(u_glu, dw_w, dw_b, ln_g, ln_b, w_out):
    a, g = jnp.split(u_glu, 2, axis=-1)
    v = a * jax.nn.sigmoid(g)
    v = causal_dwconv(v, dw_w, dw_b)
    v = jax.nn.silu(layer_norm(v, ln_g, ln_b))
    return v @ w_out

def ssd_chunked(x, dt, a_head, bm, cm):
    b, t, h, p = x.shape
    g, n = bm.shape[2], bm.shape[3]
    r = h // g
    L = SSM_CHUNK
    c = t // L
    xs = (x * dt[..., None]).reshape(b, c, L, g, r, p)
    a = (dt * a_head).reshape(b, c, L, g, r).transpose(0, 1, 3, 4, 2)
    bc = bm.reshape(b, c, L, g, n)
    cc = cm.reshape(b, c, L, g, n)
    a_cs = jnp.cumsum(a, axis=-1)
    seg = a_cs[..., :, None] - a_cs[..., None, :]
    causal = jnp.tril(jnp.ones((L, L), dtype=bool))
    decay = jnp.where(causal, jnp.exp(jnp.where(causal, seg, 0.0)), 0.0)
    cb = jnp.einsum("bclgn,bcsgn->bcgls", cc, bc)
    y_diag = jnp.einsum("bcgrls,bcsgrp->bclgrp", cb[:, :, :, None] * decay, xs)
    decay_states = jnp.exp(a_cs[..., -1:] - a_cs)
    states = jnp.einsum("bclgn,bcgrl,bclgrp->bcgrpn", bc, decay_states, xs)
    chunk_decay = jnp.exp(a_cs[..., -1])

    def step(carry, inp):
        s_c, d_c = inp
        return d_c[..., None, None] * carry + s_c, carry

    init = jnp.zeros((b, g, r, p, n), states.dtype)
    _, prev = lax.scan(step, init, (jnp.moveaxis(states, 1, 0),
                                    jnp.moveaxis(chunk_decay, 1, 0)))
    prev = jnp.moveaxis(prev, 0, 1)
    y_off = jnp.einsum("bclgn,bcgrpn,bcgrl->bclgrp", cc, prev, jnp.exp(a_cs))
    return (y_diag + y_off).reshape(b, t, h, p)

def ssd_branch(z, xbc, dt_raw, conv_w, conv_b, dt_bias, a_log, d_skip, norm_w, w_out):
    bsz, t, _ = z.shape
    xbc = jax.nn.silu(causal_dwconv(xbc, conv_w, conv_b))
    gn = SSM_GROUPS * SSM_STATE
    xs = xbc[..., :SSM_DIM]
    bm = xbc[..., SSM_DIM:SSM_DIM + gn].reshape(bsz, t, SSM_GROUPS, SSM_STATE)
    cm = xbc[..., SSM_DIM + gn:].reshape(bsz, t, SSM_GROUPS, SSM_STATE)
    dt = jax.nn.softplus(dt_raw.astype(jnp.float32) + dt_bias.astype(jnp.float32))
    a_head = -jnp.exp(a_log.astype(jnp.float32))
    xh = xs.reshape(bsz, t, SSM_HEADS, SSM_HEAD_DIM).astype(jnp.float32)
    y = ssd_chunked(xh, dt, a_head, bm.astype(jnp.float32), cm.astype(jnp.float32))
    y = y + xh * d_skip.astype(jnp.float32)[:, None]
    yg = (y.reshape(bsz, t, SSM_DIM) * jax.nn.silu(z.astype(jnp.float32)))
    yg = yg.reshape(bsz, t, SSM_GROUPS, SSM_DIM // SSM_GROUPS)
    yg = yg * lax.rsqrt(jnp.mean(jnp.square(yg), axis=-1, keepdims=True) + RMS_EPS)
    yn = (yg.reshape(bsz, t, SSM_DIM) * norm_w.astype(jnp.float32)).astype(z.dtype)
    return yn @ w_out

def conv_ffn(h, w_up, dw_w, dw_b, w_down):
    u = causal_dwconv(h @ w_up, dw_w, dw_b)
    gate, val = jnp.split(u, 2, axis=-1)
    return (jax.nn.silu(gate) * val) @ w_down

def first_inputs(seed: int = 0) -> dict:
    key = jax.random.key(seed)
    ks = jax.random.split(key, 32)
    f32 = jnp.float32
    nrm = lambda k, shape, s: (jax.random.normal(k, shape, f32) * s).astype(f32)
    gain = lambda k, shape: 1.0 + 0.05 * jax.random.normal(k, shape, f32)
    small = lambda k, shape: 0.02 * jax.random.normal(k, shape, f32)
    dt0 = jnp.exp(jax.random.uniform(ks[12], (DEPTH, SSM_HEADS), f32)
                  * (math.log(0.1) - math.log(0.001)) + math.log(0.001))
    return {
        "x": jax.random.normal(ks[0], (BATCH, SEQ, D_MODEL), f32),
        "ln_in_g": gain(ks[1], (D_MODEL,)),
        "ln_in_b": small(ks[2], (D_MODEL,)),
        "w_in": nrm(ks[3], (DEPTH, D_MODEL, IN_DIM), D_MODEL ** -0.5),
        "conv_dw_w": nrm(ks[4], (DEPTH, CONV_KERNEL, CONV_DIM), CONV_KERNEL ** -0.5),
        "conv_dw_b": small(ks[5], (DEPTH, CONV_DIM)),
        "conv_ln_g": gain(ks[6], (DEPTH, CONV_DIM)),
        "conv_ln_b": small(ks[7], (DEPTH, CONV_DIM)),
        "w_conv_out": nrm(ks[8], (DEPTH, CONV_DIM, D_MODEL), DN_BETA * CONV_DIM ** -0.5),
        "ssm_conv_w": nrm(ks[9], (DEPTH, SSM_CONV, SSM_DIM + SSM_BC), SSM_CONV ** -0.5),
        "ssm_conv_b": small(ks[10], (DEPTH, SSM_DIM + SSM_BC)),
        "ssm_dt_bias": dt0 + jnp.log(-jnp.expm1(-dt0)),
        "ssm_a_log": jnp.log(jax.random.uniform(ks[13], (DEPTH, SSM_HEADS), f32, 1.0, 16.0)),
        "ssm_d": gain(ks[14], (DEPTH, SSM_HEADS)),
        "ssm_norm_w": gain(ks[15], (DEPTH, SSM_DIM)),
        "w_ssm_out": nrm(ks[16], (DEPTH, SSM_DIM, D_MODEL), DN_BETA * SSM_DIM ** -0.5),
        "w_o": nrm(ks[17], (DEPTH, D_MODEL, D_MODEL), DN_BETA * D_MODEL ** -0.5),
        "ln1_g": gain(ks[18], (DEPTH, D_MODEL)),
        "ln1_b": small(ks[19], (DEPTH, D_MODEL)),
        "w_ffn_up": nrm(ks[20], (DEPTH, D_MODEL, 2 * FFN_DIM), DN_BETA * D_MODEL ** -0.5),
        "ffn_dw_w": nrm(ks[21], (DEPTH, FFN_CONV, 2 * FFN_DIM), FFN_CONV ** -0.5),
        "ffn_dw_b": small(ks[22], (DEPTH, 2 * FFN_DIM)),
        "w_ffn_down": nrm(ks[23], (DEPTH, FFN_DIM, D_MODEL), DN_BETA * FFN_DIM ** -0.5),
        "ln2_g": gain(ks[24], (DEPTH, D_MODEL)),
        "ln2_b": small(ks[25], (DEPTH, D_MODEL)),
    }

def first_block(x, ln_in_g, ln_in_b, w_in, conv_dw_w, conv_dw_b, conv_ln_g, conv_ln_b,
              w_conv_out, ssm_conv_w, ssm_conv_b, ssm_dt_bias, ssm_a_log, ssm_d,
              ssm_norm_w, w_ssm_out, w_o, ln1_g, ln1_b, w_ffn_up, ffn_dw_w, ffn_dw_b,
              w_ffn_down, ln2_g, ln2_b):
    h = layer_norm(x, ln_in_g, ln_in_b)
    for l in range(DEPTH):
        u = h @ w_in[l]
        u_glu, z, xbc, dt_raw, gate_a, gate_b = split_in(u)
        y_a = conformer_branch(u_glu, conv_dw_w[l], conv_dw_b[l], conv_ln_g[l],
                               conv_ln_b[l], w_conv_out[l])
        y_b = ssd_branch(z, xbc, dt_raw, ssm_conv_w[l], ssm_conv_b[l], ssm_dt_bias[l],
                         ssm_a_log[l], ssm_d[l], ssm_norm_w[l], w_ssm_out[l])
        mix = (jax.nn.sigmoid(gate_a) * y_a + jax.nn.sigmoid(gate_b) * y_b) @ w_o[l]
        h = layer_norm(DN_ALPHA * h + mix, ln1_g[l], ln1_b[l])
        ffn = conv_ffn(h, w_ffn_up[l], ffn_dw_w[l], ffn_dw_b[l], w_ffn_down[l])
        h = layer_norm(DN_ALPHA * h + ffn, ln2_g[l], ln2_b[l])
    return h


DEPTH_2 = 2

N_META = 16
MIX_WIDTH = D_MODEL
ATTN_WIDTH = MIX_WIDTH // 2
CONV_WIDTH = MIX_WIDTH - ATTN_WIDTH
HEAD_DIM = 64
N_Q_HEADS = ATTN_WIDTH // HEAD_DIM
N_KV_HEADS = 2
GROUP = N_Q_HEADS // N_KV_HEADS
KV_WIDTH = N_KV_HEADS * HEAD_DIM
CONV_GROUPS = 8
CONV_K = 3
WINDOW = 128
BLOCK = 128
LEAD_PAD = BLOCK - N_META
ROPE_THETA = 500000.0
ROT_DIM = HEAD_DIM // 4
D_FF = 4 * D_MODEL
IN_WIDTH = ATTN_WIDTH + 2 * KV_WIDTH + 3 * CONV_WIDTH
EPS = 1e-6


def rmsnorm(x, g):
    x32 = x.astype(jnp.float32)
    y = x32 * lax.rsqrt(jnp.mean(x32 * x32, axis=-1, keepdims=True) + EPS)
    return y.astype(x.dtype) * g.astype(x.dtype)

def rope_tables(n_pos):
    pos = jnp.arange(n_pos, dtype=jnp.float32)
    inv_freq = jnp.power(jnp.float32(ROPE_THETA), -jnp.arange(0, ROT_DIM, 2, dtype=jnp.float32) / ROT_DIM)
    ang = pos[:, None] * inv_freq[None, :]
    return jnp.cos(ang), jnp.sin(ang)

def partial_rope(t, cos, sin):
    half = ROT_DIM // 2
    t32 = t[..., :ROT_DIM].astype(jnp.float32)
    t1, t2 = t32[..., :half], t32[..., half:]
    c, s = cos[None, :, None, :], sin[None, :, None, :]
    rot = jnp.concatenate([t1 * c - t2 * s, t2 * c + t1 * s], axis=-1).astype(t.dtype)
    return jnp.concatenate([rot, t[..., ROT_DIM:]], axis=-1)

def sliding_window_gqa_sinks(q, k, v, sink):
    bsz, L = q.shape[0], q.shape[1]
    pad = ((0, 0), (LEAD_PAD, 0), (0, 0), (0, 0))
    q, k, v = jnp.pad(q, pad), jnp.pad(k, pad), jnp.pad(v, pad)
    Lp = L + LEAD_PAD
    nb = Lp // BLOCK
    qb = q.reshape(bsz, nb, BLOCK, N_KV_HEADS, GROUP, HEAD_DIM)

    def band(t):
        tb = t.reshape(bsz, nb, BLOCK, N_KV_HEADS, HEAD_DIM)
        prev = jnp.pad(tb, ((0, 0), (1, 0), (0, 0), (0, 0), (0, 0)))[:, :-1]
        return jnp.concatenate([prev, tb], axis=2)

    kw, vw = band(k), band(v)
    s = jnp.einsum('bnqhgd,bnkhd->bnhgqk', qb, kw,
                   preferred_element_type=jnp.float32) * (HEAD_DIM ** -0.5)
    blk = jnp.arange(nb)[:, None, None]
    qpos = blk * BLOCK + jnp.arange(BLOCK)[None, :, None]
    kpos = (blk - 1) * BLOCK + jnp.arange(2 * BLOCK)[None, None, :]
    mask = (kpos <= qpos) & (qpos - kpos < WINDOW) & (kpos >= LEAD_PAD)
    s = jnp.where(mask[None, :, None, None], s, -jnp.inf)
    sk = sink.astype(jnp.float32).reshape(1, 1, N_KV_HEADS, GROUP, 1, 1)
    m = jnp.maximum(jnp.max(s, axis=-1, keepdims=True), sk)
    e = jnp.exp(s - m)
    p = e / (jnp.sum(e, axis=-1, keepdims=True) + jnp.exp(sk - m))
    o = jnp.einsum('bnhgqk,bnkhd->bnqhgd', p.astype(v.dtype), vw)
    return o.reshape(bsz, Lp, N_Q_HEADS * HEAD_DIM)[:, LEAD_PAD:]

def short_gated_conv(b_gate, c_gate, h, w):
    u = c_gate * h
    y = lax.conv_general_dilated(u, w[:, None, :].astype(u.dtype), window_strides=(1,),
                                 padding=[(CONV_K - 1, 0)],
                                 dimension_numbers=('NWC', 'WIO', 'NWC'),
                                 feature_group_count=CONV_WIDTH)
    return b_gate * y

def second_inputs(seed: int = 0) -> dict:
    key = jax.random.key(seed)
    ks = jax.random.split(key, 16)
    f32 = jnp.float32

    def nrm(k, shape, scale):
        return jax.random.normal(k, shape, f32) * scale

    def gain(k, shape):
        return 1.0 + 0.05 * jax.random.normal(k, shape, f32)

    return {
        'x': nrm(ks[0], (BATCH, SEQ, D_MODEL), 1.0),
        'meta_tokens': nrm(ks[1], (N_META, D_MODEL), 1.0),
        'mix_pre_g': gain(ks[2], (DEPTH_2, D_MODEL)),
        'w_in': nrm(ks[3], (DEPTH_2, D_MODEL, IN_WIDTH), D_MODEL ** -0.5),
        'conv_w': nrm(ks[4], (DEPTH_2, CONV_K, CONV_WIDTH), CONV_K ** -0.5),
        'sinks': nrm(ks[5], (DEPTH_2, N_Q_HEADS), 0.5),
        'attn_out_g': gain(ks[6], (DEPTH_2, ATTN_WIDTH)),
        'conv_out_g': gain(ks[7], (DEPTH_2, CONV_WIDTH)),
        'w_out': nrm(ks[8], (DEPTH_2, MIX_WIDTH, D_MODEL), MIX_WIDTH ** -0.5),
        'mix_post_g': gain(ks[9], (DEPTH_2, D_MODEL)),
        'mlp_pre_g': gain(ks[10], (DEPTH_2, D_MODEL)),
        'w_up': nrm(ks[11], (DEPTH_2, D_MODEL, D_FF), D_MODEL ** -0.5),
        'w_down': nrm(ks[12], (DEPTH_2, D_FF, D_MODEL), D_FF ** -0.5),
        'mlp_post_g': gain(ks[13], (DEPTH_2, D_MODEL)),
    }

def second_block(x, meta_tokens, mix_pre_g, w_in, conv_w, sinks, attn_out_g, conv_out_g,
              w_out, mix_post_g, mlp_pre_g, w_up, w_down, mlp_post_g):
    bsz = x.shape[0]
    meta = jnp.broadcast_to(meta_tokens[None].astype(x.dtype), (bsz, N_META, D_MODEL))
    h = jnp.concatenate([meta, x], axis=1)
    L = h.shape[1]
    cos, sin = rope_tables(L)
    s_q = ATTN_WIDTH
    s_k = s_q + KV_WIDTH
    s_v = s_k + KV_WIDTH
    s_b = s_v + CONV_WIDTH
    s_c = s_b + CONV_WIDTH
    for l in range(DEPTH_2):
        a = rmsnorm(h, mix_pre_g[l])
        proj = a @ w_in[l]
        q = proj[..., :s_q].reshape(bsz, L, N_Q_HEADS, HEAD_DIM)
        k = proj[..., s_q:s_k].reshape(bsz, L, N_KV_HEADS, HEAD_DIM)
        v = proj[..., s_k:s_v].reshape(bsz, L, N_KV_HEADS, HEAD_DIM)
        b_gate = proj[..., s_v:s_b]
        c_gate = proj[..., s_b:s_c]
        hc = proj[..., s_c:]
        q = partial_rope(q, cos, sin)
        k = partial_rope(k, cos, sin)
        y_attn = sliding_window_gqa_sinks(q, k, v, sinks[l])
        y_conv = short_gated_conv(b_gate, c_gate, hc, conv_w[l])
        y = jnp.concatenate([rmsnorm(y_attn, attn_out_g[l]),
                             rmsnorm(y_conv, conv_out_g[l])], axis=-1)
        h = h + rmsnorm(y @ w_out[l], mix_post_g[l])
        a = rmsnorm(h, mlp_pre_g[l])
        f = jnp.square(jax.nn.relu(a @ w_up[l])) @ w_down[l]
        h = h + rmsnorm(f, mlp_post_g[l])
    return h[:, N_META:]


def setup_inputs(seed=0):
    out = dict(first_inputs(seed))
    for name, value in second_inputs(seed + 1).items():
        if name != "x":
            out[name + "_2"] = value
    return out


def reference(
    x, ln_in_g, ln_in_b, w_in, conv_dw_w, conv_dw_b, conv_ln_g, conv_ln_b, w_conv_out,
    ssm_conv_w, ssm_conv_b, ssm_dt_bias, ssm_a_log, ssm_d, ssm_norm_w, w_ssm_out, w_o, ln1_g,
    ln1_b, w_ffn_up, ffn_dw_w, ffn_dw_b, w_ffn_down, ln2_g, ln2_b, meta_tokens_2, mix_pre_g_2,
    w_in_2, conv_w_2, sinks_2, attn_out_g_2, conv_out_g_2, w_out_2, mix_post_g_2, mlp_pre_g_2,
    w_up_2, w_down_2, mlp_post_g_2,
):
    x = first_block(
        x, ln_in_g, ln_in_b, w_in, conv_dw_w, conv_dw_b, conv_ln_g, conv_ln_b, w_conv_out,
        ssm_conv_w, ssm_conv_b, ssm_dt_bias, ssm_a_log, ssm_d, ssm_norm_w, w_ssm_out, w_o,
        ln1_g, ln1_b, w_ffn_up, ffn_dw_w, ffn_dw_b, w_ffn_down, ln2_g, ln2_b,
    )
    return second_block(
        x, meta_tokens_2, mix_pre_g_2, w_in_2, conv_w_2, sinks_2, attn_out_g_2, conv_out_g_2,
        w_out_2, mix_post_g_2, mlp_pre_g_2, w_up_2, w_down_2, mlp_post_g_2,
    )


_drawn_inputs = setup_inputs


def setup_inputs(seed=0):
    import zlib

    import numpy as np

    out = dict(_drawn_inputs(seed))
    spreads = {}
    factors = {'conv_dw_b': 4.177,
     'conv_ln_g': 3.74,
     'conv_ln_b': 7.72,
     'ssm_conv_b': 6.191,
     'ssm_d': 6.994,
     'ssm_norm_w': 3.715,
     'ffn_dw_b': 6.411,
     'sinks_2': 8.0}
    for name, (base, spread) in spreads.items():
        noise = np.random.default_rng([zlib.crc32(name.encode()), seed]).standard_normal(out[name].shape)
        drawn = base * np.exp(spread * noise) if base else spread * noise
        out[name] = __import__('jax').numpy.asarray(drawn.astype(out[name].dtype))
    for name, factor in factors.items():
        out[name] = (out[name] * factor).astype(out[name].dtype)
    return out
```

```python
import math
from contextlib import ExitStack

import numpy as np
import concourse.bass as bass
from concourse import mybir

F32 = mybir.dt.float32
F32R = mybir.dt.float32r
ALU = mybir.AluOpType
ACT = mybir.ActivationFunctionType
AX_X = mybir.AxisListType.X

P = 128
D = 1024
KD = D // P
T = 512
SSM = 2 * D
HEADS, HEAD_P = SSM // 64, 64
GROUPS, STATE, CHUNK = 4, 128, 128
CHUNKS = T // CHUNK
GH = HEADS // GROUPS
GP = GH // 2
XBC = SSM + 2 * GROUPS * STATE
XT, BT0, CT0, XBCT = SSM // P, SSM // P, SSM // P + GROUPS, XBC // P
TAPS = 31
FFN = 2816
FT = FFN // P
ALPHA = 2.0 ** 0.25
LAYERS = 2
META = 16
L = T + META
HALF = L // 2
WIN = 128
NB = 5
LEAD = WIN - META
QPAD = NB * WIN
KPAD = QPAD + WIN
QH = 8
FF = 4 * D
FFH = FF // P // 2
ROT, THETA = 16, 500000.0
NEG = -1.0e30
UNIT = 16 * P


class Stage:

    def __init__(self, name, u0, first_tiles, n, nm, nk):
        self.name, self.u0, self.z0, self.n, self.nm, self.nk = name, u0, first_tiles, n, nm, nk

    def slot(self, s):
        return (self.u0 + s) % 2

    def used(self, i, s):
        return (self.u0 + s) // 2 + i


def make_plan():
    plan, u, z = {}, 0, 0
    first = [("dt", 1, 1, KD), ("xbc", XBCT // 2, 2, KD), ("glu", KD, 2, KD), ("z", XT // 2, 2, KD),
             ("gate_b", KD // 2, 2, KD), ("ssm_out", KD, 1, XT), ("gate_a", KD // 2, 2, KD),
             ("conv_out", KD // 2, 2, KD), ("w_o", KD // 2, 2, KD), ("ffn_up", FT, 2, KD),
             ("ffn_down", 2 * KD, 1, FT // 2)]
    layer = [("in", 9, 2, KD), ("out", KD // 2, 2, KD), ("up0", FFH // 2, 2, KD), ("down0", KD, 1, FFH),
             ("up1", FFH // 2, 2, KD), ("down1", KD, 1, FFH)]
    for name, n, nm, nk in first + [(f"{a}_{l}", n, nm, nk) for l in range(LAYERS) for a, n, nm, nk in layer]:
        plan[name] = Stage(name, u, z, n, nm, nk)
        u += n
        z += n if nm == 2 else 0
    return plan, u


PLAN, UNITS = make_plan()

COLS = {}


def _place_cols():
    at = 0
    for name, n in [("ln_in_g", KD), ("ln_in_b", KD), ("conv_w", KD * TAPS), ("conv_b", KD), ("conv_ln_g", KD),
                    ("conv_ln_b", KD), ("ssm_w", XBCT * 4), ("ssm_b", XBCT), ("ssm_d", XT), ("ssm_norm", XT),
                    ("ln1_g", KD), ("ln1_b", KD), ("ffn_w", 2 * FT * 3), ("ffn_b", 2 * FT), ("ln2_g", KD),
                    ("ln2_b", KD)] + [(f"{a}_{l}", n) for l in range(LAYERS) for a, n in
                                      [("mix_pre", KD), ("conv2_w", 4 * 3), ("attn_g", 4), ("conv_g", 4),
                                       ("mix_post", KD), ("mlp_pre", KD), ("mlp_post", KD), ("sinks", QH)]] + [
                   ("eps5", 1), ("eps6", 1)]:
        COLS[name] = (at, n)
        at += n
    return at


NCOLS = _place_cols()
CONST1 = {"ident": 0, "ones": 128, "causal": 256, "last": 384}
N1 = 512
CONST2 = {"rope_p": 0, "cos": 128, "sin": 128 + L, "mask": 128 + 2 * L}
N2 = 128 + 2 * L + NB * 256


def build(nc, xT, metaT, wstream, cols_d, heads_d, const1_d, const2_d, acs_d, outT):
    ctx = ExitStack()
    with ctx:
        sems = {}

        def sem(name):
            sems[name] = ctx.enter_context(nc.semaphore(name))
            return sems[name]

        top = [1152]

        def fixed(name, n, dt=F32):
            at = top[0]
            top[0] += 4 * n
            return nc.alloc_sbuf_tensor_at(name, [P, n], dt, offset=at)

        const1 = fixed("const1", N1)
        cols = fixed("cols", NCOLS + (-NCOLS) % 8)
        raw = [fixed(f"raw{s}", UNIT) for s in range(2)]
        whi = [fixed(f"whi{s}", UNIT, F32R) for s in range(2)]
        wlo = [fixed(f"wlo{s}", UNIT, F32R) for s in range(2)]
        ahi = fixed("ahi", KD * L, F32R)
        alo = fixed("alo", KD * L, F32R)
        mu, std, rstd = fixed("mu", L), fixed("std", L), fixed("rstd", L)
        R = top[0]
        R_END = 228200 // 32 * 32

        def at(name, off, n, dt=F32, parts=P):
            assert R + off + 4 * n <= R_END, (name, R + off + 4 * n - R_END)
            return nc.alloc_sbuf_tensor_at(name, [parts, n], dt, offset=R + off)

        TB = 4 * T
        H0 = (R_END - R - 4 * KD * L) // 32 * 32
        x_in = at("x_in", 32 * TB, KD * T)
        xbc = at("xbc", 0, XBCT * T)
        ssd0 = 24 * TB
        xdt = at("xdt", ssd0, 4 * T)
        xds = at("xds", ssd0 + 4 * TB, 3 * T)
        st = at("st", ssd0 + 7 * TB, 3 * T)
        b_slot = at("b_slot", ssd0 + 10 * TB, T)
        bt_sb = at("bt_sb", ssd0 + 11 * TB, T)
        x_slot = [at(f"x_slot{s}", ssd0 + (12 + s) * TB, T) for s in range(2)]
        acs_b = [at(f"acs_b{s}", ssd0 + (14 + s) * TB, T) for s in range(2)]
        m_slot = [at(f"m_slot{s}", ssd0 + (16 + s) * TB, T) for s in range(2)]
        c_slot = [at(f"c_slot{s}", ssd0 + (18 + s) * TB, T) for s in range(2)]
        tok = at("tok", ssd0 + 20 * TB, 256)
        ends = at("ends", ssd0 + 20 * TB + 1024, 256)
        dtt = [at(f"dtt{s}", ssd0 + (21 + s) * TB, T, parts=32) for s in range(8)]
        heads = at("heads", ssd0 + 29 * TB, 8, parts=32)
        yn_lo = at("yn_lo", 0, XT * T, F32R)
        yn_hi = at("yn_hi", 16 * TB, XT * T, F32R)
        VW = T + TAPS - 1
        v0 = 32 * TB
        vpad = at("vpad", v0, KD * VW)
        vo0 = v0 + 4 * KD * VW + (-4 * KD * VW) % 64
        vout = at("vout", vo0, KD * T)
        gb0 = vo0 + 8 * TB
        gb = at("gb", gb0, KD * T)
        t0 = gb0 + 8 * TB
        sig = [at(f"sig{s}", t0 + s * TB, T) for s in range(2)]
        sumsq = at("sumsq", t0, 4 * T)
        zs = [at(f"zs{s}", t0 + (4 + s) * TB, T) for s in range(2)]
        ysq = [at(f"ysq{s}", t0 + (6 + s) * TB, T) for s in range(2)]
        yv = at("yv", t0, 4 * T)
        rst4 = at("rst4", t0 + 4 * TB, 4 * T)
        sq1 = [at(f"sq1{s}", t0 + s * TB, T) for s in range(2)]
        ga = at("ga", 8 * TB, KD * T)
        chi = at("chi", 16 * TB, KD * T, F32R)
        clo = at("clo", 0, KD * T, F32R)
        mixhi = at("mixhi", 24 * TB, KD * T, F32R)
        mixlo = at("mixlo", v0, KD * T, F32R)
        res1 = at("res1", vo0, KD * T)
        fhi = at("fhi", 0, FT * T, F32R)
        flo = at("flo", FT * TB, FT * T, F32R)
        fg = [[at(f"fg{s}{m}", (2 * FT + 2 * s + m) * TB, T) for m in range(2)] for s in range(2)]
        res2 = at("res2", (2 * FT + 4) * TB, KD * T)
        sq2 = [at(f"sq2{s}", (2 * FT + s) * TB, T) for s in range(2)]
        assert (2 * FT + 4 + KD) * TB <= H0
        LB = 4 * L
        hres = at("hres", H0, KD * L)
        const2 = at("const2", 0, N2)
        q0 = 4 * N2 + (-4 * N2) % 64
        qpad = at("qpad", q0, 4 * QPAD)
        kpad = at("kpad", q0 + 16 * QPAD, KPAD)
        vch = at("vch", q0 + 16 * QPAD + 4 * KPAD, KPAD)
        vtok = at("vtok", q0 + 16 * QPAD + 8 * KPAD, KPAD)
        c0 = q0 + 16 * QPAD + 12 * KPAD
        qraw = at("qraw", c0, 5 * L)
        yconv = at("yconv", c0 + 5 * LB, 4 * L)
        UP = L + 8
        cgate = [at(f"cgate{s}", c0 + 9 * LB + s * LB, L) for s in range(2)]
        upad = [at(f"upad{s}", c0 + 11 * LB + 4 * s * UP, UP) for s in range(2)]
        rot = at("rot", c0 + 11 * LB + 8 * UP, 2 * L)
        a0 = c0 + 13 * LB + 8 * UP
        q_slot = at("q_slot", c0, 4 * WIN)
        k_slot = at("k_slot", c0 + 2048, 2 * WIN)
        v_slot = at("v_slot", c0 + 3072, 2 * WIN)
        sc = [at(f"sc{z}", a0 + 8192 * z, 1024) for z in range(2)]
        pT = [at(f"pT{z}", a0 + 8192 * z + 4096, 1024) for z in range(2)]
        small = at("small", c0 + 4096, 64)
        y_tok = at("y_tok", a0 + 16384, NB * 512)
        y_n = at("y_n", c0 + 9 * LB, 512)
        ya = at("ya", q0, 4 * QPAD)
        zres = at("zres", 0, KD * L)
        f2hi = at("f2hi", KD * LB, FFH * L, F32R)
        f2lo = at("f2lo", (KD + FFH) * LB, FFH * L, F32R)
        rl = [at(f"rl{s}", (KD + 2 * FFH + s) * LB, L) for s in range(4)]
        sq3 = [at(f"sq3{s}", a0 + 26624 + s * LB, L) for s in range(2)]
        nv = [at(f"nv{s}", a0 + 26624 + (2 + s) * LB, L) for s in range(2)]
        assert a0 + 26624 + 4 * LB <= H0, a0 + 26624 + 4 * LB - H0
        assert (KD + 2 * FFH + 4) * LB <= H0

        PS = ctx.enter_context(nc.psum_tensor("PS", [P, 8 * 512], F32))

        def bank(b, n=512, off=0, parts=P):
            return PS[0:parts, b * 512 + off:b * 512 + off + n]

        def wide(b):
            return PS[:, b * 512:(b + 2) * 512].rearrange("p (a c) -> p a c", a=2)[:, :, 0:HALF]

        def split2(ap):
            return ap.rearrange("p (a c) -> p a c", a=2)

        def col(name, k):
            a = COLS[name][0]
            if isinstance(k, int):
                return cols[:, a + k:a + k + 1]
            return cols[:, bass.ds(k + a, 1)]

        def cut(t, start, n):
            return t[:, start:start + n] if isinstance(start, int) else t[:, bass.ds(start, n)]

        ident, ones = const1[:, 0:128], const1[:, 128:256]
        causal, last_row = const1[:, 256:384], const1[:, 384:512]

        params_in, x_in_s, meta_in, const2_in = sem("params_in"), sem("x_loaded"), sem("meta_in"), sem("const2_in")
        raw_in = [sem(f"raw_in{s}") for s in range(2)]
        hi_ready, lo_ready = sem("whi_ready"), sem("wlo_ready")
        unit_done, tile0_done = sem("unit_done"), sem("tile0_done")
        psum_free = [sem(f"psum_free{s}") for s in range(2)]
        out_done = sem("out_done")
        turn = {e: sem(f"turn_{e}") for e in ("pe", "act", "dve", "pool", "sp")}

        class Counter:

            def __init__(self, s, base=0):
                self.sem, self.base = s, base

        def norm_sems(name, what="pe act dve hi lo"):
            return {a: sem(f"{name}_{a}") for a in what.split()}

        def after(eng, counter, value):
            eng.wait_ge(counter.sem, value + counter.base)

        n_in, n_conv, n_1, n_2 = ({a: Counter(s) for a, s in norm_sems(name).items()}
                                  for name in ("ln_in", "ln_conv", "ln1", "ln2"))
        dt_exp, dt_ready, dt_ps, dt_tok, end_ps, end_in, ends_ok = (
            sem(a) for a in ("dt_exp", "dt_ready", "dt_tok_ps", "dt_tok", "end_ps", "end_in", "ends_ok"))
        conv4_acc, conv4_tap, conv4_out = sem("conv4_acc"), sem("conv4_tap"), sem("conv4_out")
        scratch_in = sem("acs_stored")
        acs_in = [sem(f"acs_in{s}") for s in range(2)]
        (b_ok, bt_ps, bt_ok, cb_ps, x_ok, xt_ps, xdt_ok, xds_ok, st_ps, st_ok, seg_ok, exp_ok, mc_ok, y_mm, y_ok) = (
            sem(a) for a in ("b_ok", "bt_ps", "bt_ok", "cb_ps", "x_ok", "xt_ps", "xdt_ok", "xds_ok", "st_ps",
                             "st_ok", "seg_ok", "exp_ok", "mc_ok", "y_mm", "y_ok"))
        sig_ok, v_ok = sem("sig_ok"), sem("glu_used")
        zs_ok, yg_ok, ysq_ok, ysq_sum = sem("zs_ok"), sem("yg_ok"), sem("ysq_ok"), sem("ysq_sum")
        ss_ps, ss_std, ss_rstd = sem("ss_ps"), sem("ss_std"), sem("ss_rstd")
        yv_ok, yhi_ok, ylo_ok = sem("yv_ok"), sem("yhi_ok"), sem("ylo_ok")
        vout_ok = sem("vout_ok")
        mix_ok, mixhi_ok, mixlo_ok = sem("mix_ok"), sem("mixhi_ok"), sem("mixlo_ok")
        r1_ok, r2_ok = sem("r1_ok"), sem("r2_ok")
        fa_ok, ft_ok, fs_ok, ff_ok, fhi_ok, flo_ok = (sem(a) for a in ("ffn_acc", "ffn_tap0", "ffn_silu", "ffn_prod",
                                                                      "ffn_hi", "ffn_lo"))

        per_layer = {
            "in_c": 4, "in_u": 4, "swap_ps": 5, "rope_ok": 5, "v_ps": 1, "v_ok": 1, "slot_ok": NB, "sc_ps": 2 * NB,
            "neg_ok": 2 * NB, "p_ok": 2 * NB, "pt_ps": 2 * NB, "pt_ok": 2 * NB, "o_ps": 2 * NB, "o_ok": 2 * NB,
            "astd_ok": 1, "yn_ok": NB, "yt_ps": NB, "ya_ok": NB, "zc_ok": 2, "pad_ok": 1, "dn_ok1": KD,
            "rl_ok0": FFH // 2, "f_ok0": FFH, "f2hi_ok0": FFH, "f2lo_ok0": FFH,
            "rl_ok1": FFH // 2, "f_ok1": FFH, "f2hi_ok1": FFH, "f2lo_ok1": FFH}
        norms = {"pre": (KD, "pe act dve hi lo"), "conv": (4, "pe act dve hi lo"), "attn": (4, "dve hi lo"),
                 "post": (KD, "pe act dve"), "mpre": (KD, "pe act dve hi lo"), "mpost": (KD, "pe act dve")}
        layer_sems = {a: sem(a) for a in per_layer}
        norm_sem = {a: norm_sems(a, what) for a, (_, what) in norms.items()}

        def layer_counters(l):
            y = {a: Counter(layer_sems[a], l * n) for a, n in per_layer.items()}
            for a, (nk, _) in norms.items():
                y["n_" + a] = {e: Counter(s, l * (nk + (e == "act"))) for e, s in norm_sem[a].items()}
            return y

        layers = [layer_counters(l) for l in range(LAYERS)]

        block = ctx.enter_context(nc.Block())

        def hold(eng, s, value, who):
            if isinstance(s, Counter):
                s, value = s.sem, value + s.base
            if isinstance(value, int):
                assert value >= 0
                if value > 0:
                    eng.wait_ge(s, value)
            else:
                eng.wait_ge(s, value)
                eng.sem_inc(turn[who])

        def unit_loop(eng, stage, body, tail=0):
            pairs = (stage.n - tail) // 2
            if pairs > 0:
                with eng.Fori(0, pairs) as i:
                    for s in range(2):
                        body(i, s)
            for u in range(2 * pairs, stage.n):
                body(u // 2, u % 2)

        @block.sync
        def _(sp):
            sp.dma_start(const1[:, :], const1_d).then_inc(params_in, 16)
            sp.dma_start(cols[:, 0:NCOLS], cols_d).then_inc(params_in, 16)
            sp.dma_start(heads[:, 0:2], heads_d).then_inc(params_in, 16)
            sp.dma_start(x_in[:, :], xT).then_inc(x_in_s, 16)
            for s in range(2):
                sp.dma_start(raw[s][:, :], wstream[s]).then_inc(raw_in[s], 16)
            with sp.Fori(1, UNITS // 2) as i:
                for s in range(2):
                    sp.wait_ge(lo_ready, 2 * i + s - 1)
                    sp.dma_start(raw[s][:, :], wstream[bass.ds(2 * i + s, 1)].rearrange("a p n -> (a p) n")
                                 ).then_inc(raw_in[s], 16)
            for u in range(UNITS // 2 * 2, UNITS):
                sp.wait_ge(lo_ready, u - 1)
                sp.dma_start(raw[u % 2][:, :], wstream[u]).then_inc(raw_in[u % 2], 16)
            after(sp, layers[-1]["n_mpost"]["dve"], KD)
            sp.dma_start(outT, hres[:, :].rearrange("p (k t) -> p k t", k=KD)[:, :, META:L]).then_inc(out_done, 16)
            sp.wait_ge(out_done, 16)

        @block.gpsimd
        def _(pool):
            def low(s, value):
                hold(pool, hi_ready, value, "pool")
                nc.gpsimd.tensor_tensor(wlo[s][:, :], raw[s][:, :], whi[s][:, :].bitcast(F32),
                                        ALU.subtract).then_inc(lo_ready, 1)

            with pool.Fori(0, UNITS // 2) as i:
                for s in range(2):
                    low(s, 2 * i + s + 1)
            for u in range(UNITS // 2 * 2, UNITS):
                low(u % 2, u + 1)

        @block.tensor
        def _(pe):
            def passes(out, wslot, blk, hi, lo, first, last):
                wh, wl = whi[wslot][:, blk * P:(blk + 1) * P], wlo[wslot][:, blk * P:(blk + 1) * P]
                n = len(out)
                for o, h in zip(out, hi):
                    nc.tensor.matmul(o, wh, h, start=first, stop=False)
                for o, h in zip(out, lo):
                    nc.tensor.matmul(o, wh, h, start=False, stop=False)
                for j in range(n):
                    mm = nc.tensor.matmul(out[j], wl, hi[j], start=False, stop=last)
                return mm

            def linear(stage, hi, lo, width, parts=1):
                def unit(i, s):
                    slot, g = stage.slot(s), stage.u0 + s + 2 * i
                    hold(pe, lo_ready, g + 1, "pe")
                    hold(pe, psum_free[slot], stage.used(i, s), "pe")
                    for m in range(stage.nm):
                        banks = [slot * 2 * parts + m * parts + h for h in range(parts)]
                        out = [bank(b, width) for b in banks]
                        for k in range(stage.nk):
                            cs = [k * width * parts + h * width for h in range(parts)]
                            mm = passes(out, slot, m * stage.nk + k, [hi[:, c:c + width] for c in cs],
                                        [lo[:, c:c + width] for c in cs], k == 0, k == stage.nk - 1)
                        mm.then_inc(tile0_done if m < stage.nm - 1 else unit_done, 1)
                unit_loop(pe, stage, unit)

            def sum_tiles(b, tile, n, ready, value, done, parts=1, width=T):
                for k in range(n):
                    after(pe, ready, value(k))
                    t = tile(k)
                    for h in range(parts):
                        mm = nc.tensor.matmul(bank(b + h, width), ones, t[:, h * width:(h + 1) * width],
                                              start=(k == 0), stop=(k == n - 1))
                    mm.then_inc(done.sem, 1)

            def layer_norm(n, src, ready, value, sq):
                pe.wait_ge(ready, value)
                for k in range(KD):
                    mm = nc.tensor.matmul(bank(4), ones, src[:, k * T:(k + 1) * T], start=(k == 0), stop=(k == KD - 1))
                mm.then_inc(n["pe"].sem, 1)
                sum_tiles(6, lambda k: sq[k % 2], KD, n["act"], lambda k: 2 + k, n["pe"])

            def rms_norm(n, nk=KD):
                sum_tiles(6, lambda k: sq3[k % 2], nk, n["act"], lambda k: k + 1, n["pe"], 2, HALF)

            pe.wait_ge(params_in, 48)
            layer_norm(n_in, x_in, x_in_s, 16, sq1)
            after(pe, n_in["lo"], KD)
            linear(PLAN["dt"], ahi, alo, T)
            linear(PLAN["xbc"], ahi, alo, T)

            pe.wait_ge(dt_ready, 2)
            for j, t in enumerate((dtt[6], dtt[5])):
                for c in range(CHUNKS):
                    mm = nc.tensor.transpose(bank(4, 32, j * 128 + c * 32), t[0:32, c * P:(c + 1) * P],
                                             const1[0:32, 0:32])
            mm.then_inc(dt_ps, 1)
            pe.wait_ge(dt_tok, 1)
            nc.tensor.matmul(bank(5, 128), last_row, tok[:, 0:128], start=True, stop=True).then_inc(end_ps, 1)
            pe.wait_ge(ends_ok, 1)
            with pe.Fori(0, GROUPS) as g:
                hold(pe, b_ok, g + 1, "pe")
                hold(pe, bt_ok, g, "pe")
                for c in range(CHUNKS - 1):
                    mm = nc.tensor.transpose(bank(4, P, c * P), b_slot[:, c * P:(c + 1) * P], ident)
                mm.then_inc(bt_ps, 1)
                hold(pe, mc_ok, g * GH, "pe")
                for c in range(CHUNKS):
                    mm = nc.tensor.matmul(bank(5, P, c * P), b_slot[:, c * P:(c + 1) * P],
                                          cut(xbc, g * T + (CT0 * T + c * P), P), start=True, stop=True)
                mm.then_inc(cb_ps, 1)
                for j in range(GP):
                    hold(pe, x_ok, g * GP + (j + 1), "pe")
                    hold(pe, xdt_ok, g * GP + max(j - 1, 0), "pe")
                    for c in range(CHUNKS):
                        mm = nc.tensor.transpose(bank(6 + j % 2, P, c * P), x_slot[j % 2][:, c * P:(c + 1) * P], ident)
                    mm.then_inc(xt_ps, 1)
                hold(pe, xds_ok, g + 1, "pe")
                hold(pe, bt_ok, g + 1, "pe")
                hold(pe, y_ok, g * GP, "pe")
                for c in range(CHUNKS - 1):
                    mm = nc.tensor.matmul(bank(c), bt_sb[:, c * P:(c + 1) * P], xds[:, c * T:(c + 1) * T],
                                          start=True, stop=True)
                mm.then_inc(st_ps, 1)
                hold(pe, st_ok, g + 1, "pe")
                for j in range(GP):
                    hold(pe, y_ok, g * GP + max(j - 1, 0), "pe")
                    for hh in range(2):
                        q = 2 * j + hh
                        hold(pe, mc_ok, g * GH + (q + 1), "pe")
                        for c in range(CHUNKS):
                            o = PS[64 * hh:64 * hh + 64, (j % 2) * 512 + c * P:(j % 2) * 512 + (c + 1) * P]
                            mm = nc.tensor.matmul(o, xdt[:, c * T + q * 64:c * T + q * 64 + 64],
                                                  m_slot[hh][:, c * P:(c + 1) * P], start=True, stop=(c == 0))
                            if c:
                                mm = nc.tensor.matmul(o, st[:, (c - 1) * T + q * 64:(c - 1) * T + q * 64 + 64],
                                                      c_slot[hh][:, c * P:(c + 1) * P], start=False, stop=True)
                        mm.then_inc(y_mm, 1)

            pe.wait_ge(y_ok, XT)
            linear(PLAN["glu"], ahi, alo, T)
            linear(PLAN["z"], ahi, alo, T)
            pe.wait_ge(ysq_sum, XT)
            for g in range(GROUPS):
                mm = nc.tensor.matmul(bank(4 + g), ones, sumsq[:, g * T:(g + 1) * T], start=True, stop=True)
            mm.then_inc(ss_ps, 1)
            linear(PLAN["gate_b"], ahi, alo, T)
            pe.wait_ge(ylo_ok, XT)
            linear(PLAN["ssm_out"], yn_hi, yn_lo, T)
            layer_norm(n_conv, vout, vout_ok, KD, sq1)
            linear(PLAN["gate_a"], ahi, alo, T)
            after(pe, n_conv["lo"], KD)
            linear(PLAN["conv_out"], chi, clo, T)
            pe.wait_ge(mixlo_ok, KD)
            linear(PLAN["w_o"], mixhi, mixlo, T)
            layer_norm(n_1, res1, r1_ok, KD, sq1)
            after(pe, n_1["lo"], KD)
            linear(PLAN["ffn_up"], ahi, alo, T)

            stage = PLAN["ffn_down"]
            pe.wait_ge(flo_ok, FT)
            for k in range(2):
                pe.wait_ge(psum_free[k], (stage.u0 + 1 - k) // 2)
            with pe.Fori(0, KD // 2) as i:
                for t in range(2):
                    base = (stage.u0 + 1) // 2
                    hold(pe, psum_free[0], base + 2 * i + (t - 1), "pe")
                    for s in range(2):
                        slot = stage.slot(s)
                        hold(pe, lo_ready, stage.u0 + 4 * i + (2 * t + s + 1), "pe")
                        for k in range(FT // 2):
                            kk = s * (FT // 2) + k
                            mm = passes([bank(2 * t)], slot, k, [fhi[:, kk * T:(kk + 1) * T]],
                                        [flo[:, kk * T:(kk + 1) * T]], kk == 0, kk == FT - 1)
                        mm.then_inc(unit_done, 1)
            layer_norm(n_2, res2, r2_ok, KD, sq2)

            for l, y in enumerate(layers):
                rms_norm(y["n_pre"])
                after(pe, y["n_pre"]["lo"], KD)
                linear(PLAN[f"in_{l}"], ahi, alo, HALF, 2)
                after(pe, y["in_u"], 4)
                pe.wait_ge(const2_in, 16 * (l + 1))
                pe.wait_ge(psum_free[0], (PLAN[f"out_{l}"].u0 + 1) // 2)
                pe.wait_ge(psum_free[1], PLAN[f"out_{l}"].u0 // 2)
                for j in range(5):
                    if j >= 2:
                        after(pe, y["rope_ok"], j - 1)
                    for h in range(2):
                        mm = nc.tensor.matmul(bank(2 * (j % 2) + h, HALF), const2[:, 0:128],
                                              qraw[:, j * L + h * HALF:j * L + (h + 1) * HALF], start=True, stop=True)
                    mm.then_inc(y["swap_ps"].sem, 1)
                for b in range(NB):
                    mm = nc.tensor.transpose(bank(4 + b // 4, P, (b % 4) * P), vch[:, (b + 1) * P:(b + 2) * P], ident)
                mm.then_inc(y["v_ps"].sem, 1)
                after(pe, y["rope_ok"], 5)
                after(pe, y["v_ok"], 1)
                with pe.Fori(0, NB) as b:
                    hold(pe, y["slot_ok"], b + 1, "pe")
                    for z in range(2):
                        hold(pe, y["o_ok"], 2 * b, "pe")
                        for j in range(4):
                            mm = nc.tensor.matmul(bank(2 * z + j // 2, 256, (j % 2) * 256),
                                                  q_slot[64 * z:64 * z + 64, j * P:(j + 1) * P],
                                                  k_slot[64 * z:64 * z + 64, :], start=True, stop=True)
                        mm.then_inc(y["sc_ps"].sem, 1)
                    for z in range(2):
                        hold(pe, y["p_ok"], 2 * b + (z + 1), "pe")
                        hold(pe, y["pt_ok"], 2 * b, "pe")
                        for kb in range(2):
                            for j in range(4):
                                mm = nc.tensor.transpose(bank(4 + 2 * z + kb, P, j * P),
                                                         sc[z][:, j * 256 + kb * P:j * 256 + (kb + 1) * P], ident)
                        mm.then_inc(y["pt_ps"].sem, 1)
                    for z in range(2):
                        hold(pe, y["pt_ok"], 2 * b + (z + 1), "pe")
                        for j in range(4):
                            for kb in range(2):
                                mm = nc.tensor.matmul(bank(2 * z, 64, j * 64),
                                                      pT[z][:, kb * 512 + j * P:kb * 512 + (j + 1) * P],
                                                      v_slot[:, kb * P + 64 * z:kb * P + 64 * z + 64],
                                                      start=(kb == 0), stop=(kb == 1))
                        mm.then_inc(y["o_ps"].sem, 1)
                with pe.Fori(0, NB) as b:
                    hold(pe, y["yn_ok"], b + 1, "pe")
                    hold(pe, y["ya_ok"], b, "pe")
                    for j in range(4):
                        mm = nc.tensor.transpose(bank(4, P, j * P), y_n[:, j * P:(j + 1) * P], ident)
                    mm.then_inc(y["yt_ps"].sem, 1)
                rms_norm(y["n_conv"], 4)
                after(pe, y["n_attn"]["lo"], 4)
                after(pe, y["n_conv"]["lo"], 4)
                linear(PLAN[f"out_{l}"], ahi, alo, HALF, 2)
                rms_norm(y["n_post"])
                rms_norm(y["n_mpre"])
                after(pe, y["n_mpre"]["lo"], KD)
                for h in range(2):
                    linear(PLAN[f"up{h}_{l}"], ahi, alo, HALF, 2)
                    after(pe, y[f"f2lo_ok{h}"], FFH)
                    linear(PLAN[f"down{h}_{l}"], f2hi, f2lo, HALF, 2)
                rms_norm(y["n_mpost"])

        @block.scalar
        def _(act):
            drain = nc.scalar.drain

            def split_first(u):
                act.wait_ge(raw_in[u % 2], 16 * (u // 2 + 1))
                nc.scalar.activation(whi[u % 2][:, :], raw[u % 2][:, :], ACT.Copy).then_inc(hi_ready, 1)

            def split_next(stage, i, s):
                if isinstance(i, int) and stage.u0 + 2 * i + s + 2 >= UNITS:
                    hold(act, unit_done, stage.u0 + s + 2 * i + 1, "act")
                    return
                slot = stage.slot(s)
                hold(act, unit_done, stage.u0 + s + 1 + 2 * i, "act")
                hold(act, raw_in[slot], 16 * i + 16 * ((stage.u0 + s) // 2 + 2), "act")
                nc.scalar.activation(whi[slot][:, :], raw[slot][:, :], ACT.Copy).then_inc(hi_ready, 1)

            def evacuate(stage, body, tail=0):
                def unit(i, s):
                    split_next(stage, i, s)
                    body(i, s, stage.slot(s))
                unit_loop(act, stage, unit, tail)

            def layer_norm(n, src, sq, g, b, func, dst, hi, lo_free=None):
                after(act, n["pe"], 1)
                nc.scalar.activation(mu[:, 0:T], bank(4), ACT.Copy, scale=1.0 / D).then_inc(n["act"].sem, 1)
                for k in range(KD):
                    after(act, n["dve"], k + 1)
                    if k >= 2:
                        after(act, n["pe"], k)
                    nc.scalar.activation(sq[k % 2][:, :], src[:, k * T:(k + 1) * T], ACT.Square).then_inc(n["act"].sem, 1)
                after(act, n["pe"], KD + 1)
                nc.scalar.activation(std[:, 0:T], bank(6), ACT.Sqrt, bias=col("eps5", 0), scale=1.0 / D
                                     ).then_inc(n["act"].sem, 1)
                for k in range(KD):
                    after(act, n["dve"], KD + k + 1)
                    nc.scalar.activation(dst(k), src[:, k * T:(k + 1) * T], func, bias=col(b, k), scale=col(g, k))
                    if hi is not None:
                        drain()
                        nc.scalar.activation(hi[:, k * T:(k + 1) * T], dst(k), ACT.Copy).then_inc(n["hi"].sem, 1)
                if hi is None:
                    drain().then_inc(n["hi"].sem, 1)

            def squares(n, tile, nk, ready=None, value=None):
                for k in range(nk):
                    if ready is not None:
                        after(act, ready, value(k))
                    if k >= 2:
                        after(act, n["pe"], k - 1)
                    nc.scalar.activation(sq3[k % 2][:, :], tile(k), ACT.Square).then_inc(n["act"].sem, 1)
                after(act, n["pe"], nk)
                nc.scalar.activation(split2(std[:, :]), wide(6), ACT.Sqrt, bias=col("eps6", 0),
                                     scale=1.0 / (nk * P)).then_inc(n["act"].sem, 1)

            def highs(n, nk, first):
                for k in range(nk):
                    after(act, n["dve"], k + 1)
                    nc.scalar.activation(ahi[:, (first + k) * L:(first + k + 1) * L], nv[k % 2][:, :], ACT.Copy
                                         ).then_inc(n["hi"].sem, 1)

            for u in range(2):
                split_first(u)
            act.wait_ge(params_in, 48)
            layer_norm(n_in, x_in, sq1, "ln_in_g", "ln_in_b", ACT.Identity,
                       lambda k: x_in[:, k * T:(k + 1) * T], ahi)

            stage = PLAN["dt"]
            split_next(stage, 0, 0)
            nc.scalar.activation(dtt[0][:, :], bank(0, parts=32), ACT.Identity, bias=heads[:, 0:1]
                                 ).then_inc(psum_free[0], 1)
            drain()
            nc.scalar.activation(dtt[1][:, :], dtt[0][:, :], ACT.Abs)
            nc.scalar.activation(heads[:, 2:3], heads[:, 1:2], ACT.Exp)
            drain()
            nc.scalar.activation(dtt[2][:, :], dtt[1][:, :], ACT.Exp, scale=-1.0).then_inc(dt_exp, 1)

            stage = PLAN["xbc"]

            def xbc_unit(i, s, slot):
                for m in range(2):
                    k = 4 * i + (2 * s + m)
                    nc.scalar.activation(cut(xbc, 2048 * i + (2 * s + m) * T, T), bank(2 * slot + m), ACT.Identity,
                                         bias=col("ssm_b", k), scale=col("ssm_w", 4 * k + 3)).then_inc(conv4_acc, 1)
                for m in range(2):
                    if m == 0:
                        hold(act, conv4_tap, 2 * i + (s + 1), "act")
                    else:
                        hold(act, psum_free[slot], stage.used(i, s) + 1, "act")
                    tile = cut(xbc, 2048 * i + (2 * s + m) * T, T)
                    nc.scalar.activation(tile, tile, ACT.Silu).then_inc(conv4_out, 1)

            evacuate(stage, xbc_unit)

            act.wait_ge(dt_ready, 2)
            act.dma_start(acs_d[0:32, :], dtt[6][:, :]).then_inc(scratch_in, 16)
            act.dma_start(acs_d[32:34, :], dtt[6][0:2, :]).then_inc(scratch_in, 16)
            act.wait_ge(dt_ps, 1)
            nc.scalar.activation(tok[:, :], bank(4, 256), ACT.Copy).then_inc(dt_tok, 1)
            act.wait_ge(end_in, 1)
            nc.scalar.activation(ends[:, 0:128], ends[:, 0:128], ACT.Exp)
            nc.scalar.activation(ends[:, 128:256], bank(5, 128), ACT.Exp)
            drain().then_inc(ends_ok, 1)
            act.wait_ge(scratch_in, 32)
            for s in range(2):
                act.dma_start(acs_b[s][:, :], acs_d[s, :].partition_broadcast(P)).then_inc(acs_in[s], 16)
            with act.Fori(0, GROUPS) as g:
                hold(act, cb_ps, g, "act")
                nc.scalar.activation(b_slot[:, :], cut(xbc, g * T + BT0 * T, T), ACT.Copy).then_inc(b_ok, 1)

                def x_copy(j):
                    hold(act, xt_ps, g * GP + max(j - 1, 0), "act")
                    nc.scalar.activation(x_slot[j % 2][:, :], cut(xbc, g * (GP * T) + j * T, T), ACT.Copy
                                         ).then_inc(x_ok, 1)

                x_copy(0)
                x_copy(1)
                hold(act, bt_ps, g + 1, "act")
                hold(act, st_ps, g, "act")
                nc.scalar.activation(bt_sb[:, 0:384], bank(4, 384), ACT.Copy).then_inc(bt_ok, 1)
                x_copy(2)
                x_copy(3)
                for q in range(GH):
                    s = q % 2
                    hold(act, seg_ok, g * GH + (q + 1), "act")
                    nc.scalar.activation(m_slot[s][:, :], m_slot[s][:, :], ACT.Exp)
                    nc.scalar.activation(c_slot[s][:, :], acs_b[s][:, :], ACT.Exp)
                    drain().then_inc(exp_ok, 1)
                    act.dma_start(acs_b[s][:, :], acs_d[bass.ds(g * GH + (q + 2), 1), :].rearrange("a t -> (a t)")
                                  .partition_broadcast(P)).then_inc(acs_in[s], 16)
            for s in range(2):
                act.wait_ge(acs_in[s], 16 * (HEADS // 2 + 1))

            stage_g = PLAN["glu"]

            def glu_unit(i, s, slot):
                hold(act, v_ok, 2 * i, "act")
                nc.scalar.activation(sig[s][:, :], bank(2 * slot + 1), ACT.Sigmoid).then_inc(sig_ok, 1)

            act.wait_ge(y_ok, XT)
            evacuate(stage_g, glu_unit)

            def z_unit(i, s, slot):
                for m in range(2):
                    hold(act, yg_ok, 4 * i + 2 * s, "act")
                    z = nc.scalar.activation(zs[m][:, :], bank(2 * slot + m), ACT.Silu)
                    if m == 0:
                        z.then_inc(zs_ok, 1)
                    else:
                        z.then_inc(psum_free[slot], 1)
                for m in range(2):
                    hold(act, yg_ok, 4 * i + (2 * s + m + 1), "act")
                    hold(act, ysq_sum, 4 * i + 2 * s, "act")
                    nc.scalar.activation(ysq[m][:, :], cut(xbc, 2048 * i + (2 * s + m) * T, T), ACT.Square
                                         ).then_inc(ysq_ok, 1)

            evacuate(PLAN["z"], z_unit)

            act.wait_ge(ss_ps, 1)
            for g in range(GROUPS):
                nc.scalar.activation(rst4[:, g * T:(g + 1) * T], bank(4 + g), ACT.Sqrt, bias=col("eps5", 0),
                                     scale=1.0 / (GP * P)).then_inc(ss_std, 1)

            def gate_b_unit(i, s, slot):
                for m in range(2):
                    z = nc.scalar.activation(cut(gb, 2048 * i + (2 * s + m) * T, T), bank(2 * slot + m), ACT.Sigmoid)
                z.then_inc(psum_free[slot], 1)
                for j in range(GP):
                    hold(act, yv_ok, 8 * i + (GP * s + j + 1), "act")
                    nc.scalar.activation(cut(yn_hi, 8 * T * i + (GP * s + j) * T, T), yv[:, j * T:(j + 1) * T], ACT.Copy
                                         ).then_inc(yhi_ok, 1)

            evacuate(PLAN["gate_b"], gate_b_unit)
            evacuate(PLAN["ssm_out"], lambda i, s, slot: None)
            layer_norm(n_conv, vout, sq1, "conv_ln_g", "conv_ln_b", ACT.Silu, lambda k: vout[:, k * T:(k + 1) * T], chi)

            def gate_a_unit(i, s, slot):
                for m in range(2):
                    z = nc.scalar.activation(cut(ga, 2048 * i + (2 * s + m) * T, T), bank(2 * slot + m), ACT.Sigmoid)
                z.then_inc(psum_free[slot], 1)

            evacuate(PLAN["gate_a"], gate_a_unit)

            def mix_unit(i, s, slot):
                for m in range(2):
                    hold(act, mix_ok, 4 * i + (2 * s + m + 1), "act")
                    c = 2048 * i + (2 * s + m) * T
                    nc.scalar.activation(cut(mixhi, c, T), cut(gb, c, T), ACT.Copy).then_inc(mixhi_ok, 1)

            evacuate(PLAN["conv_out"], mix_unit)
            evacuate(PLAN["w_o"], lambda i, s, slot: None)
            layer_norm(n_1, res1, sq1, "ln1_g", "ln1_b", ACT.Identity, lambda k: res1[:, k * T:(k + 1) * T], ahi)

            stage_u = PLAN["ffn_up"]

            def up_unit(i, s, slot):
                for m in range(2):
                    k = 2 * i + (s + m * FT)
                    hold(act, flo_ok, 2 * i, "act")
                    nc.scalar.activation(fg[s][m][:, :], bank(2 * slot + m), ACT.Identity, bias=col("ffn_b", k),
                                         scale=col("ffn_w", 3 * k + 2)).then_inc(fa_ok, 1)
                hold(act, ft_ok, 2 * i + (s + 1), "act")
                nc.scalar.activation(fg[s][0][:, :], fg[s][0][:, :], ACT.Silu).then_inc(fs_ok, 1)
                hold(act, ff_ok, 2 * i + (s + 1), "act")
                nc.scalar.activation(cut(fhi, 2 * T * i + s * T, T), fg[s][1][:, :], ACT.Copy).then_inc(fhi_ok, 1)

            evacuate(stage_u, up_unit)
            stage_d = PLAN["ffn_down"]
            act.wait_ge(flo_ok, FT)
            evacuate(stage_d, lambda i, s, slot: None)
            act.dma_start(hres[:, :].rearrange("p (k t) -> p k t", k=KD)[:, :, 0:META], metaT).then_inc(meta_in, 16)
            hview = [hres[:, k * L + META:(k + 1) * L] for k in range(KD)]
            layer_norm(n_2, res2, sq2, "ln2_g", "ln2_b", ACT.Identity, lambda k: hview[k], None)
            act.wait_ge(meta_in, 16)

            for l, y in enumerate(layers):
                if l == 0:
                    after(act, n_2["hi"], 1)
                def h_tile(k):
                    return hres[:, k * L:(k + 1) * L]
                if l == 0:
                    squares(y["n_pre"], h_tile, KD)
                else:
                    squares(y["n_pre"], h_tile, KD, layers[l - 1]["n_mpost"]["dve"], lambda k: k + 1)
                highs(y["n_pre"], KD, 0)
                after(act, y["pad_ok"], 1)
                act.dma_start(const2[:, :], const2_d).then_inc(const2_in, 16)
                stage = PLAN[f"in_{l}"]

                def in_unit(u):
                    i, s = u // 2, u % 2
                    slot = stage.slot(s)
                    split_next(stage, i, s)
                    b = [wide(slot * 4 + 2 * m) for m in range(2)]
                    if u < 3:
                        for m in range(2):
                            j = 2 * u + m
                            if j < 5:
                                o = nc.scalar.activation(split2(qraw[:, j * L:(j + 1) * L]), b[m], ACT.Copy)
                            else:
                                o = nc.scalar.activation(split2(vch[:, WIN + LEAD:KPAD]), b[m], ACT.Copy)
                        o.then_inc(psum_free[slot], 1)
                    elif u < 7:
                        if u >= 5:
                            after(act, y["in_u"], u - 4)
                        nc.scalar.activation(split2(cgate[u % 2][:, :]), b[0], ACT.Copy).then_inc(y["in_c"].sem, 1)

                for u in range(9):
                    in_unit(u)

                after(act, y["v_ps"], 1)
                nc.scalar.activation(vtok[:, P:KPAD], PS[:, 4 * 512:4 * 512 + NB * P], ACT.Copy).then_inc(y["v_ok"].sem, 1)
                after(act, y["rope_ok"], 5)
                drain()
                with act.Fori(0, NB) as b:
                    hold(act, y["o_ps"], 2 * b, "act")
                    nc.scalar.activation(q_slot[:, :].rearrange("p (j t) -> p j t", j=4),
                                         qpad[:, :].rearrange("p (j t) -> p j t", j=4)[:, :, bass.ds(b * WIN, WIN)],
                                         ACT.Copy)
                    nc.scalar.activation(k_slot[:, :], cut(kpad, b * WIN, 2 * WIN), ACT.Copy)
                    nc.scalar.activation(v_slot[:, :], cut(vtok, b * WIN, 2 * WIN), ACT.Copy)
                    drain().then_inc(y["slot_ok"].sem, 1)
                    for z in range(2):
                        hold(act, y["neg_ok"], 2 * b + (z + 1), "act")
                        for j in range(4):
                            p = sc[z][:, j * 256:(j + 1) * 256]
                            nc.scalar.activation(p, p, ACT.Exp, bias=small[:, 8 * z + j:8 * z + j + 1],
                                                 accum_out=small[:, 16 + 8 * z + j:17 + 8 * z + j])
                        nc.scalar.activation(small[:, 32 + 8 * z:36 + 8 * z], small[:, 32 + 8 * z:36 + 8 * z], ACT.Exp)
                        drain().then_inc(y["p_ok"].sem, 1)
                    for z in range(2):
                        hold(act, y["pt_ps"], 2 * b + (z + 1), "act")
                        hold(act, y["o_ps"], 2 * b, "act")
                        nc.scalar.activation(pT[z][:, :], PS[:, (4 + 2 * z) * 512:(6 + 2 * z) * 512], ACT.Copy
                                             ).then_inc(y["pt_ok"].sem, 1)
                after(act, y["o_ok"], 2 * NB)
                for b in range(NB):
                    nc.scalar.activation(sc[b % 2][:, 0:512], y_tok[:, b * 512:(b + 1) * 512], ACT.Square,
                                         accum_out=small[:, 48 + b:49 + b])
                    drain()
                nc.scalar.activation(small[:, 48:48 + NB], small[:, 48:48 + NB], ACT.Sqrt, bias=col("eps6", 0),
                                     scale=1.0 / 512).then_inc(y["astd_ok"].sem, 1)
                with act.Fori(0, NB) as b:
                    hold(act, y["yt_ps"], b + 1, "act")
                    nc.scalar.activation(ya[:, :].rearrange("p (j t) -> p j t", j=4)[:, :, bass.ds(b * WIN, WIN)],
                                         bank(4).rearrange("p (j t) -> p j t", j=4), ACT.Copy).then_inc(y["ya_ok"].sem, 1)
                highs(y["n_attn"], 4, 0)
                squares(y["n_conv"], lambda k: yconv[:, k * L:(k + 1) * L], 4, y["n_attn"]["lo"], lambda k: 4)
                highs(y["n_conv"], 4, 4)

                stage = PLAN[f"out_{l}"]

                def z_copy(st_):
                    def body(i, s, slot):
                        for m in range(st_.nm):
                            c = (2 * st_.nm * L) * i + (st_.nm * s + m) * L
                            o = nc.scalar.activation(split2(cut(zres, c, L)), wide(slot * 4 + 2 * m), ACT.Copy)
                        o.then_inc(psum_free[slot], 1)
                    return body

                after(act, y["n_conv"]["lo"], 4)
                evacuate(stage, z_copy(stage))
                drain().then_inc(y["zc_ok"].sem, 1)
                z_tile = lambda k: zres[:, k * L:(k + 1) * L]
                squares(y["n_post"], z_tile, KD)
                squares(y["n_mpre"], h_tile, KD, y["n_post"]["dve"], lambda k: k + 1)
                highs(y["n_mpre"], KD, 0)
                for h in range(2):
                    stage = PLAN[f"up{h}_{l}"]
                    rl_ok, f_ok, f2hi_ok, f2lo_ok = (y[f"{a}{h}"] for a in ("rl_ok", "f_ok", "f2hi_ok", "f2lo_ok"))

                    def up_body(i, s, slot):
                        for m in range(2):
                            hold(act, f2lo_ok, 4 * i, "act")
                            o = nc.scalar.activation(split2(rl[2 * s + m][:, :]), wide(slot * 4 + 2 * m), ACT.Relu)
                            o.then_inc(rl_ok.sem if m == 0 else psum_free[slot], 1)
                        for m in range(2):
                            hold(act, f_ok, 4 * i + (2 * s + m + 1), "act")
                            nc.scalar.activation(cut(f2hi, 4 * L * i + (2 * s + m) * L, L), rl[2 * s + m][:, :], ACT.Copy
                                                 ).then_inc(f2hi_ok.sem, 1)

                    if h == 1:
                        act.wait_ge(unit_done, stage.u0)
                    evacuate(stage, up_body)
                    stage = PLAN[f"down{h}_{l}"]
                    tail = 2 if stage.u0 + stage.n == UNITS else 0
                    if h == 0:
                        evacuate(stage, z_copy(stage), tail)
                        drain().then_inc(y["zc_ok"].sem, 1)
                    else:
                        evacuate(stage, lambda i, s, slot: None, tail)
                squares(y["n_mpost"], z_tile, KD, y["dn_ok1"], lambda k: KD)

        @block.vector
        def _(dve):
            drain = nc.vector.drain
            v = nc.vector

            def tap(acc, ps, w, sh, n=T):
                return v.scalar_tensor_tensor(acc[:, sh:n], ps[:, 0:n - sh], w, acc[:, sh:n], ALU.mult, ALU.add)

            def layer_norm(n, src, hi, lo):
                after(dve, n["act"], 1)
                for k in range(KD):
                    t = src[:, k * T:(k + 1) * T]
                    v.tensor_tensor(t, t, mu[:, 0:T], ALU.subtract).then_inc(n["dve"].sem, 1)
                after(dve, n["act"], KD + 2)
                v.reciprocal(rstd[:, 0:T], std[:, 0:T])
                drain()
                for k in range(KD):
                    t = src[:, k * T:(k + 1) * T]
                    v.tensor_tensor(t, t, rstd[:, 0:T], ALU.mult).then_inc(n["dve"].sem, 1)
                if hi is None:
                    return
                for k in range(KD):
                    after(dve, n["hi"], k + 1)
                    c = slice(k * T, (k + 1) * T)
                    v.tensor_tensor(lo[:, c], src[:, c], hi[:, c].bitcast(F32), ALU.subtract).then_inc(n["lo"].sem, 1)

            def lows(n, k, first):
                after(dve, n["hi"], k + 1)
                c = slice((first + k) * L, (first + k + 1) * L)
                v.tensor_tensor(alo[:, c], nv[k % 2][:, :], ahi[:, c].bitcast(F32), ALU.subtract).then_inc(n["lo"].sem, 1)

            def scaled(n, tile, nk, g, first, by_row=True):
                if by_row:
                    after(dve, n["act"], nk + 1)
                    v.reciprocal(rstd[:, :], std[:, :])
                    drain()
                for k in range(nk):
                    if k >= 2:
                        drain()
                    if by_row:
                        v.scalar_tensor_tensor(nv[k % 2][:, :], tile(k), col(g, k), rstd[:, :], ALU.mult, ALU.mult
                                               ).then_inc(n["dve"].sem, 1)
                    else:
                        v.tensor_scalar(nv[k % 2][:, :], tile(k), col(g, k), None, ALU.mult).then_inc(n["dve"].sem, 1)
                    if k >= 1:
                        lows(n, k - 1, first)
                lows(n, nk - 1, first)

            def residual(n, g):
                after(dve, n["act"], KD + 1)
                v.reciprocal(rstd[:, :], std[:, :])
                drain()
                for k in range(KD):
                    t = zres[:, k * L:(k + 1) * L]
                    v.scalar_tensor_tensor(t, t, col(g, k), rstd[:, :], ALU.mult, ALU.mult)
                drain()
                for k in range(KD):
                    t, h = zres[:, k * L:(k + 1) * L], hres[:, k * L:(k + 1) * L]
                    v.tensor_tensor(h, h, t, ALU.add).then_inc(n["dve"].sem, 1)

            dve.wait_ge(params_in, 48)
            layer_norm(n_in, x_in, ahi, alo)

            dve.wait_ge(dt_exp, 1)
            x_, e_, r_, s_, s2, q_, acs, dt_ = dtt[0], dtt[2], dtt[3], dtt[4], dtt[1], dtt[7], dtt[6], dtt[5]
            v.tensor_scalar(r_[:, :], e_[:, :], 2.0, None, ALU.add)
            drain()
            v.reciprocal(s_[:, :], r_[:, :])
            drain()
            v.tensor_tensor(s_[:, :], s_[:, :], e_[:, :], ALU.mult)
            drain()
            v.tensor_tensor(s2[:, :], s_[:, :], s_[:, :], ALU.mult)
            drain()
            v.tensor_scalar(q_[:, :], s2[:, :], 1.0 / 15, None, ALU.mult)
            for d in (13, 11, 9, 7, 5, 3):
                drain()
                v.scalar_tensor_tensor(q_[:, :], q_[:, :], 1.0 / d, s2[:, :], ALU.add, ALU.mult)
            drain()
            v.scalar_tensor_tensor(q_[:, :], q_[:, :], 1.0, s_[:, :], ALU.add, ALU.mult)
            v.tensor_scalar(x_[:, :], x_[:, :], 0.0, None, ALU.max)
            drain()
            v.scalar_tensor_tensor(dt_[:, :], q_[:, :], 2.0, x_[:, :], ALU.mult, ALU.add).then_inc(dt_ready, 1)
            drain()
            v.tensor_scalar(r_[:, :], dt_[:, :], heads[:, 2:3], -1.0, ALU.mult, ALU.mult)
            drain()
            for c in range(CHUNKS):
                cs = slice(c * CHUNK, (c + 1) * CHUNK)
                o = v.tensor_tensor_scan(acs[:, cs], const1[0:32, 128:256], r_[:, cs], 0.0, ALU.mult, ALU.add)
            o.then_inc(dt_ready, 1)

            stage = PLAN["xbc"]

            def xbc_unit(i, s):
                slot = stage.slot(s)
                for m in range(2):
                    k = 4 * i + (2 * s + m)
                    hold(dve, conv4_acc, 4 * i + (2 * s + m + 1), "dve")
                    c = 2048 * i + (2 * s + m) * T
                    for w in (2, 1, 0):
                        sh = 3 - w
                        o = v.scalar_tensor_tensor(cut(xbc, c + sh, T - sh), bank(2 * slot + m, T - sh),
                                                   col("ssm_w", 4 * k + w), cut(xbc, c + sh, T - sh),
                                                   ALU.mult, ALU.add)
                        if w:
                            drain()
                    o.then_inc(conv4_tap if m == 0 else psum_free[slot], 1)

            unit_loop(dve, stage, xbc_unit)

            dve.wait_ge(end_ps, 1)
            v.scalar_tensor_tensor(ends[:, 0:128], tok[:, 0:128], -1.0, bank(5, 128), ALU.mult, ALU.add
                                   ).then_inc(end_in, 1)
            dve.wait_ge(ends_ok, 1)
            dve.wait_ge(conv4_out, XBCT)

            with dve.Fori(0, GROUPS) as g:
                xdt3 = xdt[:, :].rearrange("p (c n) -> p c n", c=CHUNKS)
                for j in range(GP):
                    hold(dve, xt_ps, g * GP + (j + 1), "dve")
                    for hh in range(2):
                        o = v.tensor_tensor(
                            xdt3[:, :, j * P + hh * 64:j * P + (hh + 1) * 64],
                            bank(6 + j % 2).rearrange("p (c n) -> p c n", c=CHUNKS)[:, :, hh * 64:(hh + 1) * 64],
                            tok[:, 128:256].rearrange("p (c h) -> p c h", c=CHUNKS)[:, :, bass.ds(g * GH + (2 * j + hh), 1)]
                            .to_broadcast([P, CHUNKS, HEAD_P]), ALU.mult)
                    o.then_inc(xdt_ok, 1)
                drain()
                for c in range(CHUNKS - 1):
                    o = v.tensor_tensor(xds[:, c * T:(c + 1) * T].rearrange("p (h n) -> p h n", h=GH),
                                        xdt[:, c * T:(c + 1) * T].rearrange("p (h n) -> p h n", h=GH),
                                        ends[:, bass.ds(g * GH + c * 32, GH)].unsqueeze(2).to_broadcast([P, GH, HEAD_P]),
                                        ALU.mult)
                o.then_inc(xds_ok, 1)
                hold(dve, st_ps, g + 1, "dve")
                v.tensor_copy(st[:, 0:T], bank(0))
                for c in range(1, CHUNKS - 1):
                    drain()
                    v.tensor_tensor(st[:, c * T:(c + 1) * T].rearrange("p (h n) -> p h n", h=GH),
                                    st[:, (c - 1) * T:c * T].rearrange("p (h n) -> p h n", h=GH),
                                    ends[:, bass.ds(g * GH + (128 + c * 32), GH)].unsqueeze(2)
                                    .to_broadcast([P, GH, HEAD_P]), ALU.mult)
                    drain()
                    o = v.tensor_tensor(st[:, c * T:(c + 1) * T], st[:, c * T:(c + 1) * T], bank(c), ALU.add)
                o.then_inc(st_ok, 1)

                def segment(q):
                    s = q % 2
                    hold(dve, acs_in[s], 16 * (GH // 2) * g + 16 * (q // 2 + 1), "dve")
                    hold(dve, y_mm, g * GH + max(q - 1, 0), "dve")
                    for c in range(CHUNKS):
                        cs = slice(c * CHUNK, (c + 1) * CHUNK)
                        o = v.scalar_tensor_tensor(m_slot[s][:, cs], acs_b[s][:, cs],
                                                   tok[:, bass.ds(g * GH + (c * 32 + q), 1)], causal,
                                                   ALU.subtract, ALU.min)
                    o.then_inc(seg_ok, 1)

                def y_out(j):
                    hold(dve, y_mm, g * GH + 2 * (j + 1), "dve")
                    t = cut(xbc, g * (GP * T) + j * T, T)
                    v.scalar_tensor_tensor(t, t, col("ssm_d", g * GP + j), bank(j % 2), ALU.mult, ALU.add
                                           ).then_inc(y_ok, 1)

                segment(0)
                for q in range(GH):
                    s = q % 2
                    if q + 1 < GH:
                        segment(q + 1)
                    if q == 0:
                        hold(dve, cb_ps, g + 1, "dve")
                    hold(dve, exp_ok, g * GH + (q + 1), "dve")
                    v.tensor_tensor(c_slot[s][:, :], c_slot[s][:, :], cut(xbc, g * T + CT0 * T, T), ALU.mult)
                    v.tensor_tensor(m_slot[s][:, :], m_slot[s][:, :], bank(5), ALU.mult).then_inc(mc_ok, 1)
                    if q >= 2 and q % 2 == 0:
                        y_out(q // 2 - 1)
                y_out(GP - 1)

            stage_g = PLAN["glu"]
            for s in range(2):
                dve.wait_ge(acs_in[s], 16 * (HEADS // 2 + 1))
            v3 = vpad[:, :].rearrange("p (k t) -> p k t", k=KD)
            v.memset(v3[:, :, 0:TAPS - 1], 0.0)
            T1, T2 = 12, 22

            def long_taps(u, a, b, last=None):
                for w in range(a, b):
                    src, acc = cut(vpad, u * VW + w, T), cut(vout, u * T, T)
                    wc = col("conv_w", u * TAPS + w)
                    if w == 0:
                        o = v.tensor_scalar(acc, src, wc, col("conv_b", u), ALU.mult, ALU.add)
                    else:
                        o = v.scalar_tensor_tensor(acc, src, wc, acc, ALU.mult, ALU.add)
                    if w < b - 1:
                        drain()
                    elif last is not None:
                        o.then_inc(last, 1)

            def glu_unit(i, s):
                slot = stage_g.slot(s)
                u = 2 * i + s
                hold(dve, sig_ok, u + 1, "dve")
                drain()
                v.tensor_tensor(cut(vpad, u * VW + (TAPS - 1), T), bank(2 * slot), sig[s][:, :], ALU.mult
                                ).then_inc(psum_free[slot], 1)
                drain().then_inc(v_ok, 1)
                long_taps(u, 0, T1)

            unit_loop(dve, stage_g, glu_unit)

            stage_z = PLAN["z"]

            def z_unit(i, s):
                slot = stage_z.slot(s)
                for m in range(2):
                    if m == 0:
                        hold(dve, zs_ok, 2 * i + (s + 1), "dve")
                    else:
                        hold(dve, psum_free[slot], stage_z.used(i, s) + 1, "dve")
                    t = cut(xbc, 2048 * i + (2 * s + m) * T, T)
                    v.tensor_tensor(t, t, zs[m][:, :], ALU.mult).then_inc(yg_ok, 1)
                long_taps(2 * i + s, T1, T2)
                for m in range(2):
                    hold(dve, ysq_ok, 4 * i + (2 * s + m + 1), "dve")
                    acc = cut(sumsq, T * i, T)
                    if s == 0 and m == 0:
                        v.tensor_copy(acc, ysq[0][:, :]).then_inc(ysq_sum, 1)
                    else:
                        drain()
                        v.tensor_tensor(acc, acc, ysq[m][:, :], ALU.add).then_inc(ysq_sum, 1)

            unit_loop(dve, stage_z, z_unit)

            for g in range(GROUPS):
                dve.wait_ge(ss_std, g + 1)
                v.reciprocal(rst4[:, g * T:(g + 1) * T], rst4[:, g * T:(g + 1) * T])
            drain()

            def gate_b_unit(i, s):
                for j in range(GP):
                    c = 8 * T * i + (GP * s + j) * T
                    v.scalar_tensor_tensor(yv[:, j * T:(j + 1) * T], cut(xbc, c, T), col("ssm_norm", 8 * i + (GP * s + j)),
                                           cut(rst4, 2 * T * i + s * T, T), ALU.mult, ALU.mult).then_inc(yv_ok, 1)
                for j in range(GP):
                    c = 8 * T * i + (GP * s + j) * T
                    hold(dve, yhi_ok, 8 * i + (GP * s + j + 1), "dve")
                    v.tensor_tensor(cut(yn_lo, c, T), yv[:, j * T:(j + 1) * T], cut(yn_hi, c, T).bitcast(F32),
                                    ALU.subtract).then_inc(ylo_ok, 1)
                drain()

            unit_loop(dve, PLAN["gate_b"], gate_b_unit)

            stage_s = PLAN["ssm_out"]

            def ssm_out_unit(i, s):
                slot = stage_s.slot(s)
                u = 2 * i + s
                hold(dve, unit_done, u + (stage_s.u0 + 1), "dve")
                t = cut(gb, u * T, T)
                v.tensor_tensor(t, t, bank(2 * slot), ALU.mult).then_inc(psum_free[slot], 1)
                long_taps(u, T2, TAPS, vout_ok)

            unit_loop(dve, stage_s, ssm_out_unit)
            layer_norm(n_conv, vout, chi, clo)

            stage_c = PLAN["conv_out"]

            def mix_unit(i, s):
                slot = stage_c.slot(s)
                g = stage_c.u0 + s + 1
                for m in range(2):
                    c = 2048 * i + (2 * s + m) * T
                    if m == 0:
                        hold(dve, tile0_done, 2 * i + (stage_c.z0 + s + 1), "dve")
                    else:
                        hold(dve, unit_done, 2 * i + g, "dve")
                    o = v.tensor_tensor(cut(ga, c, T), cut(ga, c, T), bank(2 * slot + m), ALU.mult)
                    if m == 1:
                        o.then_inc(psum_free[slot], 1)
                    drain()
                    v.tensor_tensor(cut(gb, c, T), cut(gb, c, T), cut(ga, c, T), ALU.add).then_inc(mix_ok, 1)
                for m in range(2):
                    c = 2048 * i + (2 * s + m) * T
                    hold(dve, mixhi_ok, 4 * i + (2 * s + m + 1), "dve")
                    v.tensor_tensor(cut(mixlo, c, T), cut(gb, c, T), cut(mixhi, c, T).bitcast(F32), ALU.subtract
                                    ).then_inc(mixlo_ok, 1)

            unit_loop(dve, stage_c, mix_unit)

            stage_w = PLAN["w_o"]

            def w_o_unit(i, s):
                slot = stage_w.slot(s)
                for m in range(2):
                    c = 2048 * i + (2 * s + m) * T
                    if m == 0:
                        hold(dve, tile0_done, 2 * i + (stage_w.z0 + s + 1), "dve")
                    else:
                        hold(dve, unit_done, 2 * i + (stage_w.u0 + s + 1), "dve")
                    o = v.scalar_tensor_tensor(cut(res1, c, T), cut(ahi, c, T).bitcast(F32), ALPHA,
                                               bank(2 * slot + m), ALU.mult, ALU.add)
                    if m == 1:
                        o.then_inc(psum_free[slot], 1)
                    drain()
                    v.scalar_tensor_tensor(cut(res1, c, T), cut(alo, c, T).bitcast(F32), ALPHA, cut(res1, c, T),
                                           ALU.mult, ALU.add).then_inc(r1_ok, 1)

            unit_loop(dve, stage_w, w_o_unit)
            layer_norm(n_1, res1, ahi, alo)

            stage_u = PLAN["ffn_up"]

            def up_unit(i, s):
                slot = stage_u.slot(s)
                for m in range(2):
                    k = 2 * i + (s + m * FT)
                    hold(dve, fa_ok, 4 * i + (2 * s + m + 1), "dve")
                    tap(fg[s][m], bank(2 * slot + m), col("ffn_w", 3 * k + 1), 1)
                    drain()
                    tap(fg[s][m], bank(2 * slot + m), col("ffn_w", 3 * k), 2).then_inc(
                        ft_ok if m == 0 else psum_free[slot], 1)
                drain()
                hold(dve, fs_ok, 2 * i + (s + 1), "dve")
                v.tensor_tensor(fg[s][1][:, :], fg[s][1][:, :], fg[s][0][:, :], ALU.mult).then_inc(ff_ok, 1)
                hold(dve, fhi_ok, 2 * i + (s + 1), "dve")
                c = 2 * T * i + s * T
                v.tensor_tensor(cut(flo, c, T), fg[s][1][:, :], cut(fhi, c, T).bitcast(F32), ALU.subtract
                                ).then_inc(flo_ok, 1)

            unit_loop(dve, stage_u, up_unit)
            stage_d = PLAN["ffn_down"]
            with dve.Fori(0, KD // 2) as i:
                for t in range(2):
                    c = 2 * T * i + t * T
                    hold(dve, unit_done, 4 * i + (stage_d.u0 + 2 * t + 2), "dve")
                    v.scalar_tensor_tensor(cut(res2, c, T), cut(ahi, c, T).bitcast(F32), ALPHA, bank(2 * t),
                                           ALU.mult, ALU.add).then_inc(psum_free[0], 1)
                    drain().then_inc(psum_free[1], 1)
                    v.scalar_tensor_tensor(cut(res2, c, T), cut(alo, c, T).bitcast(F32), ALPHA, cut(res2, c, T),
                                           ALU.mult, ALU.add).then_inc(r2_ok, 1)
            layer_norm(n_2, res2, None, None)

            for l, y in enumerate(layers):
                h_tile = lambda k: hres[:, k * L:(k + 1) * L]
                if l == 0:
                    after(dve, n_2["hi"], 1)
                    dve.wait_ge(meta_in, 16)
                scaled(y["n_pre"], h_tile, KD, f"mix_pre_{l}", 0)
                v.memset(qpad[:, :].rearrange("p (j t) -> p j t", j=4)[:, :, 0:LEAD], 0.0)
                v.memset(kpad[:, 0:WIN + LEAD], 0.0)
                v.memset(vch[:, 0:WIN + LEAD], 0.0)
                v.memset(vtok[:, 0:P], 0.0)
                for s in range(2):
                    v.memset(upad[s][:, 0:2], 0.0)
                drain().then_inc(y["pad_ok"].sem, 1)
                stage = PLAN[f"in_{l}"]
                w2 = f"conv2_w_{l}"
                for u in range(3, 9):
                    i, s = u // 2, u % 2
                    slot = stage.slot(s)
                    b = [wide(slot * 4 + 2 * m) for m in range(2)]
                    if u < 7:
                        j, up_ = u - 3, upad[u % 2]
                        after(dve, y["in_c"], j + 1)
                        drain()
                        v.tensor_tensor(split2(up_[:, 2:2 + L]), b[1], split2(cgate[u % 2][:, :]), ALU.mult
                                        ).then_inc(psum_free[slot], 1)
                        drain().then_inc(y["in_u"].sem, 1)
                        acc = yconv[:, j * L:(j + 1) * L]
                        v.tensor_scalar(acc, up_[:, 0:L], col(w2, 3 * j), None, ALU.mult)
                        for w in (1, 2):
                            drain()
                            v.scalar_tensor_tensor(acc, up_[:, w:w + L], col(w2, 3 * j + w), acc, ALU.mult, ALU.add)
                    else:
                        drain()
                        for m in range(2):
                            j = 2 * (u - 7) + m
                            if m == 0:
                                dve.wait_ge(tile0_done, stage.z0 + u + 1)
                            else:
                                dve.wait_ge(unit_done, stage.u0 + u + 1)
                            acc = split2(yconv[:, j * L:(j + 1) * L])
                            o = v.tensor_tensor(acc, acc, b[m], ALU.mult)
                            if m == 1:
                                o.then_inc(psum_free[slot], 1)
                dve.wait_ge(const2_in, 16 * (l + 1))
                cos, sin = (const2[:, CONST2[a]:CONST2[a] + L] for a in ("cos", "sin"))
                for j in range(5):
                    after(dve, y["swap_ps"], j + 1)
                    raw_t = qraw[:, j * L:(j + 1) * L]
                    dst = qpad[:, j * QPAD + LEAD:(j + 1) * QPAD] if j < 4 else kpad[:, WIN + LEAD:KPAD]
                    drain()
                    v.tensor_tensor(split2(rot[:, 0:L]), split2(sin), wide(2 * (j % 2)), ALU.mult)
                    v.tensor_tensor(rot[:, L:2 * L], raw_t, cos, ALU.mult)
                    drain()
                    v.tensor_tensor(dst, rot[:, 0:L], rot[:, L:2 * L], ALU.add).then_inc(y["rope_ok"].sem, 1)

                sinks = f"sinks_{l}"
                with dve.Fori(0, NB) as b:
                    for z in range(2):
                        hold(dve, y["sc_ps"], 2 * b + (z + 1), "dve")
                        hold(dve, y["pt_ps"], 2 * b, "dve")
                        drain()
                        s3 = sc[z][:, :].rearrange("p (j k) -> p j k", j=4)
                        v.scalar_tensor_tensor(
                            s3, PS[:, 2 * z * 512:(2 * z + 2) * 512].rearrange("p (j k) -> p j k", j=4), 0.125,
                            cut(const2, b * 256 + CONST2["mask"], 256).unsqueeze(1).to_broadcast([P, 4, 256]),
                            ALU.mult, ALU.add)
                        drain()
                        m_, se = small[:, 8 * z:8 * z + 4], small[:, 32 + 8 * z:36 + 8 * z]
                        sink = cols[:, COLS[sinks][0] + 4 * z:COLS[sinks][0] + 4 * z + 4]
                        v.tensor_reduce(m_, s3, AX_X, ALU.max)
                        drain()
                        v.tensor_tensor(m_, m_, sink, ALU.max)
                        drain()
                        v.tensor_tensor(se, sink, m_, ALU.subtract)
                        v.tensor_scalar(m_, m_, -1.0, None, ALU.mult)
                        drain().then_inc(y["neg_ok"].sem, 1)
                    for z in range(2):
                        den = small[:, 16 + 8 * z:20 + 8 * z]
                        hold(dve, y["p_ok"], 2 * b + (z + 1), "dve")
                        v.tensor_tensor(den, den, small[:, 32 + 8 * z:36 + 8 * z], ALU.add)
                        drain()
                        v.reciprocal(den, den)
                    for z in range(2):
                        den = small[:, 16 + 8 * z:20 + 8 * z]
                        hold(dve, y["o_ps"], 2 * b + (z + 1), "dve")
                        drain()
                        o3 = cut(y_tok, b * 512, 512).rearrange("p (j n) -> p j n", j=4)[:, :, 64 * z:64 * z + 64]
                        v.tensor_tensor(o3, bank(2 * z, 256).rearrange("p (j n) -> p j n", j=4),
                                        den.unsqueeze(2).to_broadcast([P, 4, 64]), ALU.mult).then_inc(y["o_ok"].sem, 1)
                after(dve, y["astd_ok"], 1)
                v.reciprocal(small[:, 56:56 + NB], small[:, 48:48 + NB])
                drain()
                with dve.Fori(0, NB) as b:
                    hold(dve, y["yt_ps"], b, "dve")
                    v.tensor_scalar(y_n[:, :], cut(y_tok, b * 512, 512), cut(small, b + 56, 1), None, ALU.mult
                                    ).then_inc(y["yn_ok"].sem, 1)
                after(dve, y["ya_ok"], NB)
                scaled(y["n_attn"], lambda k: ya[:, k * QPAD + LEAD:(k + 1) * QPAD], 4, f"attn_g_{l}", 0, False)
                drain()
                scaled(y["n_conv"], lambda k: yconv[:, k * L:(k + 1) * L], 4, f"conv_g_{l}", 4)
                after(dve, y["zc_ok"], 1)
                residual(y["n_post"], f"mix_post_{l}")
                drain()
                scaled(y["n_mpre"], h_tile, KD, f"mlp_pre_{l}", 0)
                for h in range(2):
                    stage = PLAN[f"up{h}_{l}"]
                    rl_ok, f_ok, f2hi_ok, f2lo_ok = (y[f"{a}{h}"] for a in ("rl_ok", "f_ok", "f2hi_ok", "f2lo_ok"))

                    def up_body(i, s):
                        slot = stage.slot(s)
                        for m in range(2):
                            if m == 0:
                                hold(dve, rl_ok, 2 * i + (s + 1), "dve")
                            else:
                                hold(dve, psum_free[slot], stage.used(i, s) + 1, "dve")
                            r = rl[2 * s + m]
                            v.tensor_tensor(r[:, :], r[:, :], r[:, :], ALU.mult).then_inc(f_ok.sem, 1)
                        for m in range(2):
                            c = 4 * L * i + (2 * s + m) * L
                            hold(dve, f2hi_ok, 4 * i + (2 * s + m + 1), "dve")
                            v.tensor_tensor(cut(f2lo, c, L), rl[2 * s + m][:, :], cut(f2hi, c, L).bitcast(F32),
                                            ALU.subtract).then_inc(f2lo_ok.sem, 1)

                    unit_loop(dve, stage, up_body)
                stage = PLAN[f"down1_{l}"]
                after(dve, y["zc_ok"], 2)

                def down_body(i, s):
                    slot = stage.slot(s)
                    hold(dve, unit_done, 2 * i + (stage.u0 + s + 1), "dve")
                    t = cut(zres, 2 * L * i + s * L, L)
                    v.tensor_tensor(split2(t), split2(t), wide(slot * 4), ALU.add).then_inc(psum_free[slot], 1)
                    drain().then_inc(y["dn_ok1"].sem, 1)

                unit_loop(dve, stage, down_body)
                residual(y["n_mpost"], f"mlp_post_{l}")
                drain()


def _tiles(v):
    return np.asarray(v, np.float32).reshape(-1, P).T


def _blocks(w):
    k, n = w.shape
    return w.reshape(k // P, P, n // P, P).transpose(0, 2, 1, 3)


def _stream(i):
    s = np.zeros((UNITS, P, 16, P), np.float32)

    def put(stage, u, tiles):
        for n, b in enumerate(tiles):
            s[PLAN[stage].u0 + u, :, n, :] = b

    w_in = i["w_in"][0]
    o = np.cumsum([0, 2 * D, SSM, XBC, HEADS, D, D])
    glu, z, xbc = (_blocks(w_in[:, o[j]:o[j + 1]]) for j in range(3))
    gate_a, gate_b = (_blocks(w_in[:, o[j]:o[j + 1]]) for j in (4, 5))
    dt = np.zeros((D, P), np.float32)
    dt[:, 0:HEADS] = w_in[:, o[3]:o[4]]
    put("dt", 0, _blocks(dt)[:, 0])

    def pairs(stage, b, order=None):
        order = list(range(b.shape[1])) if order is None else order
        for u in range(len(order) // 2):
            put(stage, u, [b[k, m] for m in order[2 * u:2 * u + 2] for k in range(b.shape[0])])

    def singles(stage, b):
        for m in range(b.shape[1]):
            put(stage, m, [b[k, m] for k in range(b.shape[0])])

    pairs("xbc", xbc)
    pairs("glu", glu, [t for j in range(KD) for t in (j, KD + j)])
    pairs("z", z)
    pairs("gate_b", gate_b)
    singles("ssm_out", _blocks(i["w_ssm_out"][0]))
    pairs("gate_a", gate_a)
    pairs("conv_out", _blocks(i["w_conv_out"][0]))
    pairs("w_o", _blocks(i["w_o"][0]))
    pairs("ffn_up", _blocks(i["w_ffn_up"][0]), [t for j in range(FT) for t in (j, FT + j)])
    down = _blocks(i["w_ffn_down"][0])
    for m in range(KD):
        for h in range(2):
            put("ffn_down", 2 * m + h, [down[h * (FT // 2) + k, m] for k in range(FT // 2)])
    for l in range(LAYERS):
        w = i["w_in_2"][l]
        q = w[:, 0:512].reshape(D, 2, 4, 64).transpose(0, 2, 1, 3).reshape(D, 512)
        w = _blocks(np.concatenate([q, w[:, 512:]], axis=1))
        pairs(f"in_{l}", w, [0, 1, 2, 3, 4, 5] + [t for j in range(4) for t in (10 + j, 14 + j)] + [6, 7, 8, 9])
        w = i["w_out_2"][l]
        a = w[0:512].reshape(2, 4, 64, D).transpose(1, 0, 2, 3).reshape(512, D)
        pairs(f"out_{l}", _blocks(np.concatenate([a, w[512:]], axis=0)))
        up, down = _blocks(i["w_up_2"][l]), _blocks(i["w_down_2"][l])
        for h in range(2):
            pairs(f"up{h}_{l}", up[:, h * FFH:(h + 1) * FFH])
            singles(f"down{h}_{l}", down[h * FFH:(h + 1) * FFH])
    return s.reshape(UNITS, P, UNIT)


def _columns(i):
    def taps(w):
        k, c = w.shape
        return w.reshape(k, c // P, P).transpose(2, 1, 0).reshape(P, -1)

    c = {
        "ln_in_g": _tiles(i["ln_in_g"]), "ln_in_b": _tiles(i["ln_in_b"]), "conv_w": taps(i["conv_dw_w"][0]),
        "conv_b": _tiles(i["conv_dw_b"][0]), "conv_ln_g": _tiles(i["conv_ln_g"][0]),
        "conv_ln_b": _tiles(i["conv_ln_b"][0]), "ssm_w": taps(i["ssm_conv_w"][0]), "ssm_b": _tiles(i["ssm_conv_b"][0]),
        "ssm_d": _tiles(np.repeat(i["ssm_d"][0], HEAD_P)), "ssm_norm": _tiles(i["ssm_norm_w"][0]),
        "ln1_g": _tiles(i["ln1_g"][0]), "ln1_b": _tiles(i["ln1_b"][0]), "ffn_w": taps(i["ffn_dw_w"][0]),
        "ffn_b": _tiles(i["ffn_dw_b"][0]), "ln2_g": _tiles(i["ln2_g"][0]), "ln2_b": _tiles(i["ln2_b"][0]),
        "eps5": np.full((P, 1), 1e-5, np.float32), "eps6": np.full((P, 1), 1e-6, np.float32),
    }
    for l in range(LAYERS):
        c[f"mix_pre_{l}"] = _tiles(i["mix_pre_g_2"][l])
        c[f"conv2_w_{l}"] = taps(i["conv_w_2"][l])
        c[f"attn_g_{l}"] = _tiles(i["attn_out_g_2"][l].reshape(2, 4, 64).transpose(1, 0, 2).reshape(512))
        c[f"conv_g_{l}"] = _tiles(i["conv_out_g_2"][l])
        c[f"mix_post_{l}"] = _tiles(i["mix_post_g_2"][l])
        c[f"mlp_pre_{l}"] = _tiles(i["mlp_pre_g_2"][l])
        c[f"mlp_post_{l}"] = _tiles(i["mlp_post_g_2"][l])
        c[f"sinks_{l}"] = np.broadcast_to(i["sinks_2"][l].reshape(1, QH), (P, QH))
    return np.ascontiguousarray(np.concatenate([c[n] for n in COLS], axis=1))


def _constants():
    c1 = np.zeros((P, N1), np.float32)
    c1[:, 0:128] = np.eye(P)
    c1[:, 128:256] = 1.0
    s, t = np.arange(P)[:, None], np.arange(P)[None, :]
    c1[:, 256:384] = np.where(t >= s, 0.0, NEG)
    c1[P - 1, 384:512] = 1.0
    c2 = np.zeros((P, N2), np.float32)
    cos, sin = np.ones((P, L), np.float32), np.zeros((P, L), np.float32)
    half = ROT // 2
    inv = np.power(np.float32(THETA), -np.arange(0, ROT, 2, dtype=np.float32) / np.float32(ROT)).astype(np.float32)
    ang = (np.arange(L, dtype=np.float32)[:, None] * inv[None, :]).astype(np.float32)
    for h in range(2):
        for r in range(half):
            a, b = 64 * h + r, 64 * h + half + r
            c2[b, a] = -1.0
            c2[a, b] = 1.0
            cos[a] = cos[b] = np.cos(ang[:, r])
            sin[a] = sin[b] = np.sin(ang[:, r])
    c2[:, CONST2["cos"]:CONST2["cos"] + L] = cos
    c2[:, CONST2["sin"]:CONST2["sin"] + L] = sin
    kk = np.arange(2 * WIN)[None, :]
    for b in range(NB):
        key = b * WIN + kk
        ok = (kk <= s + WIN) & (kk > s) & (key >= WIN + LEAD)
        c2[:, CONST2["mask"] + b * 256:CONST2["mask"] + (b + 1) * 256] = np.where(ok, 0.0, NEG)
    return c1, c2


def kernel(**inputs):
    import concourse.bacc as _bacc
    from concourse.bass_utils import run_bass_kernel_spmd as _run

    i = {k: np.asarray(v) for k, v in inputs.items()}
    nc = _bacc.Bacc("TRN2", target_bir_lowering=False, num_devices=1, dynamic_dma_scratch_size=1024)
    c1, c2 = _constants()
    arrays = {
        "x_t": np.ascontiguousarray(i["x"][0].T.reshape(KD, P, T).transpose(1, 0, 2)),
        "meta_t": np.ascontiguousarray(i["meta_tokens_2"].T.reshape(KD, P, META).transpose(1, 0, 2)),
        "weights": _stream(i),
        "columns": _columns(i),
        "head_params": np.ascontiguousarray(np.stack([i["ssm_dt_bias"][0], i["ssm_a_log"][0]], axis=1)),
        "const1": c1,
        "const2": c2,
    }
    d = {n: nc.dram_tensor(n, a.shape, F32, kind="ExternalInput").ap() for n, a in arrays.items()}
    acs = nc.dram_tensor("acs_rows", (HEADS + 2, T), F32, kind="Internal").ap()
    out = nc.dram_tensor("out_t", (P, KD, T), F32, kind="ExternalOutput").ap()
    build(nc, d["x_t"].rearrange("p k t -> p (k t)"), d["meta_t"], d["weights"], d["columns"], d["head_params"],
          d["const1"], d["const2"], acs, out)
    r = _run(nc, [arrays], core_ids=[0])
    o = np.asarray(r.results[0]["out_t"])
    return np.ascontiguousarray(o.transpose(2, 1, 0).reshape(1, T, D))
```

```python
import math
from contextlib import ExitStack

import numpy as np
import concourse.bass as bass
from concourse import mybir

F32 = mybir.dt.float32
F32R = mybir.dt.float32r
ALU = mybir.AluOpType
ACT = mybir.ActivationFunctionType
AX_X = mybir.AxisListType.X

P = 128
D = 1024
KD = D // P
T = 512
SSM = 2 * D
HEADS, HEAD_P = SSM // 64, 64
GROUPS, STATE, CHUNK = 4, 128, 128
CHUNKS = T // CHUNK
GH = HEADS // GROUPS
GP = GH // 2
XBC = SSM + 2 * GROUPS * STATE
XT, BT0, CT0, XBCT = SSM // P, SSM // P, SSM // P + GROUPS, XBC // P
TAPS = 31
TAPS_GATE = 3
POOL_TILE = KD - 1
POOL_TAPS = 3
FFN = 2816
FT = FFN // P
ALPHA = 2.0 ** 0.25
LAYERS = 2
META = 16
L = T + META
HALF = L // 2
WIN = 128
NB = 5
LEAD = WIN - META
QPAD = NB * WIN
KPAD = QPAD + WIN
QH = 8
FF = 4 * D
FFH = FF // P // 2
ROT, THETA = 16, 500000.0
NEG = -1.0e30
UNIT = 16 * P


class Stage:

    def __init__(self, name, u0, first_tiles, n, nm, nk):
        self.name, self.u0, self.z0, self.n, self.nm, self.nk = name, u0, first_tiles, n, nm, nk

    def slot(self, s):
        return (self.u0 + s) % 2

    def used(self, i, s):
        return (self.u0 + s) // 2 + i


def make_plan():
    plan, u, z = {}, 0, 0
    first = [("dt", 1, 1, KD), ("xbc", XBCT // 2, 2, KD), ("z_glu", 4 * GROUPS, 2, KD),
             ("gate_b", KD // 2, 2, KD), ("ssm_out", KD, 1, XT), ("gate_a", KD // 2, 2, KD),
             ("conv_out", KD // 2, 2, KD), ("w_o", KD // 2, 2, KD), ("ffn_up", FT, 2, KD),
             ("ffn_down", 2 * KD, 1, FT // 2)]
    layer = [("in", 9, 2, KD), ("out", KD // 2, 2, KD), ("up0", FFH // 2, 2, KD), ("down0", KD, 1, FFH),
             ("up1", FFH // 2, 2, KD), ("down1", KD, 1, FFH)]
    for name, n, nm, nk in first + [(f"{a}_{l}", n, nm, nk) for l in range(LAYERS) for a, n, nm, nk in layer]:
        plan[name] = Stage(name, u, z, n, nm, nk)
        u += n
        z += n if nm == 2 else 0
    return plan, u


PLAN, UNITS = make_plan()

COLS = {}


def _place_cols():
    at = 0
    for name, n in [("ln_in_g", KD), ("ln_in_b", KD), ("conv_w", KD * TAPS), ("conv_b", KD), ("conv_ln_g", KD),
                    ("conv_ln_b", KD), ("ssm_w", XBCT * 4), ("ssm_b", XBCT), ("ssm_d", XT), ("ssm_norm", XT),
                    ("ln1_g", KD), ("ln1_b", KD), ("ffn_w", 2 * FT * 3), ("ffn_b", 2 * FT), ("ln2_g", KD),
                    ("ln2_b", KD)] + [(f"{a}_{l}", n) for l in range(LAYERS) for a, n in
                                      [("mix_pre", KD), ("conv2_w", 4 * 3), ("attn_g", 4), ("conv_g", 4),
                                       ("mix_post", KD), ("mlp_pre", KD), ("mlp_post", KD), ("sinks", QH)]] + [
                   ("eps5", 1), ("eps6", 1)]:
        COLS[name] = (at, n)
        at += n
    return at


NCOLS = _place_cols()
CONST1 = {"ident": 0, "ones": 128, "causal": 256, "last": 384}
N1 = 512
CONST2 = {"rope_p": 0, "cos": 128, "sin": 128 + L, "mask": 128 + 2 * L}
N2 = 128 + 2 * L + NB * 256


def build(nc, xT, metaT, wstream, cols_d, heads_d, const1_d, const2_d, acs_d, outT):
    ctx = ExitStack()
    with ctx:
        sems = {}

        def sem(name):
            sems[name] = ctx.enter_context(nc.semaphore(name))
            return sems[name]

        top = [1152]

        def fixed(name, n, dt=F32):
            at = top[0]
            top[0] += 4 * n
            return nc.alloc_sbuf_tensor_at(name, [P, n], dt, offset=at)

        const1 = fixed("const1", N1)
        cols = fixed("cols", NCOLS + (-NCOLS) % 8)
        raw = [fixed(f"raw{s}", UNIT) for s in range(2)]
        whi = [fixed(f"whi{s}", UNIT, F32R) for s in range(2)]
        wlo = [fixed(f"wlo{s}", UNIT, F32R) for s in range(2)]
        ahi = fixed("ahi", KD * L, F32R)
        alo = fixed("alo", KD * L, F32R)
        mu, std, rstd = fixed("mu", L), fixed("std", L), fixed("rstd", L)
        R = top[0]
        R_END = 228200 // 32 * 32

        def at(name, off, n, dt=F32, parts=P):
            assert R + off + 4 * n <= R_END, (name, R + off + 4 * n - R_END)
            return nc.alloc_sbuf_tensor_at(name, [parts, n], dt, offset=R + off)

        TB = 4 * T
        H0 = (R_END - R - 4 * KD * L) // 32 * 32
        x_in = at("x_in", 32 * TB, KD * T)
        xbc = at("xbc", 0, XBCT * T)
        ssd0 = 24 * TB
        xdt = at("xdt", ssd0, 4 * T)
        xds = at("xds", ssd0 + 4 * TB, 3 * T)
        st = at("st", ssd0 + 7 * TB, 3 * T)
        b_slot = at("b_slot", ssd0 + 10 * TB, T)
        bt_sb = at("bt_sb", ssd0 + 11 * TB, T)
        acs_b = [at(f"acs_b{s}", ssd0 + (12 + s) * TB, T) for s in range(2)]
        m_slot = [at(f"m_slot{s}", ssd0 + (14 + s) * TB, T) for s in range(2)]
        c_slot = [at(f"c_slot{s}", ssd0 + (16 + s) * TB, T) for s in range(2)]
        x_slot = c_slot
        tok = at("tok", ssd0 + 18 * TB, 256)
        ends = at("ends", ssd0 + 18 * TB + 1024, 256)
        zs = [at(f"zs{j}", ssd0 + (19 + j) * TB, T) for j in range(GP)]
        dtt = [at(f"dtt{s}", ssd0 + (23 + s) * TB, T, parts=32) for s in range(8)]
        heads = at("heads", ssd0 + 31 * TB, 8, parts=32)
        yn_lo = at("yn_lo", 0, XT * T, F32R)
        yn_hi = at("yn_hi", 16 * TB, XT * T, F32R)
        VW = T + TAPS - 1
        v0 = ssd0 + 23 * TB
        vpad = at("vpad", v0, KD * VW)
        vo0 = v0 + 4 * KD * VW + (-4 * KD * VW) % 64
        vout = at("vout", vo0, KD * T)
        t0 = ssd0 + 16 * TB
        rst4 = sumsq = at("sumsq", t0, 4 * T)
        ring = [at(f"ring{s}", t0 + s * TB, T) for s in range(2)]
        ysq = [at(f"ysq{s}", t0 + (4 + s) * TB, T) for s in range(2)]
        prod = ysq
        sq1 = ysq
        acc1 = at("acc1", t0 + 6 * TB, T)
        sig = [mu, std]
        cbm = at("cbm", vo0 + 8 * TB, T)
        gb = at("gb", ssd0 + 8 * TB, KD * T)
        ga = at("ga", 8 * TB, KD * T)
        chi = at("chi", 16 * TB, KD * T, F32R)
        clo = at("clo", 0, KD * T, F32R)
        mixhi = at("mixhi", 24 * TB, KD * T, F32R)
        mixlo = at("mixlo", v0, KD * T, F32R)
        res1 = at("res1", vo0, KD * T)
        fhi = at("fhi", 0, FT * T, F32R)
        flo = at("flo", FT * TB, FT * T, F32R)
        fg = [[at(f"fg{s}{m}", (2 * FT + 2 * s + m) * TB, T) for m in range(2)] for s in range(2)]
        res2 = at("res2", (2 * FT + 4) * TB, KD * T)
        assert (2 * FT + 4 + KD) * TB <= H0
        LB = 4 * L
        hres = at("hres", H0, KD * L)
        const2 = at("const2", 0, N2)
        q0 = 4 * N2 + (-4 * N2) % 64
        qpad = at("qpad", q0, 4 * QPAD)
        kpad = at("kpad", q0 + 16 * QPAD, KPAD)
        vch = at("vch", q0 + 16 * QPAD + 4 * KPAD, KPAD)
        vtok = at("vtok", q0 + 16 * QPAD + 8 * KPAD, KPAD)
        c0 = q0 + 16 * QPAD + 12 * KPAD
        qraw = at("qraw", c0, 5 * L)
        yconv = at("yconv", c0 + 5 * LB, 4 * L)
        UP = L + 8
        cgate = [at(f"cgate{s}", c0 + 9 * LB + s * LB, L) for s in range(2)]
        upad = [at(f"upad{s}", c0 + 11 * LB + 4 * s * UP, UP) for s in range(2)]
        rot = at("rot", c0 + 11 * LB + 8 * UP, 2 * L)
        a0 = c0 + 13 * LB + 8 * UP
        sc = [at(f"sc{z}", a0 + 8192 * z, 1024) for z in range(2)]
        pT = [at(f"pT{z}", a0 + 8192 * z + 4096, 1024) for z in range(2)]
        small = at("small", c0, 64)
        diag = [at(f"diag{s}", c0 + 256 + 512 * s, P) for s in range(2)]
        y_tok = at("y_tok", a0 + 16384, NB * 512)
        zres = at("zres", 0, KD * L)
        f2hi = at("f2hi", KD * LB, FFH * L, F32R)
        f2lo = at("f2lo", (KD + FFH) * LB, FFH * L, F32R)
        rl = [at(f"rl{s}", (KD + 2 * FFH + s) * LB, L) for s in range(4)]
        s0 = (KD + 2 * FFH + 4) * LB
        sq3 = [at(f"sq3{s}", s0 + s * LB, L) for s in range(2)]
        acc2 = at("acc2", s0 + 2 * LB, L)
        nv = [at(f"nv{s}", s0 + (3 + s) * LB, L) for s in range(2)]
        ya = at("ya", s0 + 5 * LB, 4 * L)
        rstd_sq = mu
        assert a0 + 16384 + 2048 * NB <= s0 and s0 + 9 * LB <= H0, (a0, s0, H0)

        PS = ctx.enter_context(nc.psum_tensor("PS", [P, 8 * 512], F32))

        def bank(b, n=512, off=0, parts=P):
            return PS[0:parts, b * 512 + off:b * 512 + off + n]

        def wide(b):
            return PS[:, b * 512:(b + 2) * 512].rearrange("p (a c) -> p a c", a=2)[:, :, 0:HALF]

        def split2(ap):
            return ap.rearrange("p (a c) -> p a c", a=2)

        def col(name, k):
            a = COLS[name][0]
            if isinstance(k, int):
                return cols[:, a + k:a + k + 1]
            return cols[:, bass.ds(k + a, 1)]

        def cut(t, start, n):
            return t[:, start:start + n] if isinstance(start, int) else t[:, bass.ds(start, n)]

        ident, ones = const1[:, 0:128], const1[:, 128:256]
        causal, last_row = const1[:, 256:384], const1[:, 384:512]

        params_in, x_in_s, meta_in, const2_in = sem("params_in"), sem("x_loaded"), sem("meta_in"), sem("const2_in")
        raw_in = [sem(f"raw_in{s}") for s in range(2)]
        hi_ready, lo_ready = sem("whi_ready"), sem("wlo_ready")
        unit_done, tile0_done = sem("unit_done"), sem("tile0_done")
        psum_free = [sem(f"psum_free{s}") for s in range(2)]
        out_done = sem("out_done")
        turn = {e: sem(f"turn_{e}") for e in ("pe", "act", "dve", "pool", "sp")}

        class Counter:

            def __init__(self, s, base=0):
                self.sem, self.base = s, base

        def norm_sems(name, what="pe act dve hi lo"):
            return {a: sem(f"{name}_{a}") for a in what.split()}

        def after(eng, counter, value):
            eng.wait_ge(counter.sem, value + counter.base)

        n_in, n_conv, n_1, n_2 = ({a: Counter(s) for a, s in norm_sems(name).items()}
                                  for name in ("ln_in", "ln_conv", "ln1", "ln2"))
        dt_exp, dt_ready, dt_ps, dt_tok, end_ps, end_in, ends_ok = (
            sem(a) for a in ("dt_exp", "dt_ready", "dt_tok_ps", "dt_tok", "end_ps", "end_in", "ends_ok"))
        conv4_acc, conv4_tap, conv4_out = sem("conv4_acc"), sem("conv4_tap"), sem("conv4_out")
        scratch_in = sem("acs_stored")
        acs_in = [sem(f"acs_in{s}") for s in range(2)]
        (b_ok, bt_ps, bt_ok, cb_ps, x_ok, xt_ps, xdt_ok, xds_ok, st_ps, st_ok, cbm_ok, exp_ok, mc_ok, y_mm, y_ok) = (
            sem(a) for a in ("b_ok", "bt_ps", "bt_ok", "cb_ps", "x_ok", "xt_ps", "xdt_ok", "xds_ok", "st_ps",
                             "st_ok", "cbm_ok", "exp_ok", "mc_ok", "y_mm", "y_ok"))
        sig_ok, v_ok = sem("sig_ok"), sem("glu_used")
        zs_ok, yg_ok, ysq_ok, ysq_sum = sem("zs_ok"), sem("yg_ok"), sem("ysq_ok"), sem("ysq_sum")
        ss_ps, ss_std, ss_rstd = sem("ss_ps"), sem("ss_std"), sem("ss_rstd")
        y_normed, yhi_ok, ylo_ok = sem("y_normed"), sem("yhi_ok"), sem("ylo_ok")
        xin_ok, vout_ok = sem("xin_ok"), sem("vout_ok")
        prod_ok, prod_used, vout_first, ring_ok, ring_used = (sem(a) for a in ("tap_prod", "tap_used", "tap_first", "ring_ok", "ring_used"))
        mix_ok, mixhi_ok, mixlo_ok = sem("mix_ok"), sem("mixhi_ok"), sem("mixlo_ok")
        r1_ok, r2_ok = sem("r1_ok"), sem("r2_ok")
        fa_ok, ft_ok, fs_ok, ff_ok, fhi_ok, flo_ok = (sem(a) for a in ("ffn_acc", "ffn_tap0", "ffn_silu", "ffn_prod",
                                                                      "ffn_hi", "ffn_lo"))

        STEPS = 2 * NB
        per_layer = {
            "c_ok": 4, "yc_ok": 4, "swap_ps": 5, "rope_ok": 5, "vch_ok": 1, "v_ps": 1, "v_ok": 1, "sc_ps": STEPS,
            "sc_ok": STEPS, "neg_ok": STEPS, "p_ok": STEPS, "pt_ps": STEPS, "pt_ok": STEPS, "o_ps": STEPS,
            "o_ok": STEPS, "astd_ok": NB, "dg_ok": NB, "yt_ps": NB, "ya_ok": NB, "zc_ok": 1, "pad_ok": 1, "dn_ok1": KD,
            "rl_ok0": FFH, "f_ok0": FFH, "f2hi_ok0": FFH, "f2lo_ok0": FFH,
            "rl_ok1": FFH, "f_ok1": FFH, "f2hi_ok1": FFH, "f2lo_ok1": FFH}
        norms = {"pre": (KD, "sq acc pe std hi lo"), "conv": (4, "sq acc pe std dve hi lo"), "attn": (4, "hi lo"),
                 "post": (KD, "sq acc pe std dve"), "mpre": (KD, "sq acc pe std hi lo"), "mpost": (KD, "sq acc pe std dve")}
        layer_sems = {a: sem(a) for a in per_layer}
        norm_sem = {a: norm_sems(a, what) for a, (_, what) in norms.items()}

        def layer_counters(l):
            y = {a: Counter(layer_sems[a], l * n) for a, n in per_layer.items()}
            for a, (nk, _) in norms.items():
                y["n_" + a] = {e: Counter(s, l * (1 if e in ("pe", "std") else nk)) for e, s in norm_sem[a].items()}
            return y

        layers = [layer_counters(l) for l in range(LAYERS)]

        block = ctx.enter_context(nc.Block())

        def hold(eng, s, value, who):
            if isinstance(s, Counter):
                s, value = s.sem, value + s.base
            if isinstance(value, int):
                assert value >= 0
                if value > 0:
                    eng.wait_ge(s, value)
            else:
                eng.wait_ge(s, value)
                eng.sem_inc(turn[who])

        def unit_loop(eng, stage, body, tail=0):
            pairs = (stage.n - tail) // 2
            if pairs > 0:
                with eng.Fori(0, pairs) as i:
                    for s in range(2):
                        body(i, s)
            for u in range(2 * pairs, stage.n):
                body(u // 2, u % 2)

        @block.sync
        def _(sp):
            sp.dma_start(const1[:, :], const1_d).then_inc(params_in, 16)
            sp.dma_start(cols[:, 0:NCOLS], cols_d).then_inc(params_in, 16)
            sp.dma_start(heads[:, 0:2], heads_d).then_inc(params_in, 16)
            sp.dma_start(x_in[:, :], xT).then_inc(x_in_s, 16)
            for s in range(2):
                sp.dma_start(raw[s][:, :], wstream[s]).then_inc(raw_in[s], 16)
            with sp.Fori(1, UNITS // 2) as i:
                for s in range(2):
                    sp.wait_ge(lo_ready, 2 * i + s - 1)
                    sp.dma_start(raw[s][:, :], wstream[bass.ds(2 * i + s, 1)].rearrange("a p n -> (a p) n")
                                 ).then_inc(raw_in[s], 16)
            for u in range(UNITS // 2 * 2, UNITS):
                sp.wait_ge(lo_ready, u - 1)
                sp.dma_start(raw[u % 2][:, :], wstream[u]).then_inc(raw_in[u % 2], 16)
            for k in range(KD):
                after(sp, layers[-1]["n_mpost"]["dve"], k + 1)
                sp.dma_start(outT[:, k, :], hres[:, k * L + META:(k + 1) * L]).then_inc(out_done, 16)
            sp.wait_ge(out_done, 16 * KD)

        @block.gpsimd
        def _(pool):
            def low(s, value):
                hold(pool, hi_ready, value, "pool")
                nc.gpsimd.tensor_tensor(wlo[s][:, :], raw[s][:, :], whi[s][:, :].bitcast(F32),
                                        ALU.subtract).then_inc(lo_ready, 1)

            def lows(first, end):
                if first % 2:
                    low(1, first + 1)
                if (first + 1) // 2 < end // 2:
                    with pool.Fori((first + 1) // 2, end // 2) as i:
                        for s in range(2):
                            low(s, 2 * i + s + 1)
                if end % 2:
                    low(0, end)

            stage = PLAN["z_glu"]
            n = stage.n // GROUPS
            lows(0, stage.u0 + 2)
            with pool.Fori(0, GROUPS) as g:
                def z_low(u):
                    low(stage.slot(u % 2), g * n + (stage.u0 + u + 1))

                def gated(j):
                    hold(pool, y_ok, g * GP + (j + 1), "pool")
                    hold(pool, zs_ok, 2 * g + (j // 2 + 1), "pool")
                    t = cut(xbc, g * (GP * T) + j * T, T)
                    nc.gpsimd.tensor_tensor(t, t, zs[j][:, :], ALU.mult).then_inc(yg_ok, 1)

                z_low(2)
                z_low(3)
                gated(0)
                gated(1)
                z_low(4)
                gated(2)
                gated(3)
                z_low(5)
            first = PLAN["ssm_out"].u0
            lows(stage.u0 + stage.n + 2, first)
            pool.wait_ge(vout_first, 1)
            turns = (TAPS - 1) // POOL_TAPS
            assert turns * POOL_TAPS == TAPS - 1 and turns % 2 == 0
            with pool.Fori(0, turns // 2) as i:
                for s in range(2):
                    low((first + s) % 2, 2 * i + (first + s + 1))
                    for w in range(POOL_TAPS):
                        acc = vout[:, POOL_TILE * T:(POOL_TILE + 1) * T]
                        hold(pool, prod_ok, 2 * POOL_TAPS * i + (POOL_TAPS * s + w + 1), "pool")
                        nc.gpsimd.drain()
                        nc.gpsimd.tensor_tensor(acc, acc, prod[(POOL_TAPS * s + w) % 2][:, :], ALU.add).then_inc(prod_used, 1)
            lows(first + turns, UNITS)

        @block.tensor
        def _(pe):
            def passes(out, wslot, blk, hi, lo, first, last):
                wh, wl = whi[wslot][:, blk * P:(blk + 1) * P], wlo[wslot][:, blk * P:(blk + 1) * P]
                n = len(out)
                for o, h in zip(out, hi):
                    nc.tensor.matmul(o, wh, h, start=first, stop=False)
                for o, h in zip(out, lo):
                    nc.tensor.matmul(o, wh, h, start=False, stop=False)
                for j in range(n):
                    mm = nc.tensor.matmul(out[j], wl, hi[j], start=False, stop=last)
                return mm

            def claim(stage, i, s):
                hold(pe, lo_ready, stage.u0 + s + 1 + 2 * i, "pe")
                hold(pe, psum_free[stage.slot(s)], stage.used(i, s), "pe")

            def tile(stage, hi, lo, width, parts, s, m, ks, base=None):
                slot = stage.slot(s)
                base = slot * 2 * parts if base is None else base
                out = [bank(base + m * parts + h, width) for h in range(parts)]
                for k in ks:
                    cs = [k * width * parts + h * width for h in range(parts)]
                    mm = passes(out, slot, m * stage.nk + k, [hi[:, c:c + width] for c in cs],
                                [lo[:, c:c + width] for c in cs], k == 0, k == stage.nk - 1)
                if ks[-1] == stage.nk - 1:
                    mm.then_inc(tile0_done if m < stage.nm - 1 else unit_done, 1)

            def linear(stage, hi, lo, width, parts=1, ready=None, together=0, hooks=None, amid=None,
                       end=None):
                hooks, amid, end = hooks or {}, amid or {}, end or stage.n
                every = range(stage.nk)

                def unit(i, s):
                    claim(stage, i, s)
                    for m in range(stage.nm):
                        if m and isinstance(i, int) and 2 * i + s in amid:
                            amid[2 * i + s]()
                        tile(stage, hi, lo, width, parts, s, m, every)

                def early(units, ks):
                    for k in ks:
                        ready(k)
                        for s in units:
                            for m in range(stage.nm):
                                tile(stage, hi, lo, width, parts, s, m, [k])

                straight = max([2 if ready else 0] + [u + 1 for u in (*hooks, *amid)])
                straight = min(straight + straight % 2, end)
                for u in range(straight):
                    i, s = u // 2, u % 2
                    if ready and u == 0:
                        claim(stage, 0, 0)
                        if together:
                            claim(stage, 0, 1)
                            early((0, 1), range(together))
                        early((0,), range(together, stage.nk))
                    elif together and u == 1:
                        for m in range(stage.nm):
                            tile(stage, hi, lo, width, parts, 1, m, range(together, stage.nk))
                    else:
                        unit(i, s)
                    if u in hooks:
                        hooks[u]()
                if straight // 2 < end // 2:
                    with pe.Fori(straight // 2, end // 2) as i:
                        for s in range(2):
                            unit(i, s)
                if straight < end and end % 2:
                    unit(end // 2, 0)

            def sum_tiles(b, tile, n, ready, value, done, parts=1, width=T):
                for k in range(n):
                    after(pe, ready, value(k))
                    t = tile(k)
                    for h in range(parts):
                        mm = nc.tensor.matmul(bank(b + h, width), ones, t[:, h * width:(h + 1) * width],
                                              start=(k == 0), stop=(k == n - 1))
                    mm.then_inc(done.sem, 1)

            def mean(n, ready):
                pe.wait_ge(ready, KD)
                nc.tensor.matmul(bank(4), ones, acc1[:, :], start=True, stop=True).then_inc(n["pe"].sem, 1)

            def variance(n):
                sum_tiles(6, lambda k: sq1[k % 2], KD, n["act"], lambda k: 1 + k, n["pe"])

            def normed(n):
                return lambda k: after(pe, n["lo"], k + 1)

            def sum_squares(n, nk, b):
                after(pe, n["acc"], nk)
                for h in range(2):
                    mm = nc.tensor.matmul(bank(b + h, HALF), ones, acc2[:, h * HALF:(h + 1) * HALF], start=True, stop=True)
                mm.then_inc(n["pe"].sem, 1)

            def unscaled(n, stage, end=None):
                slot = stage.slot(0)

                def sums():
                    pe.wait_ge(psum_free[slot], stage.used(0, 0) + 1)
                    sum_squares(n, KD, slot * 4 + 2)

                linear(stage, ahi, alo, HALF, 2, normed(n), 4, {1: sums}, {2: lambda: after(pe, n["std"], 1)}, end)

            def free_banks(stage):
                for k in range(2):
                    pe.wait_ge(psum_free[stage.slot(k)], stage.used(0, k))

            pe.wait_ge(params_in, 48)
            mean(n_in, xin_ok)
            variance(n_in)
            linear(PLAN["dt"], ahi, alo, T, ready=normed(n_in))
            linear(PLAN["xbc"], ahi, alo, T)

            pe.wait_ge(dt_ready, 2)
            for j, t in enumerate((dtt[6], dtt[5])):
                for c in range(CHUNKS):
                    mm = nc.tensor.transpose(bank(4, 32, j * 128 + c * 32), t[0:32, c * P:(c + 1) * P],
                                             const1[0:32, 0:32])
            mm.then_inc(dt_ps, 1)
            pe.wait_ge(dt_tok, 1)
            nc.tensor.matmul(bank(5, 128), last_row, tok[:, 0:128], start=True, stop=True).then_inc(end_ps, 1)
            pe.wait_ge(ends_ok, 1)
            stage = PLAN["z_glu"]
            with pe.Fori(0, GROUPS) as g:
                def z_glu(u, m):
                    if m == 0:
                        claim(stage, 2 * g + u // 2, u % 2)
                    tile(stage, ahi, alo, T, 1, u % 2, m, range(KD), 4 + 2 * stage.slot(u % 2))

                def x_transposes(j):
                    hold(pe, x_ok, g * GP + (j + 1), "pe")
                    hold(pe, xdt_ok, g * GP + max(j - 1, 0), "pe")
                    for c in range(CHUNKS):
                        mm = nc.tensor.transpose(bank(j % 2, P, c * P), x_slot[j % 2][:, c * P:(c + 1) * P], ident)
                    mm.then_inc(xt_ps, 1)

                def head(q):
                    j, hh = q // 2, q % 2
                    if hh == 0:
                        hold(pe, y_ok, g * GP + max(j - 1, 0), "pe")
                    hold(pe, mc_ok, g * GH + (q + 1), "pe")
                    for c in range(CHUNKS):
                        o = PS[64 * hh:64 * hh + 64, (j % 2) * 512 + c * P:(j % 2) * 512 + (c + 1) * P]
                        mm = nc.tensor.matmul(o, xdt[:, c * T + q * 64:c * T + q * 64 + 64],
                                              m_slot[hh][:, c * P:(c + 1) * P], start=True, stop=(c == 0))
                        if c:
                            mm = nc.tensor.matmul(o, st[:, (c - 1) * T + q * 64:(c - 1) * T + q * 64 + 64],
                                                  c_slot[hh][:, c * P:(c + 1) * P], start=False, stop=True)
                    mm.then_inc(y_mm, 1)

                hold(pe, b_ok, g + 1, "pe")
                hold(pe, st_ok, g, "pe")
                for c in range(CHUNKS - 1):
                    mm = nc.tensor.transpose(bank(2, P, c * P), b_slot[:, c * P:(c + 1) * P], ident)
                mm.then_inc(bt_ps, 1)
                hold(pe, cbm_ok, g, "pe")
                for c in range(CHUNKS):
                    mm = nc.tensor.matmul(bank(3, P, c * P), b_slot[:, c * P:(c + 1) * P],
                                          cut(xbc, g * T + (CT0 * T + c * P), P), start=True, stop=True)
                mm.then_inc(cb_ps, 1)
                z_glu(0, 0)
                hold(pe, y_ok, g * GP, "pe")
                x_transposes(0)
                x_transposes(1)
                z_glu(0, 1)
                x_transposes(2)
                x_transposes(3)
                z_glu(1, 0)
                hold(pe, xds_ok, g + 1, "pe")
                hold(pe, bt_ok, g + 1, "pe")
                for c in range(CHUNKS - 1):
                    mm = nc.tensor.matmul(bank(c), bt_sb[:, c * P:(c + 1) * P], xds[:, c * T:(c + 1) * T],
                                          start=True, stop=True)
                mm.then_inc(st_ps, 1)
                z_glu(1, 1)
                hold(pe, st_ok, g + 1, "pe")
                head(0)
                head(1)
                z_glu(2, 0)
                head(2)
                head(3)
                z_glu(2, 1)
                head(4)
                head(5)
                z_glu(3, 0)
                head(6)
                head(7)
                z_glu(3, 1)

            pe.wait_ge(y_ok, XT)

            def group_sums():
                pe.wait_ge(ysq_sum, XT)
                pe.wait_ge(v_ok, KD)
                for g in range(GROUPS):
                    mm = nc.tensor.matmul(bank(4 + g), ones, sumsq[:, g * T:(g + 1) * T], start=True, stop=True)
                mm.then_inc(ss_ps, 1)

            def conv_variance():
                variance(n_conv)

            def conv_mean():
                pe.wait_ge(ss_std, GROUPS)
                mean(n_conv, vout_ok)

            linear(PLAN["gate_b"], ahi, alo, T, hooks={1: group_sums})
            linear(PLAN["ssm_out"], yn_hi, yn_lo, T, ready=lambda k: pe.wait_ge(ylo_ok, k + 1))
            linear(PLAN["gate_a"], ahi, alo, T, hooks={1: conv_mean, 2: conv_variance})
            linear(PLAN["conv_out"], chi, clo, T, ready=normed(n_conv), together=4)
            linear(PLAN["w_o"], mixhi, mixlo, T, ready=lambda k: pe.wait_ge(mixlo_ok, k + 1))
            mean(n_1, r1_ok)
            variance(n_1)
            linear(PLAN["ffn_up"], ahi, alo, T, ready=normed(n_1), together=4)

            stage = PLAN["ffn_down"]
            for k in range(2):
                pe.wait_ge(psum_free[k], (stage.u0 + 1 - k) // 2)
            with pe.Fori(0, KD // 2) as i:
                for t in range(2):
                    base = (stage.u0 + 1) // 2
                    hold(pe, psum_free[0], base + 2 * i + (t - 1), "pe")
                    for s in range(2):
                        slot = stage.slot(s)
                        hold(pe, lo_ready, stage.u0 + 4 * i + (2 * t + s + 1), "pe")
                        for k in range(FT // 2):
                            kk = s * (FT // 2) + k
                            if k in (0, FT // 2 - 2):
                                pe.wait_ge(flo_ok, kk + (FT // 2 - 2 if k == 0 else 2))
                            mm = passes([bank(2 * t)], slot, k, [fhi[:, kk * T:(kk + 1) * T]],
                                        [flo[:, kk * T:(kk + 1) * T]], kk == 0, kk == FT - 1)
                        mm.then_inc(unit_done, 1)
            mean(n_2, r2_ok)
            variance(n_2)

            for l, y in enumerate(layers):
                stage = PLAN[f"in_{l}"]
                unscaled(y["n_pre"], stage, 3)
                near, far = stage.slot(1) * 4, stage.slot(0) * 4

                def part(u, m, ks=range(KD)):
                    if m == 0 and ks[0] == 0:
                        i, s = (u - 1) // 2, (u - 1) % 2
                        pe.wait_ge(lo_ready, stage.u0 + u + 1)
                        if u == 3:
                            pe.wait_ge(psum_free[stage.slot(1)], stage.used(0, 1) + 1)
                        else:
                            pe.wait_ge(psum_free[stage.slot(s)], stage.used(i, s) + 1)
                    tile(stage, ahi, alo, HALF, 2, u % 2, m, ks, near)

                def swap(j):
                    if j >= 2:
                        after(pe, y["rope_ok"], j - 1)
                    for h in range(2):
                        mm = nc.tensor.matmul(bank(far + 2 * (j % 2) + h, HALF), const2[:, 0:128],
                                              qraw[:, j * L + h * HALF:j * L + (h + 1) * HALF], start=True, stop=True)
                    mm.then_inc(y["swap_ps"].sem, 1)

                pe.wait_ge(psum_free[stage.slot(0)], stage.used(1, 0) + 1)
                pe.wait_ge(const2_in, 16 * (l + 1))
                swap(0)
                swap(1)
                part(3, 0)
                swap(2)
                swap(3)
                part(3, 1)
                swap(4)
                after(pe, y["rope_ok"], 4)
                after(pe, y["vch_ok"], 1)
                for b in range(NB):
                    mm = nc.tensor.transpose(bank(far + 2 + b // 4, P, (b % 4) * P), vch[:, (b + 1) * P:(b + 2) * P], ident)
                mm.then_inc(y["v_ps"].sem, 1)
                after(pe, y["rope_ok"], 5)

                def scores(n):
                    b, z = n // 2, n % 2
                    if n:
                        after(pe, y["sc_ok"], n)
                    for j in range(4):
                        mm = nc.tensor.matmul(bank(far + j // 2, 256, (j % 2) * 256),
                                              qpad[64 * z:64 * z + 64, j * QPAD + b * WIN:j * QPAD + (b + 1) * WIN],
                                              kpad[64 * z:64 * z + 64, b * WIN:(b + 2) * WIN], start=True, stop=True)
                    mm.then_inc(y["sc_ps"].sem, 1)

                def turn_p(n):
                    after(pe, y["p_ok"], n + 1)
                    if n:
                        after(pe, y["o_ok"], n)
                    else:
                        after(pe, y["v_ok"], 1)
                    if n >= 3 and n % 2:
                        after(pe, y["ya_ok"], n // 2)
                    for kb in range(2):
                        for j in range(4):
                            mm = nc.tensor.transpose(bank(far + 2 + kb, P, j * P),
                                                     sc[n % 2][:, j * 256 + kb * P:j * 256 + (kb + 1) * P], ident)
                    mm.then_inc(y["pt_ps"].sem, 1)

                def outputs(n):
                    b, z = n // 2, n % 2
                    after(pe, y["pt_ok"], n + 1)
                    for j in range(4):
                        for kb in range(2):
                            v0_ = (b + kb) * WIN + 64 * z
                            mm = nc.tensor.matmul(bank(far + 2, 64, j * 64),
                                                  pT[z][:, kb * 512 + j * P:kb * 512 + (j + 1) * P],
                                                  vtok[:, v0_:v0_ + 64], start=(kb == 0), stop=(kb == 1))
                    mm.then_inc(y["o_ps"].sem, 1)

                def turn_y(b):
                    after(pe, y["dg_ok"], b + 1)
                    for j in range(4):
                        mm = nc.tensor.matmul(bank(far + 3, P, j * P), y_tok[:, b * 512 + j * P:b * 512 + (j + 1) * P],
                                              diag[b % 2][:, :], start=True, stop=True)
                    mm.then_inc(y["yt_ps"].sem, 1)

                for n in range(STEPS):
                    u, m = 4 + n // 2, n % 2
                    if n:
                        turn_p(n - 1)
                    scores(n)
                    part(u, m, range(KD // 2))
                    if n:
                        outputs(n - 1)
                    if n >= 3 and n % 2:
                        turn_y((n - 3) // 2)
                    part(u, m, range(KD // 2, KD))
                turn_p(STEPS - 1)
                outputs(STEPS - 1)
                free_banks(PLAN[f"out_{l}"])
                sum_squares(y["n_conv"], 4, near)
                turn_y(NB - 1)
                after(pe, y["n_conv"]["std"], 1)
                after(pe, y["ya_ok"], NB)

                def mixed(k):
                    after(pe, y["n_attn" if k < 4 else "n_conv"]["lo"], k % 4 + 1)

                stage = PLAN[f"out_{l}"]
                linear(stage, ahi, alo, HALF, 2, mixed, 4)
                up = PLAN[f"up0_{l}"]
                free_banks(up)
                sum_squares(y["n_post"], KD, 0)
                unscaled(y["n_mpre"], up)
                for h in range(2):
                    if h:
                        linear(PLAN[f"up{h}_{l}"], ahi, alo, HALF, 2)
                    f2lo_ok = y[f"f2lo_ok{h}"]
                    linear(PLAN[f"down{h}_{l}"], f2hi, f2lo, HALF, 2, lambda k: after(pe, f2lo_ok, k + 1))
                sum_squares(y["n_mpost"], KD, 0)

        @block.scalar
        def _(act):
            drain = nc.scalar.drain

            def split_first(u):
                act.wait_ge(raw_in[u % 2], 16 * (u // 2 + 1))
                nc.scalar.activation(whi[u % 2][:, :], raw[u % 2][:, :], ACT.Copy).then_inc(hi_ready, 1)

            def split_next(stage, i, s):
                if isinstance(i, int) and stage.u0 + 2 * i + s + 2 >= UNITS:
                    hold(act, unit_done, stage.u0 + s + 2 * i + 1, "act")
                    return
                slot = stage.slot(s)
                hold(act, unit_done, stage.u0 + s + 1 + 2 * i, "act")
                hold(act, raw_in[slot], 16 * i + 16 * ((stage.u0 + s) // 2 + 2), "act")
                nc.scalar.activation(whi[slot][:, :], raw[slot][:, :], ACT.Copy).then_inc(hi_ready, 1)

            def evacuate(stage, body, tail=0):
                def unit(i, s):
                    split_next(stage, i, s)
                    body(i, s, stage.slot(s))
                unit_loop(act, stage, unit, tail)

            def ln_squares(n, src):
                for k in range(KD):
                    after(act, n["dve"], k + 1)
                    if k >= 2:
                        after(act, n["pe"], k)
                    nc.scalar.activation(sq1[k % 2][:, :], src[:, k * T:(k + 1) * T], ACT.Square).then_inc(n["act"].sem, 1)

            def ln_std(n):
                after(act, n["pe"], KD + 1)
                nc.scalar.activation(std[:, 0:T], bank(6), ACT.Sqrt, bias=col("eps5", 0), scale=1.0 / D
                                     ).then_inc(n["act"].sem, 1)

            def ln_out(n, src, g, b, func, dst, hi, tiles=range(KD)):
                for k in tiles:
                    after(act, n["dve"], KD + k + 1)
                    nc.scalar.activation(dst(k), src[:, k * T:(k + 1) * T], func, bias=col(b, k), scale=col(g, k))
                    if hi is not None:
                        drain()
                        nc.scalar.activation(hi[:, k * T:(k + 1) * T], dst(k), ACT.Copy).then_inc(n["hi"].sem, 1)
                    else:
                        drain()
                        fold(layers[0]["n_pre"], "mix_pre_0", k)

            def square(n, k, src):
                if k >= 2:
                    after(act, n["acc"], k - 1)
                dst = sq3[k % 2][:, :]
                nc.scalar.activation(dst if src.shape == dst.shape else split2(dst), src, ACT.Square).then_inc(n["sq"].sem, 1)

            def root(n, nk, b):
                after(act, n["pe"], 1)
                nc.scalar.activation(split2(std[:, :]), wide(b), ACT.Sqrt, bias=col("eps6", 0),
                                     scale=1.0 / (nk * P)).then_inc(n["std"].sem, 1)

            def fold(n, g, k):
                t = hres[:, k * L:(k + 1) * L]
                nc.scalar.activation(ahi[:, k * L:(k + 1) * L], t, ACT.Copy, scale=col(g, k)).then_inc(n["hi"].sem, 1)
                square(n, k, t)

            for u in range(2):
                split_first(u)
            act.wait_ge(params_in, 48)
            ln_squares(n_in, x_in)
            ln_std(n_in)
            ln_out(n_in, x_in, "ln_in_g", "ln_in_b", ACT.Identity, lambda k: x_in[:, k * T:(k + 1) * T], ahi)

            stage = PLAN["dt"]
            split_next(stage, 0, 0)
            nc.scalar.activation(dtt[0][:, :], bank(0, parts=32), ACT.Identity, bias=heads[:, 0:1]
                                 ).then_inc(psum_free[0], 1)
            drain()
            nc.scalar.activation(dtt[1][:, :], dtt[0][:, :], ACT.Abs)
            nc.scalar.activation(heads[:, 2:3], heads[:, 1:2], ACT.Exp)
            drain()
            nc.scalar.activation(dtt[2][:, :], dtt[1][:, :], ACT.Exp, scale=-1.0).then_inc(dt_exp, 1)

            stage = PLAN["xbc"]

            def xbc_unit(i, s, slot):
                for m in range(2):
                    k = 4 * i + (2 * s + m)
                    nc.scalar.activation(cut(xbc, 2048 * i + (2 * s + m) * T, T), bank(2 * slot + m), ACT.Identity,
                                         bias=col("ssm_b", k), scale=col("ssm_w", 4 * k + 3)).then_inc(conv4_acc, 1)
                for m in range(2):
                    if m == 0:
                        hold(act, conv4_tap, 2 * i + (s + 1), "act")
                    else:
                        hold(act, psum_free[slot], stage.used(i, s) + 1, "act")
                    tile = cut(xbc, 2048 * i + (2 * s + m) * T, T)
                    nc.scalar.activation(tile, tile, ACT.Silu).then_inc(conv4_out, 1)

            evacuate(stage, xbc_unit)

            act.wait_ge(dt_ready, 2)
            act.dma_start(acs_d[0:32, :], dtt[6][:, :]).then_inc(scratch_in, 16)
            act.dma_start(acs_d[32:34, :], dtt[6][0:2, :]).then_inc(scratch_in, 16)
            act.wait_ge(dt_ps, 1)
            nc.scalar.activation(tok[:, :], bank(4, 256), ACT.Copy).then_inc(dt_tok, 1)
            act.wait_ge(end_in, 1)
            nc.scalar.activation(ends[:, 0:128], ends[:, 0:128], ACT.Exp)
            nc.scalar.activation(ends[:, 128:256], bank(5, 128), ACT.Exp)
            drain().then_inc(ends_ok, 1)
            act.wait_ge(scratch_in, 32)
            for s in range(2):
                act.dma_start(acs_b[s][:, :], acs_d[s, :].partition_broadcast(P)).then_inc(acs_in[s], 16)
            stage = PLAN["z_glu"]

            def x_copy(g, j):
                nc.scalar.activation(x_slot[j % 2][:, :], cut(xbc, g * (GP * T) + j * T, T), ACT.Copy).then_inc(x_ok, 1)

            def group_start(g):
                nc.scalar.activation(b_slot[:, :], cut(xbc, g * T + BT0 * T, T), ACT.Copy).then_inc(b_ok, 1)
                for j in range(2):
                    x_copy(g, j)

            group_start(0)
            with act.Fori(0, GROUPS) as g:
                def z_unit(u):
                    slot = stage.slot(0)
                    split_next(stage, 2 * g + u // 2, 0)
                    hold(act, yg_ok, g * GP, "act")
                    for m in range(2):
                        o = nc.scalar.activation(zs[u + m][:, :], bank(4 + 2 * slot + m), ACT.Silu)
                    o.then_inc(psum_free[slot], 1)
                    drain().then_inc(zs_ok, 1)

                def glu_unit(u):
                    slot = stage.slot(1)
                    split_next(stage, 2 * g + u // 2, 1)
                    hold(act, v_ok, 2 * g, "act")
                    nc.scalar.activation(sig[u // 2][:, 0:T], bank(4 + 2 * slot + 1), ACT.Sigmoid).then_inc(sig_ok, 1)

                def head(q):
                    s = q % 2
                    hold(act, acs_in[s], 16 * (GH // 2) * g + 16 * (q // 2 + 1), "act")
                    if q == 0:
                        hold(act, xt_ps, g * GP + GP, "act")
                    if q >= 2:
                        hold(act, y_mm, g * GH + (q - 1), "act")
                    for c in range(CHUNKS):
                        cs = slice(c * CHUNK, (c + 1) * CHUNK)
                        nc.scalar.activation(m_slot[s][:, cs], acs_b[s][:, cs], ACT.Relu,
                                             bias=tok[:, bass.ds(g * GH + (c * 32 + q), 1)], scale=-1.0)
                    drain()
                    nc.scalar.activation(m_slot[s][:, :], m_slot[s][:, :], ACT.Exp, scale=-1.0)
                    nc.scalar.activation(c_slot[s][:, :], acs_b[s][:, :], ACT.Exp)
                    drain().then_inc(exp_ok, 1)
                    act.dma_start(acs_b[s][:, :], acs_d[bass.ds(g * GH + (q + 2), 1), :].rearrange("a t -> (a t)")
                                  .partition_broadcast(P)).then_inc(acs_in[s], 16)

                hold(act, bt_ps, g + 1, "act")
                hold(act, st_ps, g, "act")
                nc.scalar.activation(bt_sb[:, 0:384], bank(2, 384), ACT.Copy).then_inc(bt_ok, 1)
                for j in (2, 3):
                    hold(act, xt_ps, g * GP + (j - 1), "act")
                    x_copy(g, j)
                z_unit(0)
                head(0)
                head(1)
                glu_unit(1)
                for q in range(2, 6):
                    head(q)
                z_unit(2)
                head(6)
                head(7)
                hold(act, cb_ps, g + 1, "act")
                hold(act, y_mm, g * GH + GH, "act")
                group_start(g + 1)
                glu_unit(3)
            for s in range(2):
                act.wait_ge(acs_in[s], 16 * (HEADS // 2 + 1))

            def y_squares(first, end):
                with act.Fori(first // 2, end // 2) as i:
                    for m in range(2):
                        hold(act, ysq_sum, 2 * i, "act")
                        nc.scalar.activation(ysq[m][:, :], cut(xbc, 2 * T * i + m * T, T), ACT.Square
                                             ).then_inc(ysq_ok, 1)

            def gate(stage, u, dst):
                split_next(stage, u // 2, u % 2)
                slot = stage.slot(u % 2)
                for m in range(2):
                    o = nc.scalar.activation(dst[:, (2 * u + m) * T:(2 * u + m + 1) * T], bank(2 * slot + m), ACT.Sigmoid)
                o.then_inc(psum_free[slot], 1)

            def y_high(tiles):
                for k in tiles:
                    act.wait_ge(y_normed, k + 1)
                    nc.scalar.activation(yn_hi[:, k * T:(k + 1) * T], xbc[:, k * T:(k + 1) * T], ACT.Copy
                                         ).then_inc(yhi_ok, 1)

            stage = PLAN["gate_b"]
            act.wait_ge(yg_ok, XT)
            y_squares(0, XT // 2)
            gate(stage, 0, gb)
            y_squares(XT // 2, XT)
            gate(stage, 1, gb)
            act.wait_ge(ss_ps, 1)
            for g in range(GROUPS):
                nc.scalar.activation(rst4[:, g * T:(g + 1) * T], bank(4 + g), ACT.Sqrt, bias=col("eps5", 0),
                                     scale=1.0 / (GP * P)).then_inc(ss_std, 1)
            def products(w, start=None):
                for n in range(w, w + POOL_TAPS):
                    if start is not None or n >= 2:
                        hold(act, prod_used, n - 1 if start is None else start + (n - 1), "act")
                    tap = n + 1 if start is None else start + (n + 1)
                    nc.scalar.activation(prod[n % 2][:, :], cut(vpad, tap + POOL_TILE * VW, T), ACT.Copy,
                                         scale=col("conv_w", tap + POOL_TILE * TAPS)).then_inc(prod_ok, 1)

            nc.scalar.activation(vout[:, POOL_TILE * T:(POOL_TILE + 1) * T], vpad[:, POOL_TILE * VW:POOL_TILE * VW + T],
                                 ACT.Identity, bias=col("conv_b", POOL_TILE), scale=col("conv_w", POOL_TILE * TAPS)
                                 ).then_inc(vout_first, 1)
            y_high(range(0, 4))
            gate(stage, 2, gb)
            products(0)
            y_high(range(4, 12))
            gate(stage, 3, gb)
            products(POOL_TAPS)
            y_high(range(12, XT))

            def ssm_out_unit(i, s, slot):
                hold(act, ring_used, 2 * i, "act")
                nc.scalar.activation(ring[s][:, :], bank(2 * slot), ACT.Copy).then_inc(psum_free[slot], 1)
                drain().then_inc(ring_ok, 1)
                products(POOL_TAPS * s, 2 * POOL_TAPS * i + 2 * POOL_TAPS)

            evacuate(PLAN["ssm_out"], ssm_out_unit)

            stage = PLAN["gate_a"]
            conv_out = (vout, "conv_ln_g", "conv_ln_b", ACT.Silu, lambda k: vout[:, k * T:(k + 1) * T], chi)
            gate(stage, 0, ga)
            gate(stage, 1, ga)
            ln_squares(n_conv, vout)
            gate(stage, 2, ga)
            ln_std(n_conv)
            ln_out(n_conv, *conv_out, range(0, 4))
            gate(stage, 3, ga)
            ln_out(n_conv, *conv_out, range(4, KD))

            def mix_unit(i, s, slot):
                for m in range(2):
                    hold(act, mix_ok, 4 * i + (2 * s + m + 1), "act")
                    c = 2048 * i + (2 * s + m) * T
                    nc.scalar.activation(cut(mixhi, c, T), cut(gb, c, T), ACT.Copy).then_inc(mixhi_ok, 1)

            evacuate(PLAN["conv_out"], mix_unit)
            evacuate(PLAN["w_o"], lambda i, s, slot: None)
            ln_squares(n_1, res1)
            ln_std(n_1)
            ln_out(n_1, res1, "ln1_g", "ln1_b", ACT.Identity, lambda k: res1[:, k * T:(k + 1) * T], ahi)

            stage_u = PLAN["ffn_up"]

            def up_unit(i, s, slot):
                for m in range(2):
                    k = 2 * i + (s + m * FT)
                    hold(act, flo_ok, 2 * i, "act")
                    nc.scalar.activation(fg[s][m][:, :], bank(2 * slot + m), ACT.Identity, bias=col("ffn_b", k),
                                         scale=col("ffn_w", 3 * k + 2)).then_inc(fa_ok, 1)
                hold(act, ft_ok, 2 * i + (s + 1), "act")
                nc.scalar.activation(fg[s][0][:, :], fg[s][0][:, :], ACT.Silu).then_inc(fs_ok, 1)
                hold(act, ff_ok, 2 * i + (s + 1), "act")
                nc.scalar.activation(cut(fhi, 2 * T * i + s * T, T), fg[s][1][:, :], ACT.Copy).then_inc(fhi_ok, 1)

            evacuate(stage_u, up_unit)
            stage_d = PLAN["ffn_down"]
            act.wait_ge(flo_ok, FT)
            evacuate(stage_d, lambda i, s, slot: None)
            act.dma_start(hres[:, :].rearrange("p (k t) -> p k t", k=KD)[:, :, 0:META], metaT).then_inc(meta_in, 16)
            act.wait_ge(meta_in, 16)
            hview = [hres[:, k * L + META:(k + 1) * L] for k in range(KD)]
            ln_squares(n_2, res2)
            ln_std(n_2)
            ln_out(n_2, res2, "ln2_g", "ln2_b", ACT.Identity, lambda k: hview[k], None)

            for l, y in enumerate(layers):
                if l:
                    for k in range(KD):
                        after(act, layers[l - 1]["n_mpost"]["dve"], k + 1)
                        fold(y["n_pre"], f"mix_pre_{l}", k)
                after(act, y["pad_ok"], 1)
                act.dma_start(const2[:, :], const2_d).then_inc(const2_in, 16)
                stage = PLAN[f"in_{l}"]
                near, far = stage.slot(1) * 4, stage.slot(0) * 4

                for u in range(3):
                    split_next(stage, u // 2, u % 2)
                    slot = stage.slot(u % 2)
                    for m in range(2):
                        j = 2 * u + m
                        dst = qraw[:, j * L:(j + 1) * L] if j < 5 else vch[:, WIN + LEAD:KPAD]
                        o = nc.scalar.activation(split2(dst), wide(slot * 4 + 2 * m), ACT.Copy)
                    o.then_inc(psum_free[slot], 1)
                    if u == 1:
                        root(y["n_pre"], KD, far + 2)
                split_next(stage, 1, 1)
                after(act, y["v_ps"], 1)
                nc.scalar.activation(vtok[:, P:KPAD], PS[:, (far + 2) * 512:(far + 2) * 512 + NB * P], ACT.Copy
                                     ).then_inc(y["v_ok"].sem, 1)

                def exps(n):
                    z = n % 2
                    after(act, y["neg_ok"], n + 1)
                    for j in range(4):
                        p = sc[z][:, j * 256:(j + 1) * 256]
                        nc.scalar.activation(p, p, ACT.Exp, bias=small[:, 8 * z + j:8 * z + j + 1],
                                             accum_out=small[:, 16 + 8 * z + j:17 + 8 * z + j])
                    nc.scalar.activation(small[:, 32 + 8 * z:36 + 8 * z], small[:, 32 + 8 * z:36 + 8 * z], ACT.Exp)
                    drain().then_inc(y["p_ok"].sem, 1)

                def turned_p(n):
                    after(act, y["pt_ps"], n + 1)
                    if n >= 2:
                        after(act, y["o_ps"], n - 1)
                    nc.scalar.activation(pT[n % 2][:, :], PS[:, (far + 2) * 512:(far + 4) * 512], ACT.Copy
                                         ).then_inc(y["pt_ok"].sem, 1)

                def token_rms(b):
                    after(act, y["o_ok"], 2 * b + 2)
                    nc.scalar.activation(nv[0][:, 0:512], y_tok[:, b * 512:(b + 1) * 512], ACT.Square,
                                         accum_out=small[:, 48 + b:49 + b])
                    drain()
                    nc.scalar.activation(small[:, 48 + b:49 + b], small[:, 48 + b:49 + b], ACT.Sqrt, bias=col("eps6", 0),
                                         scale=1.0 / 512).then_inc(y["astd_ok"].sem, 1)

                def turned_y(b):
                    after(act, y["yt_ps"], b + 1)
                    t0_, skip = max(b * WIN - LEAD, 0), LEAD if b == 0 else 0
                    for j in range(4):
                        o = nc.scalar.activation(ya[:, j * L + t0_:j * L + t0_ + WIN - skip],
                                                 bank(far + 3, WIN - skip, j * P + skip), ACT.Copy,
                                                 scale=col(f"attn_g_{l}", j))
                    o.then_inc(y["ya_ok"].sem, 1)

                def conv_square(j):
                    after(act, y["yc_ok"], j + 1)
                    square(y["n_conv"], j, yconv[:, j * L:(j + 1) * L])

                for n in range(STEPS):
                    if n:
                        turned_p(n - 1)
                    exps(n)
                    if n >= 2 and n % 2 == 0:
                        token_rms(n // 2 - 1)
                    if n >= 3 and n % 2:
                        turned_y((n - 3) // 2)
                    if n == STEPS - 2:
                        conv_square(0)
                        conv_square(1)
                    if n % 2:
                        split_next(stage, (4 + n // 2) // 2, n // 2 % 2)
                conv_square(2)
                turned_p(STEPS - 1)
                conv_square(3)
                token_rms(NB - 1)
                root(y["n_conv"], 4, near)
                turned_y(NB - 1)
                drain()
                for k in range(4):
                    nc.scalar.activation(ahi[:, k * L:(k + 1) * L], ya[:, k * L:(k + 1) * L], ACT.Copy
                                         ).then_inc(y["n_attn"]["hi"].sem, 1)
                for k in range(4):
                    after(act, y["n_conv"]["dve"], k + 1)
                    nc.scalar.activation(ahi[:, (4 + k) * L:(5 + k) * L], nv[k % 2][:, :], ACT.Copy
                                         ).then_inc(y["n_conv"]["hi"].sem, 1)

                stage = PLAN[f"out_{l}"]

                def out_unit(i, s, slot):
                    for m in range(2):
                        k = 2 * (2 * i + s) + m
                        square(y["n_post"], k, wide(slot * 4 + 2 * m))
                        o = nc.scalar.activation(split2(zres[:, k * L:(k + 1) * L]), wide(slot * 4 + 2 * m), ACT.Copy)
                    o.then_inc(psum_free[slot], 1)

                for u in range(stage.n):
                    split_next(stage, u // 2, u % 2)
                    out_unit(u // 2, u % 2, stage.slot(u % 2))
                root(y["n_post"], KD, 0)
                for k in range(KD):
                    after(act, y["n_post"]["dve"], k + 1)
                    fold(y["n_mpre"], f"mlp_pre_{l}", k)

                for h in range(2):
                    stage = PLAN[f"up{h}_{l}"]
                    rl_ok, f_ok, f2hi_ok, f2lo_ok = (y[f"{a}{h}"] for a in ("rl_ok", "f_ok", "f2hi_ok", "f2lo_ok"))

                    def relus(i, s, slot):
                        for m in range(2):
                            hold(act, f2lo_ok, 4 * i, "act")
                            nc.scalar.activation(split2(rl[2 * s + m][:, :]), wide(slot * 4 + 2 * m), ACT.Relu
                                                 ).then_inc(rl_ok.sem, 1)
                        drain().then_inc(psum_free[slot], 1)

                    def highs(i, s):
                        for m in range(2):
                            hold(act, f_ok, 4 * i + (2 * s + m + 1), "act")
                            nc.scalar.activation(cut(f2hi, 4 * L * i + (2 * s + m) * L, L), rl[2 * s + m][:, :], ACT.Copy
                                                 ).then_inc(f2hi_ok.sem, 1)

                    for s in range(2):
                        split_next(stage, 0, s)
                        relus(0, s, stage.slot(s))
                    if h == 0:
                        root(y["n_mpre"], KD, stage.slot(0) * 4 + 2)
                    for s in range(2):
                        highs(0, s)
                    with act.Fori(1, stage.n // 2) as i:
                        for s in range(2):
                            split_next(stage, i, s)
                            relus(i, s, stage.slot(s))
                            highs(i, s)
                    stage = PLAN[f"down{h}_{l}"]
                    if h == 0:
                        def copy_unit(i, s, slot):
                            nc.scalar.activation(split2(cut(zres, 2 * L * i + s * L, L)), wide(slot * 4), ACT.Copy
                                                 ).then_inc(psum_free[slot], 1)

                        evacuate(stage, copy_unit)
                        drain().then_inc(y["zc_ok"].sem, 1)
                    else:
                        for u in range(stage.n):
                            split_next(stage, u // 2, u % 2)
                            after(act, y["dn_ok1"], u + 1)
                            square(y["n_mpost"], u, zres[:, u * L:(u + 1) * L])
                root(y["n_mpost"], KD, 0)

        @block.vector
        def _(dve):
            drain = nc.vector.drain
            v = nc.vector

            def tap(acc, ps, w, sh, n=T):
                return v.scalar_tensor_tensor(acc[:, sh:n], ps[:, 0:n - sh], w, acc[:, sh:n], ALU.mult, ALU.add)

            def layer_norm(n, src, hi, lo, each=None):
                after(dve, n["pe"], 1)
                for k in range(KD):
                    t = src[:, k * T:(k + 1) * T]
                    v.scalar_tensor_tensor(t, bank(4), -1.0 / D, t, ALU.mult, ALU.add).then_inc(n["dve"].sem, 1)
                after(dve, n["act"], KD + 1)
                v.reciprocal(rstd[:, 0:T], std[:, 0:T])
                drain()

                def low(k):
                    after(dve, n["hi"], k + 1)
                    c = slice(k * T, (k + 1) * T)
                    v.tensor_tensor(lo[:, c], src[:, c], hi[:, c].bitcast(F32), ALU.subtract).then_inc(n["lo"].sem, 1)

                for k in range(KD):
                    t = src[:, k * T:(k + 1) * T]
                    v.tensor_tensor(t, t, rstd[:, 0:T], ALU.mult).then_inc(n["dve"].sem, 1)
                    if each is not None:
                        each(k)
                    if hi is not None and k >= 2:
                        low(k - 2)
                if hi is not None:
                    low(KD - 2)
                    low(KD - 1)

            def add_up(tile, done):
                drain()
                v.tensor_tensor(acc1[:, :], acc1[:, :], tile, ALU.add).then_inc(done, 1)

            def lows(n, k, src, first):
                after(dve, n["hi"], k + 1)
                c = slice((first + k) * L, (first + k + 1) * L)
                v.tensor_tensor(alo[:, c], src, ahi[:, c].bitcast(F32), ALU.subtract).then_inc(n["lo"].sem, 1)

            def add_square(n, k):
                after(dve, n["sq"], k + 1)
                drain()
                if k == 0:
                    v.tensor_copy(acc2[:, :], sq3[0][:, :]).then_inc(n["acc"].sem, 1)
                else:
                    v.tensor_tensor(acc2[:, :], acc2[:, :], sq3[k % 2][:, :], ALU.add).then_inc(n["acc"].sem, 1)

            def fold(n, g, k):
                after(dve, n["hi"], k + 1)
                c = slice(k * L, (k + 1) * L)
                v.scalar_tensor_tensor(alo[:, c], hres[:, c], col(g, k), ahi[:, c].bitcast(F32), ALU.mult, ALU.subtract
                                       ).then_inc(n["lo"].sem, 1)
                add_square(n, k)

            def row_scale(n):
                after(dve, n["std"], 1)
                v.reciprocal(rstd[:, :], std[:, :])
                drain()

            def residual(n, g, each):
                row_scale(n)
                for k in range(KD):
                    t, h = zres[:, k * L:(k + 1) * L], hres[:, k * L:(k + 1) * L]
                    v.scalar_tensor_tensor(t, t, col(g, k), rstd[:, :], ALU.mult, ALU.mult)
                    drain()
                    v.tensor_tensor(h, h, t, ALU.add).then_inc(n["dve"].sem, 1)
                    each(k)

            def folding(n, g):
                def each(k):
                    if k:
                        fold(n, g, k - 1)
                    if k == KD - 1:
                        fold(n, g, k)
                return each

            dve.wait_ge(params_in, 48)
            v.memset(acc1[:, :], 0.0)
            dve.wait_ge(x_in_s, 16)
            for k in range(KD):
                add_up(x_in[:, k * T:(k + 1) * T], xin_ok)
            layer_norm(n_in, x_in, ahi, alo)

            dve.wait_ge(dt_exp, 1)
            x_, e_, r_, s_, s2, q_, acs, dt_ = dtt[0], dtt[2], dtt[3], dtt[4], dtt[1], dtt[7], dtt[6], dtt[5]
            v.tensor_scalar(r_[:, :], e_[:, :], 2.0, None, ALU.add)
            drain()
            v.reciprocal(s_[:, :], r_[:, :])
            drain()
            v.tensor_tensor(s_[:, :], s_[:, :], e_[:, :], ALU.mult)
            drain()
            v.tensor_tensor(s2[:, :], s_[:, :], s_[:, :], ALU.mult)
            drain()
            v.tensor_scalar(q_[:, :], s2[:, :], 1.0 / 15, None, ALU.mult)
            for d in (13, 11, 9, 7, 5, 3):
                drain()
                v.scalar_tensor_tensor(q_[:, :], q_[:, :], 1.0 / d, s2[:, :], ALU.add, ALU.mult)
            drain()
            v.scalar_tensor_tensor(q_[:, :], q_[:, :], 1.0, s_[:, :], ALU.add, ALU.mult)
            v.tensor_scalar(x_[:, :], x_[:, :], 0.0, None, ALU.max)
            drain()
            v.scalar_tensor_tensor(dt_[:, :], q_[:, :], 2.0, x_[:, :], ALU.mult, ALU.add).then_inc(dt_ready, 1)
            drain()
            v.tensor_scalar(r_[:, :], dt_[:, :], heads[:, 2:3], -1.0, ALU.mult, ALU.mult)
            drain()
            for c in range(CHUNKS):
                cs = slice(c * CHUNK, (c + 1) * CHUNK)
                o = v.tensor_tensor_scan(acs[:, cs], const1[0:32, 128:256], r_[:, cs], 0.0, ALU.mult, ALU.add)
            o.then_inc(dt_ready, 1)

            stage = PLAN["xbc"]

            def xbc_unit(i, s):
                slot = stage.slot(s)
                for m in range(2):
                    k = 4 * i + (2 * s + m)
                    hold(dve, conv4_acc, 4 * i + (2 * s + m + 1), "dve")
                    c = 2048 * i + (2 * s + m) * T
                    for w in (2, 1, 0):
                        sh = 3 - w
                        o = v.scalar_tensor_tensor(cut(xbc, c + sh, T - sh), bank(2 * slot + m, T - sh),
                                                   col("ssm_w", 4 * k + w), cut(xbc, c + sh, T - sh),
                                                   ALU.mult, ALU.add)
                        if w:
                            drain()
                    o.then_inc(conv4_tap if m == 0 else psum_free[slot], 1)

            unit_loop(dve, stage, xbc_unit)

            dve.wait_ge(end_ps, 1)
            v.scalar_tensor_tensor(ends[:, 0:128], tok[:, 0:128], -1.0, bank(5, 128), ALU.mult, ALU.add
                                   ).then_inc(end_in, 1)
            dve.wait_ge(ends_ok, 1)
            dve.wait_ge(conv4_out, XBCT)
            dve.wait_ge(scratch_in, 32)
            v3 = vpad[:, :].rearrange("p (k t) -> p k t", k=KD)
            v.memset(v3[:, :, 0:TAPS - 1], 0.0)
            stage = PLAN["z_glu"]

            odd = [u for u in range(1, KD, 2) if u != POOL_TILE]

            def long_taps(tiles, a, b, start=None):
                for w in range(a, b) if start is None else [start + k for k in range(a, b)]:
                    drain()
                    for u in tiles:
                        src, acc = cut(vpad, u * VW + w, T), cut(vout, u * T, T)
                        wc = col("conv_w", u * TAPS + w)
                        if isinstance(w, int) and w == 0:
                            v.tensor_scalar(acc, src, wc, col("conv_b", u), ALU.mult, ALU.add)
                        else:
                            v.scalar_tensor_tensor(acc, src, wc, acc, ALU.mult, ALU.add)

            with dve.Fori(0, GROUPS) as g:
                xdt3 = xdt[:, :].rearrange("p (c n) -> p c n", c=CHUNKS)
                for j in range(GP):
                    hold(dve, xt_ps, g * GP + (j + 1), "dve")
                    for hh in range(2):
                        o = v.tensor_tensor(
                            xdt3[:, :, j * P + hh * 64:j * P + (hh + 1) * 64],
                            bank(j % 2).rearrange("p (c n) -> p c n", c=CHUNKS)[:, :, hh * 64:(hh + 1) * 64],
                            tok[:, 128:256].rearrange("p (c h) -> p c h", c=CHUNKS)[:, :, bass.ds(g * GH + (2 * j + hh), 1)]
                            .to_broadcast([P, CHUNKS, HEAD_P]), ALU.mult)
                    o.then_inc(xdt_ok, 1)
                drain()
                for c in range(CHUNKS - 1):
                    o = v.tensor_tensor(xds[:, c * T:(c + 1) * T].rearrange("p (h n) -> p h n", h=GH),
                                        xdt[:, c * T:(c + 1) * T].rearrange("p (h n) -> p h n", h=GH),
                                        ends[:, bass.ds(g * GH + c * 32, GH)].unsqueeze(2).to_broadcast([P, GH, HEAD_P]),
                                        ALU.mult)
                o.then_inc(xds_ok, 1)
                hold(dve, cb_ps, g + 1, "dve")
                v.tensor_tensor(cbm[:, :].rearrange("p (c t) -> p c t", c=CHUNKS),
                                bank(3).rearrange("p (c t) -> p c t", c=CHUNKS),
                                causal.unsqueeze(1).to_broadcast([P, CHUNKS, P]), ALU.mult).then_inc(cbm_ok, 1)
                hold(dve, st_ps, g + 1, "dve")
                v.tensor_copy(st[:, 0:T], bank(0))
                for c in range(1, CHUNKS - 1):
                    drain()
                    v.tensor_tensor(st[:, c * T:(c + 1) * T].rearrange("p (h n) -> p h n", h=GH),
                                    st[:, (c - 1) * T:c * T].rearrange("p (h n) -> p h n", h=GH),
                                    ends[:, bass.ds(g * GH + (128 + c * 32), GH)].unsqueeze(2)
                                    .to_broadcast([P, GH, HEAD_P]), ALU.mult)
                    drain()
                    o = v.tensor_tensor(st[:, c * T:(c + 1) * T], st[:, c * T:(c + 1) * T], bank(c), ALU.add)
                o.then_inc(st_ok, 1)

                def y_out(j):
                    hold(dve, y_mm, g * GH + 2 * (j + 1), "dve")
                    t = cut(xbc, g * (GP * T) + j * T, T)
                    v.scalar_tensor_tensor(t, t, col("ssm_d", g * GP + j), bank(j % 2), ALU.mult, ALU.add
                                           ).then_inc(y_ok, 1)

                def glu(h):
                    slot = stage.slot(1)
                    hold(dve, sig_ok, 2 * g + (h + 1), "dve")
                    v.tensor_tensor(cut(vpad, 2 * VW * g + (h * VW + TAPS - 1), T), bank(4 + 2 * slot), sig[h][:, 0:T],
                                    ALU.mult).then_inc(psum_free[slot], 1)
                    drain().then_inc(v_ok, 1)

                for q in range(GH):
                    s = q % 2
                    hold(dve, exp_ok, g * GH + (q + 1), "dve")
                    v.tensor_tensor(c_slot[s][:, :], c_slot[s][:, :], cut(xbc, g * T + CT0 * T, T), ALU.mult)
                    v.tensor_tensor(m_slot[s][:, :], m_slot[s][:, :], cbm[:, :], ALU.mult).then_inc(mc_ok, 1)
                    if q % 2:
                        if q == 1:
                            glu(0)
                        else:
                            y_out(q // 2 - 1)
                        long_taps([2 * g], q // 2 * TAPS // GP, (q // 2 + 1) * TAPS // GP)
                y_out(GP - 1)
                glu(1)

            for s in range(2):
                dve.wait_ge(acs_in[s], 16 * (HEADS // 2 + 1))

            with dve.Fori(0, GROUPS) as g:
                acc = cut(sumsq, T * g, T)
                for j in range(GP):
                    hold(dve, ysq_ok, GP * g + (j + 1), "dve")
                    if j == 0:
                        v.tensor_copy(acc, ysq[0][:, :]).then_inc(ysq_sum, 1)
                    else:
                        drain()
                        v.tensor_tensor(acc, acc, ysq[j % 2][:, :], ALU.add).then_inc(ysq_sum, 1)

            long_taps(odd, 0, TAPS_GATE)

            for g in range(GROUPS):
                dve.wait_ge(ss_std, g + 1)
                v.reciprocal(rst4[:, g * T:(g + 1) * T], rst4[:, g * T:(g + 1) * T])
            drain()

            def y_low(k):
                dve.wait_ge(yhi_ok, k + 1)
                c = slice(k * T, (k + 1) * T)
                v.tensor_tensor(yn_lo[:, c], xbc[:, c], yn_hi[:, c].bitcast(F32), ALU.subtract).then_inc(ylo_ok, 1)

            for k in range(XT):
                c = slice(k * T, (k + 1) * T)
                v.scalar_tensor_tensor(xbc[:, c], xbc[:, c], col("ssm_norm", k), rst4[:, k // GP * T:(k // GP + 1) * T],
                                       ALU.mult, ALU.mult).then_inc(y_normed, 1)
                if k >= 2:
                    y_low(k - 2)
            y_low(XT - 2)
            y_low(XT - 1)

            v.memset(acc1[:, :], 0.0)
            for u in range(0, KD, 2):
                add_up(vout[:, u * T:(u + 1) * T], vout_ok)
            n = (TAPS - TAPS_GATE) // 4
            assert 4 * n + TAPS_GATE == TAPS
            with dve.Fori(0, KD // 2) as i:
                long_taps(odd, 0, n, n * i + TAPS_GATE)
                for s in range(2):
                    hold(dve, ring_ok, 2 * i + (s + 1), "dve")
                    t = cut(gb, 2 * T * i + s * T, T)
                    v.tensor_tensor(t, t, ring[s][:, :], ALU.mult).then_inc(ring_used, 1)
            drain()
            for u in odd:
                add_up(vout[:, u * T:(u + 1) * T], vout_ok)
            dve.wait_ge(prod_used, TAPS - 1)
            add_up(vout[:, POOL_TILE * T:(POOL_TILE + 1) * T], vout_ok)
            layer_norm(n_conv, vout, chi, clo)

            stage_c = PLAN["conv_out"]

            def mix_unit(i, s):
                slot = stage_c.slot(s)
                g = stage_c.u0 + s + 1
                for m in range(2):
                    c = 2048 * i + (2 * s + m) * T
                    if m == 0:
                        hold(dve, tile0_done, 2 * i + (stage_c.z0 + s + 1), "dve")
                    else:
                        hold(dve, unit_done, 2 * i + g, "dve")
                    o = v.tensor_tensor(cut(ga, c, T), cut(ga, c, T), bank(2 * slot + m), ALU.mult)
                    if m == 1:
                        o.then_inc(psum_free[slot], 1)
                    drain()
                    v.tensor_tensor(cut(gb, c, T), cut(gb, c, T), cut(ga, c, T), ALU.add).then_inc(mix_ok, 1)
                for m in range(2):
                    c = 2048 * i + (2 * s + m) * T
                    hold(dve, mixhi_ok, 4 * i + (2 * s + m + 1), "dve")
                    v.tensor_tensor(cut(mixlo, c, T), cut(gb, c, T), cut(mixhi, c, T).bitcast(F32), ALU.subtract
                                    ).then_inc(mixlo_ok, 1)

            unit_loop(dve, stage_c, mix_unit)

            stage_w = PLAN["w_o"]

            def w_o_unit(i, s):
                slot = stage_w.slot(s)
                for m in range(2):
                    c = 2048 * i + (2 * s + m) * T
                    if m == 0:
                        hold(dve, tile0_done, 2 * i + (stage_w.z0 + s + 1), "dve")
                    else:
                        hold(dve, unit_done, 2 * i + (stage_w.u0 + s + 1), "dve")
                    o = v.scalar_tensor_tensor(cut(res1, c, T), cut(ahi, c, T).bitcast(F32), ALPHA,
                                               bank(2 * slot + m), ALU.mult, ALU.add)
                    if m == 1:
                        o.then_inc(psum_free[slot], 1)
                    drain()
                    v.scalar_tensor_tensor(cut(res1, c, T), cut(alo, c, T).bitcast(F32), ALPHA, cut(res1, c, T),
                                           ALU.mult, ALU.add)
                    add_up(cut(res1, c, T), r1_ok)

            v.memset(acc1[:, :], 0.0)
            unit_loop(dve, stage_w, w_o_unit)
            layer_norm(n_1, res1, ahi, alo)

            stage_u = PLAN["ffn_up"]

            def up_unit(i, s):
                slot = stage_u.slot(s)
                for m in range(2):
                    k = 2 * i + (s + m * FT)
                    hold(dve, fa_ok, 4 * i + (2 * s + m + 1), "dve")
                    tap(fg[s][m], bank(2 * slot + m), col("ffn_w", 3 * k + 1), 1)
                    drain()
                    tap(fg[s][m], bank(2 * slot + m), col("ffn_w", 3 * k), 2).then_inc(
                        ft_ok if m == 0 else psum_free[slot], 1)
                drain()
                hold(dve, fs_ok, 2 * i + (s + 1), "dve")
                v.tensor_tensor(fg[s][1][:, :], fg[s][1][:, :], fg[s][0][:, :], ALU.mult).then_inc(ff_ok, 1)
                hold(dve, fhi_ok, 2 * i + (s + 1), "dve")
                c = 2 * T * i + s * T
                v.tensor_tensor(cut(flo, c, T), fg[s][1][:, :], cut(fhi, c, T).bitcast(F32), ALU.subtract
                                ).then_inc(flo_ok, 1)

            unit_loop(dve, stage_u, up_unit)
            stage_d = PLAN["ffn_down"]
            v.memset(acc1[:, :], 0.0)
            with dve.Fori(0, KD // 2) as i:
                for t in range(2):
                    c = 2 * T * i + t * T
                    hold(dve, unit_done, 4 * i + (stage_d.u0 + 2 * t + 2), "dve")
                    v.scalar_tensor_tensor(cut(res2, c, T), cut(ahi, c, T).bitcast(F32), ALPHA, bank(2 * t),
                                           ALU.mult, ALU.add).then_inc(psum_free[0], 1)
                    drain().then_inc(psum_free[1], 1)
                    v.scalar_tensor_tensor(cut(res2, c, T), cut(alo, c, T).bitcast(F32), ALPHA, cut(res2, c, T),
                                           ALU.mult, ALU.add)
                    add_up(cut(res2, c, T), r2_ok)
            layer_norm(n_2, res2, None, None, folding(layers[0]["n_pre"], "mix_pre_0"))

            for l, y in enumerate(layers):
                v.memset(qpad[:, :].rearrange("p (j t) -> p j t", j=4)[:, :, 0:LEAD], 0.0)
                v.memset(kpad[:, 0:WIN + LEAD], 0.0)
                v.memset(vch[:, 0:WIN + LEAD], 0.0)
                v.memset(vtok[:, 0:P], 0.0)
                for s in range(2):
                    v.memset(upad[s][:, 0:2], 0.0)
                drain().then_inc(y["pad_ok"].sem, 1)
                stage = PLAN[f"in_{l}"]
                near, far = stage.slot(1) * 4, stage.slot(0) * 4
                w2 = f"conv2_w_{l}"
                row_scale(y["n_pre"])
                v.tensor_tensor(rstd_sq[:, :], rstd[:, :], rstd[:, :], ALU.mult)
                dve.wait_ge(const2_in, 16 * (l + 1))
                cos, sin = (const2[:, CONST2[a]:CONST2[a] + L] for a in ("cos", "sin"))
                for t in (cos, sin):
                    v.tensor_tensor(t, t, rstd[:, :], ALU.mult)

                def rope(j):
                    after(dve, y["swap_ps"], j + 1)
                    raw_t = qraw[:, j * L:(j + 1) * L]
                    dst = qpad[:, j * QPAD + LEAD:(j + 1) * QPAD] if j < 4 else kpad[:, WIN + LEAD:KPAD]
                    drain()
                    v.tensor_tensor(split2(rot[:, 0:L]), split2(sin), wide(far + 2 * (j % 2)), ALU.mult)
                    v.tensor_tensor(rot[:, L:2 * L], raw_t, cos, ALU.mult)
                    drain()
                    v.tensor_tensor(dst, rot[:, 0:L], rot[:, L:2 * L], ALU.add).then_inc(y["rope_ok"].sem, 1)

                def c_gate(j):
                    dve.wait_ge(tile0_done, stage.z0 + 4 + j)
                    drain()
                    v.tensor_tensor(split2(cgate[j % 2][:, :]), wide(near), split2(rstd_sq[:, :]), ALU.mult)

                def gated(j):
                    dve.wait_ge(unit_done, stage.u0 + 4 + j)
                    drain()
                    v.tensor_tensor(split2(upad[j % 2][:, 2:2 + L]), wide(near + 2), split2(cgate[j % 2][:, :]), ALU.mult
                                    ).then_inc(psum_free[stage.slot((3 + j) % 2)], 1)

                def conv(j):
                    acc, up_ = yconv[:, j * L:(j + 1) * L], upad[j % 2]
                    drain()
                    v.tensor_scalar(acc, up_[:, 0:L], col(w2, 3 * j), None, ALU.mult)
                    for w in (1, 2):
                        drain()
                        v.scalar_tensor_tensor(acc, up_[:, w:w + L], col(w2, 3 * j + w), acc, ALU.mult, ALU.add)
                    drain()
                    v.tensor_tensor(acc, acc, rstd[:, :], ALU.mult)

                def b_gate(j):
                    u, m = 7 + j // 2, j % 2
                    if m == 0:
                        dve.wait_ge(tile0_done, stage.z0 + u + 1)
                    else:
                        dve.wait_ge(unit_done, stage.u0 + u + 1)
                    acc = split2(yconv[:, j * L:(j + 1) * L])
                    drain()
                    v.tensor_tensor(acc, acc, wide(near + 2 * m), ALU.mult).then_inc(y["yc_ok"].sem, 1)
                    if m:
                        drain().then_inc(psum_free[stage.slot(u % 2)], 1)

                dve.wait_ge(psum_free[stage.slot(0)], stage.used(1, 0) + 1)
                vt = vch[:, WIN + LEAD:KPAD]
                v.tensor_tensor(vt, vt, rstd[:, :], ALU.mult).then_inc(y["vch_ok"].sem, 1)
                rope(0)
                rope(1)
                c_gate(0)
                rope(2)
                rope(3)
                gated(0)
                rope(4)
                conv(0)

                sinks = f"sinks_{l}"

                def softmax(n):
                    b, z = n // 2, n % 2
                    after(dve, y["sc_ps"], n + 1)
                    if n >= 2:
                        after(dve, y["pt_ps"], n - 1)
                    drain()
                    s3 = sc[z][:, :].rearrange("p (j k) -> p j k", j=4)
                    mask = const2[:, CONST2["mask"] + b * 256:CONST2["mask"] + (b + 1) * 256]
                    v.scalar_tensor_tensor(s3, PS[:, far * 512:(far + 2) * 512].rearrange("p (j k) -> p j k", j=4), 0.125,
                                           mask.unsqueeze(1).to_broadcast([P, 4, 256]), ALU.mult, ALU.add
                                           ).then_inc(y["sc_ok"].sem, 1)
                    drain()
                    m_, se = small[:, 8 * z:8 * z + 4], small[:, 32 + 8 * z:36 + 8 * z]
                    sink = cols[:, COLS[sinks][0] + 4 * z:COLS[sinks][0] + 4 * z + 4]
                    v.tensor_reduce(m_, s3, AX_X, ALU.max)
                    drain()
                    v.tensor_tensor(m_, m_, sink, ALU.max)
                    drain()
                    v.tensor_tensor(se, sink, m_, ALU.subtract)
                    v.tensor_scalar(m_, m_, -1.0, None, ALU.mult)
                    drain().then_inc(y["neg_ok"].sem, 1)

                def output(n):
                    b, z = n // 2, n % 2
                    den = small[:, 16 + 8 * z:20 + 8 * z]
                    after(dve, y["p_ok"], n + 1)
                    v.tensor_tensor(den, den, small[:, 32 + 8 * z:36 + 8 * z], ALU.add)
                    drain()
                    v.reciprocal(den, den)
                    after(dve, y["o_ps"], n + 1)
                    drain()
                    o3 = y_tok[:, b * 512:(b + 1) * 512].rearrange("p (j n) -> p j n", j=4)[:, :, 64 * z:64 * z + 64]
                    v.tensor_tensor(o3, bank(far + 2, 256).rearrange("p (j n) -> p j n", j=4),
                                    den.unsqueeze(2).to_broadcast([P, 4, 64]), ALU.mult).then_inc(y["o_ok"].sem, 1)

                def token_scale(b):
                    after(dve, y["astd_ok"], b + 1)
                    if b >= 2:
                        after(dve, y["yt_ps"], b - 1)
                    v.reciprocal(small[:, 56 + b:57 + b], small[:, 48 + b:49 + b])
                    drain()
                    v.tensor_scalar(diag[b % 2][:, :], ident, small[:, 56 + b:57 + b], None, ALU.mult
                                    ).then_inc(y["dg_ok"].sem, 1)

                for n in range(STEPS):
                    u, m = 4 + n // 2, n % 2
                    softmax(n)
                    if n:
                        output(n - 1)
                    if n and m == 0 and u <= 7:
                        conv(u - 4)
                    if n >= 3 and m:
                        token_scale((n - 3) // 2)
                    if u >= 7:
                        b_gate(2 * (u - 7) + m)
                    elif m == 0:
                        c_gate(u - 3)
                    else:
                        gated(u - 3)
                    if n == STEPS - 2:
                        add_square(y["n_conv"], 0)
                        add_square(y["n_conv"], 1)
                add_square(y["n_conv"], 2)
                add_square(y["n_conv"], 3)
                output(STEPS - 1)
                token_scale(NB - 1)
                row_scale(y["n_conv"])

                def conv_normed(k):
                    v.scalar_tensor_tensor(nv[k % 2][:, :], yconv[:, k * L:(k + 1) * L], col(f"conv_g_{l}", k), rstd[:, :],
                                           ALU.mult, ALU.mult).then_inc(y["n_conv"]["dve"].sem, 1)

                conv_normed(0)
                conv_normed(1)
                for k in range(4):
                    lows(y["n_attn"], k, ya[:, k * L:(k + 1) * L], 0)
                for k in range(4):
                    lows(y["n_conv"], k, nv[k % 2][:, :], 4)
                    if k < 2:
                        drain()
                        conv_normed(k + 2)

                for k in range(KD):
                    add_square(y["n_post"], k)
                residual(y["n_post"], f"mix_post_{l}", folding(y["n_mpre"], f"mlp_pre_{l}"))
                row_scale(y["n_mpre"])
                for h in range(2):
                    stage = PLAN[f"up{h}_{l}"]
                    rl_ok, f_ok, f2hi_ok, f2lo_ok = (y[f"{a}{h}"] for a in ("rl_ok", "f_ok", "f2hi_ok", "f2lo_ok"))

                    def up_body(i, s):
                        for m in range(2):
                            hold(dve, rl_ok, 4 * i + (2 * s + m + 1), "dve")
                            r = rl[2 * s + m]
                            v.tensor_tensor(r[:, :], r[:, :], rstd[:, :], ALU.mult)
                            drain()
                            v.tensor_tensor(r[:, :], r[:, :], r[:, :], ALU.mult).then_inc(f_ok.sem, 1)
                        for m in range(2):
                            c = 4 * L * i + (2 * s + m) * L
                            hold(dve, f2hi_ok, 4 * i + (2 * s + m + 1), "dve")
                            v.tensor_tensor(cut(f2lo, c, L), rl[2 * s + m][:, :], cut(f2hi, c, L).bitcast(F32),
                                            ALU.subtract).then_inc(f2lo_ok.sem, 1)

                    unit_loop(dve, stage, up_body)
                stage = PLAN[f"down1_{l}"]
                after(dve, y["zc_ok"], 1)
                for u in range(stage.n):
                    slot = stage.slot(u % 2)
                    dve.wait_ge(unit_done, stage.u0 + u + 1)
                    t = zres[:, u * L:(u + 1) * L]
                    v.tensor_tensor(split2(t), split2(t), wide(slot * 4), ALU.add).then_inc(psum_free[slot], 1)
                    drain().then_inc(y["dn_ok1"].sem, 1)
                    if u:
                        add_square(y["n_mpost"], u - 1)
                add_square(y["n_mpost"], KD - 1)
                if l + 1 < LAYERS:
                    residual(y["n_mpost"], f"mlp_post_{l}", folding(layers[l + 1]["n_pre"], f"mix_pre_{l + 1}"))
                else:
                    residual(y["n_mpost"], f"mlp_post_{l}", lambda k: None)


def _tiles(v):
    return np.asarray(v, np.float32).reshape(-1, P).T


def _blocks(w):
    k, n = w.shape
    return w.reshape(k // P, P, n // P, P).transpose(0, 2, 1, 3)


def _stream(i):
    s = np.zeros((UNITS, P, 16, P), np.float32)

    def put(stage, u, tiles):
        for n, b in enumerate(tiles):
            s[PLAN[stage].u0 + u, :, n, :] = b

    w_in = i["w_in"][0]
    o = np.cumsum([0, 2 * D, SSM, XBC, HEADS, D, D])
    glu, z, xbc = (_blocks(w_in[:, o[j]:o[j + 1]]) for j in range(3))
    gate_a, gate_b = (_blocks(w_in[:, o[j]:o[j + 1]]) for j in (4, 5))
    dt = np.zeros((D, P), np.float32)
    dt[:, 0:HEADS] = w_in[:, o[3]:o[4]]
    put("dt", 0, _blocks(dt)[:, 0])

    def pairs(stage, b, order=None):
        order = list(range(b.shape[1])) if order is None else order
        for u in range(len(order) // 2):
            put(stage, u, [b[k, m] for m in order[2 * u:2 * u + 2] for k in range(b.shape[0])])

    def singles(stage, b):
        for m in range(b.shape[1]):
            put(stage, m, [b[k, m] for k in range(b.shape[0])])

    pairs("xbc", xbc)
    for g in range(GROUPS):
        for h in range(2):
            j = 2 * g + h
            put("z_glu", 2 * j, [z[k, m] for m in (2 * j, 2 * j + 1) for k in range(KD)])
            put("z_glu", 2 * j + 1, [glu[k, m] for m in (j, KD + j) for k in range(KD)])
    pairs("gate_b", gate_b)
    singles("ssm_out", _blocks(i["w_ssm_out"][0]))
    pairs("gate_a", gate_a)
    pairs("conv_out", _blocks(i["w_conv_out"][0]))
    pairs("w_o", _blocks(i["w_o"][0]))
    pairs("ffn_up", _blocks(i["w_ffn_up"][0]), [t for j in range(FT) for t in (j, FT + j)])
    down = _blocks(i["w_ffn_down"][0])
    for m in range(KD):
        for h in range(2):
            put("ffn_down", 2 * m + h, [down[h * (FT // 2) + k, m] for k in range(FT // 2)])
    for l in range(LAYERS):
        w = i["w_in_2"][l]
        q = w[:, 0:512].reshape(D, 2, 4, 64).transpose(0, 2, 1, 3).reshape(D, 512)
        w = _blocks(np.concatenate([q, w[:, 512:]], axis=1))
        pairs(f"in_{l}", w, [0, 1, 2, 3, 4, 5] + [t for j in range(4) for t in (10 + j, 14 + j)] + [6, 7, 8, 9])
        w = i["w_out_2"][l]
        a = w[0:512].reshape(2, 4, 64, D).transpose(1, 0, 2, 3).reshape(512, D)
        pairs(f"out_{l}", _blocks(np.concatenate([a, w[512:]], axis=0)))
        up, down = _blocks(i["w_up_2"][l]), _blocks(i["w_down_2"][l])
        for h in range(2):
            pairs(f"up{h}_{l}", up[:, h * FFH:(h + 1) * FFH])
            singles(f"down{h}_{l}", down[h * FFH:(h + 1) * FFH])
    return s.reshape(UNITS, P, UNIT)


def _columns(i):
    def taps(w):
        k, c = w.shape
        return w.reshape(k, c // P, P).transpose(2, 1, 0).reshape(P, -1)

    c = {
        "ln_in_g": _tiles(i["ln_in_g"]), "ln_in_b": _tiles(i["ln_in_b"]), "conv_w": taps(i["conv_dw_w"][0]),
        "conv_b": _tiles(i["conv_dw_b"][0]), "conv_ln_g": _tiles(i["conv_ln_g"][0]),
        "conv_ln_b": _tiles(i["conv_ln_b"][0]), "ssm_w": taps(i["ssm_conv_w"][0]), "ssm_b": _tiles(i["ssm_conv_b"][0]),
        "ssm_d": _tiles(np.repeat(i["ssm_d"][0], HEAD_P)), "ssm_norm": _tiles(i["ssm_norm_w"][0]),
        "ln1_g": _tiles(i["ln1_g"][0]), "ln1_b": _tiles(i["ln1_b"][0]), "ffn_w": taps(i["ffn_dw_w"][0]),
        "ffn_b": _tiles(i["ffn_dw_b"][0]), "ln2_g": _tiles(i["ln2_g"][0]), "ln2_b": _tiles(i["ln2_b"][0]),
        "eps5": np.full((P, 1), 1e-5, np.float32), "eps6": np.full((P, 1), 1e-6, np.float32),
    }
    for l in range(LAYERS):
        c[f"mix_pre_{l}"] = _tiles(i["mix_pre_g_2"][l])
        c[f"conv2_w_{l}"] = taps(i["conv_w_2"][l])
        c[f"attn_g_{l}"] = _tiles(i["attn_out_g_2"][l].reshape(2, 4, 64).transpose(1, 0, 2).reshape(512))
        c[f"conv_g_{l}"] = _tiles(i["conv_out_g_2"][l])
        c[f"mix_post_{l}"] = _tiles(i["mix_post_g_2"][l])
        c[f"mlp_pre_{l}"] = _tiles(i["mlp_pre_g_2"][l])
        c[f"mlp_post_{l}"] = _tiles(i["mlp_post_g_2"][l])
        c[f"sinks_{l}"] = np.broadcast_to(i["sinks_2"][l].reshape(1, QH), (P, QH))
    return np.ascontiguousarray(np.concatenate([c[n] for n in COLS], axis=1))


def _constants():
    c1 = np.zeros((P, N1), np.float32)
    c1[:, 0:128] = np.eye(P)
    c1[:, 128:256] = 1.0
    s, t = np.arange(P)[:, None], np.arange(P)[None, :]
    c1[:, 256:384] = t >= s
    c1[P - 1, 384:512] = 1.0
    c2 = np.zeros((P, N2), np.float32)
    cos, sin = np.ones((P, L), np.float32), np.zeros((P, L), np.float32)
    half = ROT // 2
    inv = np.power(np.float32(THETA), -np.arange(0, ROT, 2, dtype=np.float32) / np.float32(ROT)).astype(np.float32)
    ang = (np.arange(L, dtype=np.float32)[:, None] * inv[None, :]).astype(np.float32)
    for h in range(2):
        for r in range(half):
            a, b = 64 * h + r, 64 * h + half + r
            c2[b, a] = -1.0
            c2[a, b] = 1.0
            cos[a] = cos[b] = np.cos(ang[:, r])
            sin[a] = sin[b] = np.sin(ang[:, r])
    c2[:, CONST2["cos"]:CONST2["cos"] + L] = cos
    c2[:, CONST2["sin"]:CONST2["sin"] + L] = sin
    kk = np.arange(2 * WIN)[None, :]
    for b in range(NB):
        key = b * WIN + kk
        ok = (kk <= s + WIN) & (kk > s) & (key >= WIN + LEAD)
        c2[:, CONST2["mask"] + b * 256:CONST2["mask"] + (b + 1) * 256] = np.where(ok, 0.0, NEG)
    return c1, c2


def kernel(**inputs):
    import concourse.bacc as _bacc
    from concourse.bass_utils import run_bass_kernel_spmd as _run

    i = {k: np.asarray(v) for k, v in inputs.items()}
    nc = _bacc.Bacc("TRN2", target_bir_lowering=False, num_devices=1, dynamic_dma_scratch_size=1024)
    c1, c2 = _constants()
    arrays = {
        "x_t": np.ascontiguousarray(i["x"][0].T.reshape(KD, P, T).transpose(1, 0, 2)),
        "meta_t": np.ascontiguousarray(i["meta_tokens_2"].T.reshape(KD, P, META).transpose(1, 0, 2)),
        "weights": _stream(i),
        "columns": _columns(i),
        "head_params": np.ascontiguousarray(np.stack([i["ssm_dt_bias"][0], i["ssm_a_log"][0]], axis=1)),
        "const1": c1,
        "const2": c2,
    }
    d = {n: nc.dram_tensor(n, a.shape, F32, kind="ExternalInput").ap() for n, a in arrays.items()}
    acs = nc.dram_tensor("acs_rows", (HEADS + 2, T), F32, kind="Internal").ap()
    out = nc.dram_tensor("out_t", (P, KD, T), F32, kind="ExternalOutput").ap()
    build(nc, d["x_t"].rearrange("p k t -> p (k t)"), d["meta_t"], d["weights"], d["columns"], d["head_params"],
          d["const1"], d["const2"], acs, out)
    r = _run(nc, [arrays], core_ids=[0])
    o = np.asarray(r.results[0]["out_t"])
    return np.ascontiguousarray(o.transpose(2, 1, 0).reshape(1, T, D))
```

```python
import math
from contextlib import ExitStack

import numpy as np
import concourse.bass as bass
from concourse import mybir

F32 = mybir.dt.float32
F32R = mybir.dt.float32r
ALU = mybir.AluOpType
ACT = mybir.ActivationFunctionType
AX_X = mybir.AxisListType.X

P = 128
D = 1024
KD = D // P
T = 512
SSM = 2 * D
HEADS, HEAD_P = SSM // 64, 64
GROUPS, STATE, CHUNK = 4, 128, 128
CHUNKS = T // CHUNK
GH = HEADS // GROUPS
GP = GH // 2
XBC = SSM + 2 * GROUPS * STATE
XT, BT0, CT0, XBCT = SSM // P, SSM // P, SSM // P + GROUPS, XBC // P
TAPS = 31
TAPS_AT = [0, 4, 4, 9, 10, 14, 15, 19, 20, 20]
TAPS_GATE = 3
POOL_TILE = KD - 1
POOL_TAPS = 3
POOL_TURNS = KD
POOL_ENDS = 1 + POOL_TURNS * POOL_TAPS
FFN = 2816
FT = FFN // P
ALPHA = 2.0 ** 0.25
LAYERS = 2
X_PARTS = 4
DT_AT = 6
META = 16
L = T + META
HALF = L // 2
WIN = 128
NB = 5
LEAD = WIN - META
QPAD = NB * WIN
KPAD = QPAD + WIN
QH = 8
FF = 4 * D
FFH = FF // P // 2
ROT, THETA = 16, 500000.0
NEG = -1.0e30
UNIT = 16 * P


class Stage:

    def __init__(self, name, u0, first_tiles, n, nm, nk):
        self.name, self.u0, self.z0, self.n, self.nm, self.nk = name, u0, first_tiles, n, nm, nk

    def slot(self, s):
        return (self.u0 + s) % 2

    def used(self, i, s):
        return (self.u0 + s) // 2 + i


def make_plan():
    plan, u, z = {}, 0, 0
    first = [("dt", 1, 1, KD), ("xbc", XBCT // 2, 2, KD), ("z_glu", 4 * GROUPS, 2, KD),
             ("gate_b", KD // 2, 2, KD), ("ssm_out", KD, 1, XT), ("gate_a", KD // 2, 2, KD),
             ("conv_out", KD // 2, 2, KD), ("w_o", KD // 2, 2, KD), ("ffn_up", FT, 2, KD),
             ("ffn_down", 2 * KD, 1, FT // 2)]
    layer = [("in", 9, 2, KD), ("out", KD // 2, 2, KD), ("up0", FFH // 2, 2, KD), ("down0", KD, 1, FFH),
             ("up1", FFH // 2, 2, KD), ("down1", KD, 1, FFH)]
    for name, n, nm, nk in first + [(f"{a}_{l}", n, nm, nk) for l in range(LAYERS) for a, n, nm, nk in layer]:
        plan[name] = Stage(name, u, z, n, nm, nk)
        u += n
        z += n if nm == 2 else 0
    return plan, u


PLAN, UNITS = make_plan()

COLS = {}


def _place_cols():
    at = 0
    for name, n in [("ln_in_g", KD), ("ln_in_b", KD), ("conv_w", KD * TAPS), ("conv_b", KD), ("conv_ln_g", KD),
                    ("conv_ln_b", KD), ("ssm_w", XBCT * 4), ("ssm_b", XBCT), ("ssm_d", XT), ("ssm_norm", XT),
                    ("ln1_g", KD), ("ln1_b", KD), ("ffn_w", 2 * FT * 3), ("ffn_b", 2 * FT), ("ln2_g", KD),
                    ("ln2_b", KD)] + [(f"{a}_{l}", n) for l in range(LAYERS) for a, n in
                                      [("mix_pre", KD), ("conv2_w", 4 * 3), ("attn_g", 4), ("conv_g", 4),
                                       ("mix_post", KD), ("mlp_pre", KD), ("mlp_post", KD), ("sinks", QH)]] + [
                   ("eps5", 1), ("eps6", 1)]:
        COLS[name] = (at, n)
        at += n
    return at


NCOLS = _place_cols()
CONST1 = {"ident": 0, "ones": 128, "causal": 256, "last": 384}
N1 = 512
CONST2 = {"rope_p": 0, "cos": 128, "sin": 128 + L, "mask": 128 + 2 * L}
N2 = 128 + 2 * L + NB * 256


def build(nc, xT, metaT, wstream, cols_d, heads_d, const1_d, const2_d, acs_d, outT):
    ctx = ExitStack()
    with ctx:
        sems = {}

        def sem(name):
            sems[name] = ctx.enter_context(nc.semaphore(name))
            return sems[name]

        top = [1152]

        def fixed(name, n, dt=F32):
            at = top[0]
            top[0] += 4 * n
            return nc.alloc_sbuf_tensor_at(name, [P, n], dt, offset=at)

        const1 = fixed("const1", N1)
        cols = fixed("cols", NCOLS + (-NCOLS) % 8)
        raw = [fixed(f"raw{s}", UNIT) for s in range(2)]
        whi = [fixed(f"whi{s}", UNIT, F32R) for s in range(2)]
        wlo = [fixed(f"wlo{s}", UNIT, F32R) for s in range(2)]
        ahi = fixed("ahi", KD * L, F32R)
        alo = fixed("alo", KD * L, F32R)
        mu, std, rstd = fixed("mu", L), fixed("std", L), fixed("rstd", L)
        R = top[0]
        R_END = 228200 // 32 * 32

        def at(name, off, n, dt=F32, parts=P):
            assert R + off + 4 * n <= R_END, (name, R + off + 4 * n - R_END)
            return nc.alloc_sbuf_tensor_at(name, [parts, n], dt, offset=R + off)

        TB = 4 * T
        H0 = (R_END - R - 4 * KD * L) // 32 * 32
        x_in = at("x_in", 32 * TB, KD * T)
        xbc = at("xbc", 0, XBCT * T)
        ssd0 = 24 * TB
        xdt = at("xdt", ssd0, 4 * T)
        xds = at("xds", ssd0 + 4 * TB, 3 * T)
        st = at("st", ssd0 + 7 * TB, 3 * T)
        b_slot = at("b_slot", ssd0 + 10 * TB, T)
        bt_sb = at("bt_sb", ssd0 + 11 * TB, T)
        acs_b = [at(f"acs_b{s}", ssd0 + (12 + s) * TB, T) for s in range(2)]
        m_slot = [at(f"m_slot{s}", ssd0 + (14 + s) * TB, T) for s in range(2)]
        c_slot = [at(f"c_slot{s}", ssd0 + (16 + s) * TB, T) for s in range(2)]
        x_slot = c_slot
        tok = at("tok", ssd0 + 18 * TB, 256)
        ends = at("ends", ssd0 + 18 * TB + 1024, 256)
        zs = [at(f"zs{j}", ssd0 + (19 + j) * TB, T) for j in range(GP)]
        dtt = [at(f"dtt{s}", ssd0 + (23 + s) * TB, T, parts=32) for s in range(8)]
        heads = at("heads", ssd0 + 31 * TB, 8, parts=32)
        yn_lo = at("yn_lo", 0, XT * T, F32R)
        yn_hi = at("yn_hi", 16 * TB, XT * T, F32R)
        VW = T + TAPS - 1
        v0 = ssd0 + 23 * TB
        vpad = at("vpad", v0, KD * VW)
        vo0 = v0 + 4 * KD * VW + (-4 * KD * VW) % 64
        vout = at("vout", vo0, KD * T)
        t0 = ssd0 + 16 * TB
        rst4 = sumsq = at("sumsq", t0, 4 * T)
        ring = [at(f"ring{s}", t0 + s * TB, T) for s in range(2)]
        ysq = [at(f"ysq{s}", t0 + (4 + s) * TB, T) for s in range(2)]
        prod = ysq + [at("prod2", v0, T)]
        sq1 = ysq
        acc1 = at("acc1", t0 + 6 * TB, T)
        sig = [mu, std]
        cbm = at("cbm", vo0 + 8 * TB, T)
        gb = at("gb", ssd0 + 8 * TB, KD * T)
        ga = at("ga", 8 * TB, KD * T)
        chi = at("chi", 16 * TB, KD * T, F32R)
        clo = at("clo", 0, KD * T, F32R)
        mixhi = at("mixhi", 24 * TB, KD * T, F32R)
        mixlo = at("mixlo", v0, KD * T, F32R)
        res1 = at("res1", vo0, KD * T)
        fhi = at("fhi", 0, FT * T, F32R)
        flo = at("flo", FT * TB, FT * T, F32R)
        fg = [[at(f"fg{s}{m}", (2 * FT + 2 * s + m) * TB, T) for m in range(2)] for s in range(2)]
        res2 = at("res2", (2 * FT + 4) * TB, KD * T)
        assert (2 * FT + 4 + KD) * TB <= H0
        LB = 4 * L
        hres = at("hres", H0, KD * L)
        const2 = at("const2", 0, N2)
        q0 = 4 * N2 + (-4 * N2) % 64
        qpad = at("qpad", q0, 4 * QPAD)
        kpad = at("kpad", q0 + 16 * QPAD, KPAD)
        vch = at("vch", q0 + 16 * QPAD + 4 * KPAD, KPAD)
        vtok = at("vtok", q0 + 16 * QPAD + 8 * KPAD, KPAD)
        c0 = q0 + 16 * QPAD + 12 * KPAD
        qraw = at("qraw", c0, 5 * L)
        yconv = at("yconv", c0 + 5 * LB, 4 * L)
        UP = L + 8
        cgate = [at(f"cgate{s}", c0 + 9 * LB + s * LB, L) for s in range(2)]
        upad = [at(f"upad{s}", c0 + 11 * LB + 4 * s * UP, UP) for s in range(2)]
        rot = at("rot", c0 + 11 * LB + 8 * UP, 2 * L)
        a0 = c0 + 13 * LB + 8 * UP
        sc = [at(f"sc{z}", a0 + 8192 * z, 1024) for z in range(2)]
        pT = [at(f"pT{z}", a0 + 8192 * z + 4096, 1024) for z in range(2)]
        small = at("small", c0, 64)
        diag = [at(f"diag{s}", c0 + 256 + 512 * s, P) for s in range(2)]
        y_tok = at("y_tok", a0 + 16384, NB * 512)
        zres = at("zres", 0, KD * L)
        f2hi = at("f2hi", KD * LB, FFH * L, F32R)
        f2lo = at("f2lo", (KD + FFH) * LB, FFH * L, F32R)
        rl = [at(f"rl{s}", (KD + 2 * FFH + s) * LB, L) for s in range(4)]
        s0 = (KD + 2 * FFH + 4) * LB
        sq3 = [at(f"sq3{s}", s0 + s * LB, L) for s in range(2)]
        acc2 = at("acc2", s0 + 2 * LB, L)
        nv = [at(f"nv{s}", s0 + (3 + s) * LB, L) for s in range(2)]
        ya = at("ya", s0 + 5 * LB, 4 * L)
        rstd_sq = mu
        assert a0 + 16384 + 2048 * NB <= s0 and s0 + 9 * LB <= H0, (a0, s0, H0)

        PS = ctx.enter_context(nc.psum_tensor("PS", [P, 8 * 512], F32))

        def bank(b, n=512, off=0, parts=P):
            return PS[0:parts, b * 512 + off:b * 512 + off + n]

        def wide(b):
            return PS[:, b * 512:(b + 2) * 512].rearrange("p (a c) -> p a c", a=2)[:, :, 0:HALF]

        class Span:

            def __init__(self, meta):
                self.first, self.n, self.parts = (0, L, 2) if meta else (META, T, 1)
                self.width = self.n // self.parts

            def of(self, t, k):
                return t[:, k * L + self.first:(k + 1) * L]

            def fit(self, ap):
                return split2(ap) if self.parts == 2 else ap

            def psum(self, b):
                return wide(b) if self.parts == 2 else bank(b)

            def tile(self, slot, m):
                return self.psum((slot * 2 + m) * self.parts)

        every = Span(True)

        def span_of(l):
            return Span(l + 1 < LAYERS)

        def first_step(l):
            return 0 if l + 1 < LAYERS else 2

        def keys(b):
            return (1,) if b == 0 else (0, 1)

        def split2(ap):
            return ap.rearrange("p (a c) -> p a c", a=2)

        def col(name, k):
            a = COLS[name][0]
            if isinstance(k, int):
                return cols[:, a + k:a + k + 1]
            return cols[:, bass.ds(k + a, 1)]

        def cut(t, start, n):
            return t[:, start:start + n] if isinstance(start, int) else t[:, bass.ds(start, n)]

        ident, ones = const1[:, 0:128], const1[:, 128:256]
        causal, last_row = const1[:, 256:384], const1[:, 384:512]

        params_in, meta_in, const2_in = sem("params_in"), sem("meta_in"), sem("const2_in")
        x_in_s = [sem(f"x_loaded{j}") for j in range(X_PARTS)]
        raw_in = [sem(f"raw_in{s}") for s in range(2)]
        hi_ready, lo_ready = sem("whi_ready"), sem("wlo_ready")
        unit_done, tile0_done = sem("unit_done"), sem("tile0_done")
        psum_free = [sem(f"psum_free{s}") for s in range(2)]
        out_done = sem("out_done")
        turn = {e: sem(f"turn_{e}") for e in ("pe", "act", "dve", "pool", "sp")}

        class Counter:

            def __init__(self, s, base=0):
                self.sem, self.base = s, base

        def norm_sems(name, what="pe act dve hi lo"):
            return {a: sem(f"{name}_{a}") for a in what.split()}

        def after(eng, counter, value):
            eng.wait_ge(counter.sem, value + counter.base)

        n_in, n_conv, n_1, n_2 = ({a: Counter(s) for a, s in norm_sems(name).items()}
                                  for name in ("ln_in", "ln_conv", "ln1", "ln2"))
        dt_exp, dt_ready, dt_ps, dt_tok, end_ps, end_in, ends_ok = (
            sem(a) for a in ("dt_exp", "dt_ready", "dt_tok_ps", "dt_tok", "end_ps", "end_in", "ends_ok"))
        conv4_acc, conv4_tap, conv4_out = sem("conv4_acc"), sem("conv4_tap"), sem("conv4_out")
        scratch_in = sem("acs_stored")
        acs_in = [sem(f"acs_in{s}") for s in range(2)]
        (b_ok, bt_ps, bt_ok, cb_ps, x_ok, xt_ps, xdt_ok, xds_ok, st_ps, st_ok, cbm_ok, exp_ok, mc_ok, y_mm, y_ok) = (
            sem(a) for a in ("b_ok", "bt_ps", "bt_ok", "cb_ps", "x_ok", "xt_ps", "xdt_ok", "xds_ok", "st_ps",
                             "st_ok", "cbm_ok", "exp_ok", "mc_ok", "y_mm", "y_ok"))
        sig_ok, v_ok = sem("sig_ok"), sem("glu_used")
        zs_ok, yg_ok, ysq_ok, ysq_sum = sem("zs_ok"), sem("yg_ok"), sem("ysq_ok"), sem("ysq_sum")
        ss_ps, ss_std = sem("ss_ps"), sem("ss_std")
        y_normed, yhi_ok, ylo_ok = sem("y_normed"), sem("yhi_ok"), sem("ylo_ok")
        xin_ok, vout_ok = sem("xin_ok"), sem("vout_ok")
        prod_ok, prod_used, vout_first, ring_ok, ring_used = (sem(a) for a in (
            "tap_prod", "tap_used", "tap_first", "ring_ok", "ring_used"))
        mix_ok, mixhi_ok, mixlo_ok = sem("mix_ok"), sem("mixhi_ok"), sem("mixlo_ok")
        r1_ok, r2_ok = sem("r1_ok"), sem("r2_ok")
        fa_ok, ft_ok, fs_ok, ff_ok, fhi_ok, flo_ok = (sem(a) for a in ("ffn_acc", "ffn_tap0", "ffn_silu", "ffn_prod",
                                                                      "ffn_hi", "ffn_lo"))

        STEPS = 2 * NB
        per_layer = {
            "c_ok": 4, "yc_ok": 4, "swap_ps": 5, "rope_ok": 5, "vch_ok": 1, "v_ps": 1, "v_ok": 1, "sc_ps": STEPS,
            "sc_ok": STEPS, "neg_ok": STEPS, "p_ok": STEPS, "pt_ps": STEPS, "pt_ok": STEPS, "o_ps": STEPS,
            "o_ok": STEPS, "astd_ok": NB, "dg_ok": NB, "yt_ps": NB, "ya_ok": NB, "zc_ok": 1, "pad_ok": 1, "dn_ok1": KD,
            "rl_ok": 2 * FFH, "f_ok": 2 * FFH, "f2hi_ok": 2 * FFH, "f2lo_ok": 2 * FFH}
        norms = {"pre": (KD, "sq acc pe std hi lo"), "conv": (4, "sq acc pe std dve hi lo"), "attn": (4, "hi lo"),
                 "post": (KD, "sq acc pe std dve"), "mpre": (KD, "sq acc pe std hi lo"), "mpost": (KD, "sq acc pe std dve")}
        layer_sems = {a: sem(a) for a in per_layer}
        norm_sem = {a: norm_sems(a, what) for a, (_, what) in norms.items()}

        def layer_counters(l):
            y = {a: Counter(layer_sems[a], l * n) for a, n in per_layer.items()}
            for a in ("rl_ok", "f_ok", "f2hi_ok", "f2lo_ok"):
                for h in range(2):
                    y[f"{a}{h}"] = Counter(layer_sems[a], (2 * l + h) * FFH)
            for a, (nk, _) in norms.items():
                y["n_" + a] = {e: Counter(s, l * (1 if e in ("pe", "std") else nk)) for e, s in norm_sem[a].items()}
            return y

        layers = [layer_counters(l) for l in range(LAYERS)]

        def centred(k, pe_odd):
            return k + 1 + (k // 2 if pe_odd else max(k - 1, 0))

        def summed(pe_odd):
            return KD + (KD // 2 if pe_odd else KD)

        block = ctx.enter_context(nc.Block())

        def hold(eng, s, value, who):
            if isinstance(s, Counter):
                s, value = s.sem, value + s.base
            if isinstance(value, int):
                assert value >= 0
                if value > 0:
                    eng.wait_ge(s, value)
            else:
                eng.wait_ge(s, value)
                eng.sem_inc(turn[who])

        def unit_loop(eng, stage, body, first=0, end=None):
            end = stage.n if end is None else end
            pairs = end // 2
            if pairs > first // 2:
                with eng.Fori(first // 2, pairs) as i:
                    for s in range(2):
                        body(i, s)
            for u in range(2 * pairs, end):
                body(u // 2, u % 2)

        @block.sync
        def _(sp):
            for j in range(X_PARTS):
                c = slice(j * KD // X_PARTS * T, (j + 1) * KD // X_PARTS * T)
                sp.dma_start(x_in[:, c], xT[:, c]).then_inc(x_in_s[j], 16)
            sp.dma_start(const1[:, :], const1_d).then_inc(params_in, 16)
            sp.dma_start(cols[:, 0:NCOLS], cols_d).then_inc(params_in, 16)
            sp.dma_start(heads[:, 0:2], heads_d).then_inc(params_in, 16)
            for s in range(2):
                sp.dma_start(raw[s][:, :], wstream[s]).then_inc(raw_in[s], 16)
            with sp.Fori(1, UNITS // 2) as i:
                for s in range(2):
                    sp.wait_ge(lo_ready, 2 * i + s - 1)
                    sp.dma_start(raw[s][:, :], wstream[bass.ds(2 * i + s, 1)].rearrange("a p n -> (a p) n")
                                 ).then_inc(raw_in[s], 16)
            for u in range(UNITS // 2 * 2, UNITS):
                sp.wait_ge(lo_ready, u - 1)
                sp.dma_start(raw[u % 2][:, :], wstream[u]).then_inc(raw_in[u % 2], 16)
            for k in range(KD):
                after(sp, layers[-1]["n_mpost"]["dve"], k + 1)
                sp.dma_start(outT[:, k, :], hres[:, k * L + META:(k + 1) * L]).then_inc(out_done, 16)
            sp.wait_ge(out_done, 16 * KD)

        @block.gpsimd
        def _(pool):
            def low(s, value):
                hold(pool, hi_ready, value, "pool")
                nc.gpsimd.tensor_tensor(wlo[s][:, :], raw[s][:, :], whi[s][:, :].bitcast(F32),
                                        ALU.subtract).then_inc(lo_ready, 1)

            def lows(first, end):
                if first % 2:
                    low(1, first + 1)
                if (first + 1) // 2 < end // 2:
                    with pool.Fori((first + 1) // 2, end // 2) as i:
                        for s in range(2):
                            low(s, 2 * i + s + 1)
                if end % 2:
                    low(0, end)

            stage = PLAN["z_glu"]
            n = stage.n // GROUPS
            lows(0, stage.u0 + 2)
            with pool.Fori(0, GROUPS) as g:
                def z_low(u):
                    low(stage.slot(u % 2), g * n + (stage.u0 + u + 1))

                def gated(j):
                    hold(pool, y_ok, g * GP + (j + 1), "pool")
                    hold(pool, zs_ok, 2 * g + (j // 2 + 1), "pool")
                    t = cut(xbc, g * (GP * T) + j * T, T)
                    nc.gpsimd.tensor_tensor(t, t, zs[j][:, :], ALU.mult).then_inc(yg_ok, 1)

                z_low(2)
                z_low(3)
                gated(0)
                gated(1)
                z_low(4)
                gated(2)
                gated(3)
                z_low(5)
            first = PLAN["ssm_out"].u0
            lows(stage.u0 + stage.n + 2, first + 1)
            pool.wait_ge(vout_first, 1)
            with pool.Fori(0, POOL_TURNS // 2) as i:
                for s in range(2):
                    low((first + s + 1) % 2, 2 * i + (first + s + 2))
                    for w in range(POOL_TAPS):
                        acc = vout[:, POOL_TILE * T:(POOL_TILE + 1) * T]
                        hold(pool, prod_ok, 2 * POOL_TAPS * i + (POOL_TAPS * s + w + 1), "pool")
                        nc.gpsimd.drain()
                        nc.gpsimd.tensor_tensor(acc, acc, prod[w][:, :], ALU.add).then_inc(prod_used, 1)

            def add_squares(n, span):
                a = acc2[:, 0:span.n]
                for k in range(1, KD):
                    after(pool, n["sq"], k + 1)
                    nc.gpsimd.drain()
                    nc.gpsimd.tensor_tensor(a, sq3[0][:, 0:span.n] if k == 1 else a, sq3[k % 2][:, 0:span.n], ALU.add
                                            ).then_inc(n["acc"].sem, 2 if k == 1 else 1)

            done = first + POOL_TURNS + 1
            for l, y in enumerate(layers):
                for stage, n, span in ((f"in_{l}", y["n_pre"], every), (f"up0_{l}", y["n_mpre"], span_of(l))):
                    lows(done, PLAN[stage].u0 + 2)
                    add_squares(n, span)
                    done = PLAN[stage].u0 + 2
            lows(done, UNITS)

        @block.tensor
        def _(pe):
            def passes(out, wslot, blk, hi, lo, first, last):
                wh, wl = whi[wslot][:, blk * P:(blk + 1) * P], wlo[wslot][:, blk * P:(blk + 1) * P]
                n = len(out)
                for o, h in zip(out, hi):
                    nc.tensor.matmul(o, wh, h, start=first, stop=False)
                for o, h in zip(out, lo):
                    nc.tensor.matmul(o, wh, h, start=False, stop=False)
                for j in range(n):
                    mm = nc.tensor.matmul(out[j], wl, hi[j], start=False, stop=last)
                return mm

            def claim(stage, i, s):
                hold(pe, lo_ready, stage.u0 + s + 1 + 2 * i, "pe")
                hold(pe, psum_free[stage.slot(s)], stage.used(i, s), "pe")

            def tile(stage, hi, lo, width, parts, s, m, ks, base=None, stride=None, first=0):
                slot = stage.slot(s)
                base = slot * 2 * parts if base is None else base
                out = [bank(base + m * parts + h, width) for h in range(parts)]
                for k in ks:
                    cs = [k * (stride or width * parts) + first + h * width for h in range(parts)]
                    mm = passes(out, slot, m * stage.nk + k, [hi[:, c:c + width] for c in cs],
                                [lo[:, c:c + width] for c in cs], k == 0, k == stage.nk - 1)
                if ks[-1] == stage.nk - 1:
                    mm.then_inc(tile0_done if m < stage.nm - 1 else unit_done, 1)

            def linear(stage, hi, lo, width, parts=1, ready=None, together=0, hooks=None, amid=None,
                       end=None, stride=None, first=0, begun=0, behind=0):
                hooks, amid, end = hooks or {}, amid or {}, end or stage.n
                all_k = range(stage.nk)

                def unit(i, s):
                    claim(stage, i, s)
                    for m in range(stage.nm):
                        if m and isinstance(i, int) and 2 * i + s in amid:
                            amid[2 * i + s]()
                        tile(stage, hi, lo, width, parts, s, m, all_k, None, stride, first)

                def early(units, ks):
                    for k in ks:
                        ready(k)
                        for s in units:
                            for m in range(stage.nm):
                                tile(stage, hi, lo, width, parts, s, m, [k], None, stride, first)

                straight = max([2 if ready else 0] + [u + 1 for u in (*hooks, *amid)])
                straight = min(straight + straight % 2, end)
                for u in range(begun, straight):
                    i, s = u // 2, u % 2
                    if ready and u == 0:
                        claim(stage, 0, 0)
                        if together:
                            claim(stage, 0, 1)
                            early((0, 1), range(together))
                        early((0,), range(together, behind or stage.nk))
                        if behind:
                            claim(stage, 0, 1)
                        for k in range(behind, stage.nk if behind else 0):
                            early((0,), [k])
                            early((1,), [k - behind])
                    elif (together or behind) and u == 1:
                        for m in range(stage.nm):
                            tile(stage, hi, lo, width, parts, 1, m, range(together or stage.nk - behind, stage.nk), None,
                                 stride, first)
                    else:
                        unit(i, s)
                    if u in hooks:
                        hooks[u]()
                if straight // 2 < end // 2:
                    with pe.Fori(straight // 2, end // 2) as i:
                        for s in range(2):
                            unit(i, s)
                if straight < end and end % 2:
                    unit(end // 2, 0)

            def mean(n, ready):
                pe.wait_ge(ready, KD)
                nc.tensor.matmul(bank(4), ones, acc1[:, :], start=True, stop=True).then_inc(n["pe"].sem, 1)

            def variance(n, pe_odd=True):
                for k in range(1, KD, 2) if pe_odd else ():
                    after(pe, n["act"], k + 1)
                    nc.tensor.matmul(bank(6), ones, sq1[1][:, :], start=(k == 1), stop=False).then_inc(n["pe"].sem, 1)
                after(pe, n["dve"], summed(pe_odd))
                nc.tensor.matmul(bank(6), ones, acc1[:, :], start=not pe_odd, stop=True).then_inc(n["pe"].sem, 1)

            def normed(n):
                return lambda k: after(pe, n["lo"], k + 1)

            def sum_squares(n, nk, b, span=every):
                after(pe, n["acc"], nk)
                w = span.width
                for h in range(span.parts):
                    mm = nc.tensor.matmul(bank(b + h, w), ones, acc2[:, h * w:(h + 1) * w], start=True, stop=True)
                mm.then_inc(n["pe"].sem, 1)

            def linear2(stage, hi, lo, span, *args, **more):
                linear(stage, hi, lo, span.width, span.parts, *args, **more)

            def unscaled(n, stage, span=every, end=None):
                slot = stage.slot(0)

                def sums():
                    pe.wait_ge(psum_free[slot], stage.used(0, 0) + 1)
                    sum_squares(n, KD, (slot * 2 + 1) * span.parts, span)

                linear2(stage, ahi, alo, span, normed(n), 4, {1: sums}, {2: lambda: after(pe, n["std"], 1)}, end,
                        stride=L, first=span.first)

            def free_banks(stage):
                for k in range(2):
                    pe.wait_ge(psum_free[stage.slot(k)], stage.used(0, k))

            pe.wait_ge(params_in, 48)
            mean(n_in, xin_ok)
            variance(n_in)
            pair = PLAN["dt"], PLAN["xbc"]
            for stage in pair:
                claim(stage, 0, 0)
            for k in range(KD):
                after(pe, n_in["lo"], k + 1)
                for stage in pair:
                    tile(stage, ahi, alo, T, 1, 0, 0, [k])
            tile(PLAN["xbc"], ahi, alo, T, 1, 0, 1, range(KD))

            def dt_tokens():
                pe.wait_ge(dt_ready, 2)
                for j, t in enumerate((dtt[6], dtt[5])):
                    for c in range(CHUNKS):
                        mm = nc.tensor.transpose(bank(4, 32, j * 128 + c * 32), t[0:32, c * P:(c + 1) * P],
                                                 const1[0:32, 0:32])
                mm.then_inc(dt_ps, 1)

            def chunk_ends():
                pe.wait_ge(dt_tok, 1)
                nc.tensor.matmul(bank(5, 128), last_row, tok[:, 0:128], start=True, stop=True).then_inc(end_ps, 1)

            linear(PLAN["xbc"], ahi, alo, T, begun=1, hooks={DT_AT - 1: dt_tokens, DT_AT + 1: chunk_ends})
            pe.wait_ge(ends_ok, 1)
            stage = PLAN["z_glu"]
            with pe.Fori(0, GROUPS) as g:
                def z_glu(u, m):
                    if m == 0:
                        claim(stage, 2 * g + u // 2, u % 2)
                    tile(stage, ahi, alo, T, 1, u % 2, m, range(KD), 4 + 2 * stage.slot(u % 2))

                def x_transposes(j):
                    hold(pe, x_ok, g * GP + (j + 1), "pe")
                    hold(pe, xdt_ok, g * GP + max(j - 1, 0), "pe")
                    for c in range(CHUNKS):
                        mm = nc.tensor.transpose(bank(j % 2, P, c * P), x_slot[j % 2][:, c * P:(c + 1) * P], ident)
                    mm.then_inc(xt_ps, 1)

                def head(q):
                    j, hh = q // 2, q % 2
                    if hh == 0:
                        hold(pe, y_ok, g * GP + max(j - 1, 0), "pe")
                    hold(pe, mc_ok, g * GH + (q + 1), "pe")
                    for c in range(CHUNKS):
                        o = PS[64 * hh:64 * hh + 64, (j % 2) * 512 + c * P:(j % 2) * 512 + (c + 1) * P]
                        mm = nc.tensor.matmul(o, xdt[:, c * T + q * 64:c * T + q * 64 + 64],
                                              m_slot[hh][:, c * P:(c + 1) * P], start=True, stop=(c == 0))
                        if c:
                            mm = nc.tensor.matmul(o, st[:, (c - 1) * T + q * 64:(c - 1) * T + q * 64 + 64],
                                                  c_slot[hh][:, c * P:(c + 1) * P], start=False, stop=True)
                    mm.then_inc(y_mm, 1)

                z_glu(0, 0)
                pe.wait_ge(conv4_out, XBCT)
                hold(pe, b_ok, g + 1, "pe")
                hold(pe, st_ok, g, "pe")
                for c in range(CHUNKS - 1):
                    mm = nc.tensor.transpose(bank(2, P, c * P), b_slot[:, c * P:(c + 1) * P], ident)
                mm.then_inc(bt_ps, 1)
                hold(pe, y_ok, g * GP, "pe")
                x_transposes(0)
                x_transposes(1)
                z_glu(0, 1)
                x_transposes(2)
                x_transposes(3)
                hold(pe, cbm_ok, g, "pe")
                for c in range(CHUNKS):
                    mm = nc.tensor.matmul(bank(3, P, c * P), b_slot[:, c * P:(c + 1) * P],
                                          cut(xbc, g * T + (CT0 * T + c * P), P), start=True, stop=True)
                mm.then_inc(cb_ps, 1)
                z_glu(1, 0)
                hold(pe, xds_ok, g + 1, "pe")
                hold(pe, bt_ok, g + 1, "pe")
                for c in range(CHUNKS - 1):
                    mm = nc.tensor.matmul(bank(c), bt_sb[:, c * P:(c + 1) * P], xds[:, c * T:(c + 1) * T],
                                          start=True, stop=True)
                mm.then_inc(st_ps, 1)
                z_glu(1, 1)
                hold(pe, st_ok, g + 1, "pe")
                head(0)
                head(1)
                z_glu(2, 0)
                head(2)
                head(3)
                z_glu(2, 1)
                head(4)
                head(5)
                z_glu(3, 0)
                head(6)
                head(7)
                z_glu(3, 1)

            pe.wait_ge(y_ok, XT)

            def group_sums():
                pe.wait_ge(ysq_sum, XT)
                pe.wait_ge(v_ok, KD)
                for g in range(GROUPS):
                    mm = nc.tensor.matmul(bank(4 + g), ones, sumsq[:, g * T:(g + 1) * T], start=True, stop=True)
                mm.then_inc(ss_ps, 1)

            def conv_variance():
                variance(n_conv, False)

            def conv_mean():
                pe.wait_ge(ss_std, GROUPS)
                mean(n_conv, vout_ok)

            linear(PLAN["gate_b"], ahi, alo, T, amid={2: group_sums})
            linear(PLAN["ssm_out"], yn_hi, yn_lo, T, ready=lambda k: pe.wait_ge(ylo_ok, k + 1), behind=XT // 2)
            linear(PLAN["gate_a"], ahi, alo, T, hooks={1: conv_mean, 2: conv_variance})
            linear(PLAN["conv_out"], chi, clo, T, ready=normed(n_conv))
            linear(PLAN["w_o"], mixhi, mixlo, T, ready=lambda k: pe.wait_ge(mixlo_ok, k + 1))
            mean(n_1, r1_ok)
            variance(n_1)
            linear(PLAN["ffn_up"], ahi, alo, T, ready=normed(n_1), together=4)

            stage = PLAN["ffn_down"]
            with pe.Fori(0, KD // 2) as i:
                for t in range(2):
                    hold(pe, psum_free[0], (stage.u0 + 1) // 2 + 2 * i + (t - 1), "pe")
                    for s in range(2):
                        slot = stage.slot(s)
                        hold(pe, lo_ready, stage.u0 + 4 * i + (2 * t + s + 1), "pe")
                        for k in range(FT // 2):
                            kk = s * (FT // 2) + k
                            if k in (0, FT // 2 - 2):
                                pe.wait_ge(flo_ok, kk + (FT // 2 - 2 if k == 0 else 2))
                            mm = passes([bank(4 + 2 * t)], slot, k, [fhi[:, kk * T:(kk + 1) * T]],
                                        [flo[:, kk * T:(kk + 1) * T]], kk == 0, kk == FT - 1)
                        mm.then_inc(unit_done, 1)
            mean(n_2, r2_ok)
            variance(n_2)

            for l, y in enumerate(layers):
                stage = PLAN[f"in_{l}"]
                unscaled(y["n_pre"], stage, end=3)
                span, n0 = span_of(l), first_step(l)
                near, far = stage.slot(1) * 4, stage.slot(0) * 4

                def part(u, m, ks=range(KD)):
                    if m == 0 and ks[0] == 0:
                        i, s = (u - 1) // 2, (u - 1) % 2
                        pe.wait_ge(lo_ready, stage.u0 + u + 1)
                        if u == 3:
                            pe.wait_ge(psum_free[stage.slot(1)], stage.used(0, 1) + 1)
                        else:
                            pe.wait_ge(psum_free[stage.slot(s)], stage.used(i, s) + 1)
                    tile(stage, ahi, alo, HALF, 2, u % 2, m, ks, near)

                def swap(j):
                    if j >= 2:
                        after(pe, y["rope_ok"], j - 1)
                    for h in range(2):
                        mm = nc.tensor.matmul(bank(far + 2 * (j % 2) + h, HALF), const2[:, 0:128],
                                              qraw[:, j * L + h * HALF:j * L + (h + 1) * HALF], start=True, stop=True)
                    mm.then_inc(y["swap_ps"].sem, 1)

                pe.wait_ge(psum_free[stage.slot(0)], stage.used(1, 0) + 1)
                pe.wait_ge(const2_in, 16 * (l + 1))
                swap(0)
                swap(1)
                part(3, 0)
                swap(2)
                swap(3)
                part(3, 1)
                swap(4)
                after(pe, y["rope_ok"], 4)
                after(pe, y["vch_ok"], 1)
                for b in range(NB):
                    mm = nc.tensor.transpose(bank(far + 2 + b // 4, P, (b % 4) * P), vch[:, (b + 1) * P:(b + 2) * P], ident)
                mm.then_inc(y["v_ps"].sem, 1)
                after(pe, y["rope_ok"], 5)

                def scores(n):
                    b, z = n // 2, n % 2
                    if n > n0:
                        after(pe, y["sc_ok"], n - n0)
                    k0 = WIN * keys(b)[0]
                    for j in range(4):
                        mm = nc.tensor.matmul(bank(far + j // 2, 256 - k0, (j % 2) * 256 + k0),
                                              qpad[64 * z:64 * z + 64, j * QPAD + b * WIN:j * QPAD + (b + 1) * WIN],
                                              kpad[64 * z:64 * z + 64, b * WIN + k0:(b + 2) * WIN], start=True, stop=True)
                    mm.then_inc(y["sc_ps"].sem, 1)

                def turn_p(n):
                    after(pe, y["p_ok"], n - n0 + 1)
                    if n > n0:
                        after(pe, y["o_ok"], n - n0)
                    else:
                        after(pe, y["v_ok"], 1)
                    if n >= n0 + 3 and n % 2:
                        after(pe, y["ya_ok"], (n - n0) // 2)
                    for kb in keys(n // 2):
                        for j in range(4):
                            mm = nc.tensor.transpose(bank(far + 2 + kb, P, j * P),
                                                     sc[n % 2][:, j * 256 + kb * P:j * 256 + (kb + 1) * P], ident)
                    mm.then_inc(y["pt_ps"].sem, 1)

                def outputs(n):
                    b, z = n // 2, n % 2
                    after(pe, y["pt_ok"], n - n0 + 1)
                    for j in range(4):
                        for kb in keys(b):
                            v0_ = (b + kb) * WIN + 64 * z
                            mm = nc.tensor.matmul(bank(far + 2, 64, j * 64),
                                                  pT[z][:, kb * 512 + j * P:kb * 512 + (j + 1) * P],
                                                  vtok[:, v0_:v0_ + 64], start=(kb == keys(b)[0]), stop=(kb == 1))
                    mm.then_inc(y["o_ps"].sem, 1)

                def turn_y(b):
                    after(pe, y["dg_ok"], b - n0 // 2 + 1)
                    for j in range(4):
                        mm = nc.tensor.matmul(bank(far + 3, P, j * P), y_tok[:, b * 512 + j * P:b * 512 + (j + 1) * P],
                                              diag[b % 2][:, :], start=True, stop=True)
                    mm.then_inc(y["yt_ps"].sem, 1)

                for n in range(STEPS):
                    u, m = 4 + n // 2, n % 2
                    if n > n0:
                        turn_p(n - 1)
                    if n >= n0:
                        scores(n)
                    part(u, m, range(KD // 2))
                    if n > n0:
                        outputs(n - 1)
                    part(u, m, range(KD // 2, 3 * KD // 4))
                    if n >= n0 + 3 and n % 2:
                        turn_y((n - 3) // 2)
                    part(u, m, range(3 * KD // 4, KD))
                turn_p(STEPS - 1)
                outputs(STEPS - 1)
                free_banks(PLAN[f"out_{l}"])
                sum_squares(y["n_conv"], 4, near)
                turn_y(NB - 1)
                after(pe, y["n_conv"]["std"], 1)
                after(pe, y["ya_ok"], NB - n0 // 2)

                def mixed(k):
                    after(pe, y["n_attn" if k < 4 else "n_conv"]["lo"], k % 4 + 1)

                stage = PLAN[f"out_{l}"]
                linear2(stage, ahi, alo, span, mixed, 4, stride=L, first=span.first)
                up = PLAN[f"up0_{l}"]
                free_banks(up)
                sum_squares(y["n_post"], KD, 0, span)
                unscaled(y["n_mpre"], up, span)
                for h in range(2):
                    if h:
                        linear2(PLAN[f"up{h}_{l}"], ahi, alo, span, stride=L, first=span.first)
                    f2lo_ok = y[f"f2lo_ok{h}"]
                    linear2(PLAN[f"down{h}_{l}"], f2hi, f2lo, span, lambda k: after(pe, f2lo_ok, k + 1))
                sum_squares(y["n_mpost"], KD, 0, span)

        @block.scalar
        def _(act):
            drain = nc.scalar.drain

            def split_first(u):
                act.wait_ge(raw_in[u % 2], 16 * (u // 2 + 1))
                nc.scalar.activation(whi[u % 2][:, :], raw[u % 2][:, :], ACT.Copy).then_inc(hi_ready, 1)

            def split_next(stage, i, s):
                if isinstance(i, int) and stage.u0 + 2 * i + s + 2 >= UNITS:
                    hold(act, unit_done, stage.u0 + s + 2 * i + 1, "act")
                    return
                slot = stage.slot(s)
                hold(act, unit_done, stage.u0 + s + 1 + 2 * i, "act")
                hold(act, raw_in[slot], 16 * i + 16 * ((stage.u0 + s) // 2 + 2), "act")
                nc.scalar.activation(whi[slot][:, :], raw[slot][:, :], ACT.Copy).then_inc(hi_ready, 1)

            def evacuate(stage, body, first=0, end=None):
                def unit(i, s):
                    split_next(stage, i, s)
                    body(i, s, stage.slot(s))
                unit_loop(act, stage, unit, first, end)

            def ln_squares(n, src, beside=None, pe_odd=True):
                for k in range(KD):
                    if beside and k in beside:
                        beside[k]()
                    after(act, n["dve"], centred(k, pe_odd))
                    if pe_odd and k % 2 and k > 1:
                        after(act, n["pe"], 1 + k // 2)
                    nc.scalar.activation(sq1[k % 2][:, :], src[:, k * T:(k + 1) * T], ACT.Square).then_inc(n["act"].sem, 1)

            def ln_std(n, pe_odd=True):
                after(act, n["pe"], 2 + (KD // 2 if pe_odd else 0))
                nc.scalar.activation(std[:, 0:T], bank(6), ACT.Sqrt, bias=col("eps5", 0), scale=1.0 / D
                                     ).then_inc(n["act"].sem, 1)

            def ln_out(n, src, g, b, func, dst, hi, tiles=range(KD), pe_odd=True):
                for k in tiles:
                    after(act, n["dve"], summed(pe_odd) + k + 1)
                    nc.scalar.activation(dst(k), src[:, k * T:(k + 1) * T], func, bias=col(b, k), scale=col(g, k))
                    if hi is not None:
                        drain()
                        nc.scalar.activation(hi[:, k * T:(k + 1) * T], dst(k), ACT.Copy).then_inc(n["hi"].sem, 1)
                    else:
                        drain()
                        fold(layers[0]["n_pre"], "mix_pre_0", k)

            def square(n, k, src, span=every):
                if k >= 2:
                    after(act, n["acc"], k - 1)
                dst = sq3[k % 2][:, 0:span.n]
                nc.scalar.activation(dst if src.shape == dst.shape else split2(dst), src, ACT.Square).then_inc(n["sq"].sem, 1)

            def root(n, nk, b, span=every):
                after(act, n["pe"], 1)
                nc.scalar.activation(span.fit(std[:, 0:span.n]), span.psum(b), ACT.Sqrt, bias=col("eps6", 0),
                                     scale=1.0 / (nk * P)).then_inc(n["std"].sem, 1)

            def fold(n, g, k, span=every):
                t = span.of(hres, k)
                nc.scalar.activation(span.of(ahi, k), t, ACT.Copy, scale=col(g, k)).then_inc(n["hi"].sem, 1)
                square(n, k, t, span)

            act.wait_ge(params_in, 48)
            ln_squares(n_in, x_in, {2: lambda: split_first(0), 4: lambda: split_first(1)})
            ln_std(n_in)
            ln_out(n_in, x_in, "ln_in_g", "ln_in_b", ACT.Identity, lambda k: x_in[:, k * T:(k + 1) * T], ahi)

            stage = PLAN["dt"]
            split_next(stage, 0, 0)
            nc.scalar.activation(dtt[0][:, :], bank(0, parts=32), ACT.Identity, bias=heads[:, 0:1]
                                 ).then_inc(psum_free[0], 1)

            def dt_exponential():
                drain()
                nc.scalar.activation(dtt[1][:, :], dtt[0][:, :], ACT.Abs)
                nc.scalar.activation(heads[:, 2:3], heads[:, 1:2], ACT.Exp)
                drain()
                nc.scalar.activation(dtt[2][:, :], dtt[1][:, :], ACT.Exp, scale=-1.0).then_inc(dt_exp, 1)

            stage = PLAN["xbc"]

            def xbc_unit(i, s, slot):
                for m in range(2):
                    k = 4 * i + (2 * s + m)
                    nc.scalar.activation(cut(xbc, 2048 * i + (2 * s + m) * T, T), bank(2 * slot + m), ACT.Identity,
                                         bias=col("ssm_b", k), scale=col("ssm_w", 4 * k + 3)).then_inc(conv4_acc, 1)
                for m in range(2):
                    if m == 0:
                        hold(act, conv4_tap, 2 * i + (s + 1), "act")
                    else:
                        hold(act, psum_free[slot], stage.used(i, s) + 1, "act")
                    tile = cut(xbc, 2048 * i + (2 * s + m) * T, T)
                    nc.scalar.activation(tile, tile, ACT.Silu).then_inc(conv4_out, 1)

            evacuate(stage, xbc_unit, 0, 2)
            dt_exponential()
            evacuate(stage, xbc_unit, 2, DT_AT)
            act.wait_ge(dt_ready, 2)
            act.dma_start(acs_d[0:32, :], dtt[6][:, :]).then_inc(scratch_in, 16)
            act.dma_start(acs_d[32:34, :], dtt[6][0:2, :]).then_inc(scratch_in, 16)
            act.wait_ge(dt_ps, 1)
            nc.scalar.activation(tok[:, :], bank(4, 256), ACT.Copy).then_inc(dt_tok, 1)
            evacuate(stage, xbc_unit, DT_AT, DT_AT + 2)
            act.wait_ge(end_in, 1)
            nc.scalar.activation(ends[:, 0:128], ends[:, 0:128], ACT.Exp)
            nc.scalar.activation(ends[:, 128:256], bank(5, 128), ACT.Exp)
            drain().then_inc(ends_ok, 1)
            evacuate(stage, xbc_unit, DT_AT + 2, XBCT // 2 - 2)

            act.wait_ge(scratch_in, 32)
            for s in range(2):
                act.dma_start(acs_b[s][:, :], acs_d[s, :].partition_broadcast(P)).then_inc(acs_in[s], 16)

            def x_copy(g, j):
                nc.scalar.activation(x_slot[j % 2][:, :], cut(xbc, g * (GP * T) + j * T, T), ACT.Copy).then_inc(x_ok, 1)

            def group_start(g):
                nc.scalar.activation(b_slot[:, :], cut(xbc, g * T + BT0 * T, T), ACT.Copy).then_inc(b_ok, 1)
                for j in range(2):
                    x_copy(g, j)

            drain()
            group_start(0)
            evacuate(stage, xbc_unit, XBCT // 2 - 2)
            stage = PLAN["z_glu"]
            with act.Fori(0, GROUPS) as g:
                def z_unit(u):
                    slot = stage.slot(u % 2)
                    hold(act, yg_ok, g * GP, "act")
                    for m in range(2):
                        if m == 0:
                            hold(act, tile0_done, 4 * g + (stage.z0 + u + 1), "act")
                        else:
                            hold(act, unit_done, 4 * g + (stage.u0 + u + 1), "act")
                        o = nc.scalar.activation(zs[u // 2 * 2 + m][:, :], bank(4 + 2 * slot + m), ACT.Silu)
                    o.then_inc(psum_free[slot], 1)
                    drain().then_inc(zs_ok, 1)

                def glu_unit(u):
                    slot = stage.slot(u % 2)
                    split_next(stage, 2 * g + u // 2, u % 2)
                    hold(act, v_ok, 2 * g, "act")
                    nc.scalar.activation(sig[u // 2][:, 0:T], bank(4 + 2 * slot + 1), ACT.Sigmoid).then_inc(sig_ok, 1)

                def head(q):
                    s = q % 2
                    hold(act, acs_in[s], 16 * (GH // 2) * g + 16 * (q // 2 + 1), "act")
                    if q == 0:
                        hold(act, xt_ps, g * GP + GP, "act")
                    if q >= 2:
                        hold(act, y_mm, g * GH + (q - 1), "act")
                    for c in range(CHUNKS):
                        cs = slice(c * CHUNK, (c + 1) * CHUNK)
                        nc.scalar.activation(m_slot[s][:, cs], acs_b[s][:, cs], ACT.Relu,
                                             bias=tok[:, bass.ds(g * GH + (c * 32 + q), 1)], scale=-1.0)
                    drain()
                    nc.scalar.activation(m_slot[s][:, :], m_slot[s][:, :], ACT.Exp, scale=-1.0)
                    nc.scalar.activation(c_slot[s][:, :], acs_b[s][:, :], ACT.Exp)
                    drain().then_inc(exp_ok, 1)
                    act.dma_start(acs_b[s][:, :], acs_d[bass.ds(g * GH + (q + 2), 1), :].rearrange("a t -> (a t)")
                                  .partition_broadcast(P)).then_inc(acs_in[s], 16)

                hold(act, bt_ps, g + 1, "act")
                hold(act, st_ps, g, "act")
                nc.scalar.activation(bt_sb[:, 0:384], bank(2, 384), ACT.Copy).then_inc(bt_ok, 1)
                for j in (2, 3):
                    hold(act, xt_ps, g * GP + (j - 1), "act")
                    x_copy(g, j)
                glu_unit(0)
                head(0)
                head(1)
                z_unit(1)
                nc.scalar.activation(rstd[:, 0:1], ident[:, 0:1], ACT.Exp, scale=0.0)
                head(2)
                head(3)
                split_next(stage, 2 * g, 1)
                head(4)
                head(5)
                split_next(stage, 2 * g + 1, 0)
                head(6)
                head(7)
                z_unit(2)
                hold(act, cb_ps, g + 1, "act")
                hold(act, y_mm, g * GH + GH, "act")
                group_start(g + 1)
                glu_unit(3)
            for s in range(2):
                act.wait_ge(acs_in[s], 16 * (HEADS // 2 + 1))

            def y_squares(first, end):
                with act.Fori(first // 2, end // 2) as i:
                    for m in range(2):
                        hold(act, ysq_sum, 2 * i, "act")
                        nc.scalar.activation(ysq[m][:, :], cut(xbc, 2 * T * i + m * T, T), ACT.Square
                                             ).then_inc(ysq_ok, 1)

            def gate(stage, u, dst):
                split_next(stage, u // 2, u % 2)
                slot = stage.slot(u % 2)
                for m in range(2):
                    o = nc.scalar.activation(dst[:, (2 * u + m) * T:(2 * u + m + 1) * T], bank(2 * slot + m), ACT.Sigmoid)
                o.then_inc(psum_free[slot], 1)

            def y_high(tiles):
                for k in tiles:
                    act.wait_ge(y_normed, k + 1)
                    nc.scalar.activation(yn_hi[:, k * T:(k + 1) * T], xbc[:, k * T:(k + 1) * T], ACT.Copy
                                         ).then_inc(yhi_ok, 1)

            stage = PLAN["gate_b"]
            act.wait_ge(yg_ok, XT)
            y_squares(0, XT // 2)
            gate(stage, 0, gb)
            y_squares(XT // 2, XT)
            gate(stage, 1, gb)
            act.wait_ge(ss_ps, 1)
            for g in range(GROUPS):
                nc.scalar.activation(rst4[:, g * T:(g + 1) * T], bank(4 + g), ACT.Sqrt, bias=col("eps5", 0),
                                     scale=1.0 / (GP * P)).then_inc(ss_std, 1)
            def products(ns, start=0):
                for n in ns:
                    if not isinstance(start, int) or n >= POOL_TAPS:
                        hold(act, prod_used, start + (n - POOL_TAPS + 1), "act")
                    tap = start + (n + 1)
                    nc.scalar.activation(prod[n % POOL_TAPS][:, :], cut(vpad, tap + POOL_TILE * VW, T), ACT.Copy,
                                         scale=col("conv_w", tap + POOL_TILE * TAPS)).then_inc(prod_ok, 1)

            nc.scalar.activation(vout[:, POOL_TILE * T:(POOL_TILE + 1) * T], vpad[:, POOL_TILE * VW:POOL_TILE * VW + T],
                                 ACT.Identity, bias=col("conv_b", POOL_TILE), scale=col("conv_w", POOL_TILE * TAPS)
                                 ).then_inc(vout_first, 1)
            gate(stage, 2, gb)
            y_high(range(0, GP))
            gate(stage, 3, gb)
            y_high(range(GP, 2 * GP))
            products(range(0, POOL_TAPS))
            y_high(range(2 * GP, 3 * GP))
            early = 2 * POOL_TAPS - 1
            products(range(POOL_TAPS, early))
            y_high(range(3 * GP, XT))

            def ssm_out_unit(i, s, slot):
                hold(act, ring_used, 2 * i, "act")
                nc.scalar.activation(ring[s][:, :], bank(2 * slot), ACT.Copy).then_inc(psum_free[slot], 1)
                drain().then_inc(ring_ok, 1)

            def ssm_out_unit_tap(i, s, slot):
                ssm_out_unit(i, s, slot)
                products(range(early + s * POOL_TAPS, early + (s + 1) * POOL_TAPS), 2 * POOL_TAPS * i)

            stage = PLAN["ssm_out"]
            evacuate(stage, ssm_out_unit_tap, 0, POOL_TURNS - 2)
            products(range(POOL_TURNS * POOL_TAPS - 1, POOL_TURNS * POOL_TAPS))
            evacuate(stage, ssm_out_unit, POOL_TURNS - 2, stage.n)

            stage = PLAN["gate_a"]
            conv_out = (vout, "conv_ln_g", "conv_ln_b", ACT.Silu, lambda k: vout[:, k * T:(k + 1) * T], chi)
            gate(stage, 0, ga)
            gate(stage, 1, ga)
            ln_squares(n_conv, vout, pe_odd=False)
            gate(stage, 2, ga)
            ln_std(n_conv, False)
            ln_out(n_conv, *conv_out, range(0, 4), False)
            gate(stage, 3, ga)
            ln_out(n_conv, *conv_out, range(4, KD), False)

            def mix_unit(i, s, slot):
                for m in range(2):
                    hold(act, mix_ok, 4 * i + (2 * s + m + 1), "act")
                    c = 2048 * i + (2 * s + m) * T
                    nc.scalar.activation(cut(mixhi, c, T), cut(gb, c, T), ACT.Copy).then_inc(mixhi_ok, 1)

            evacuate(PLAN["conv_out"], mix_unit)
            evacuate(PLAN["w_o"], lambda i, s, slot: None)
            ln_squares(n_1, res1)
            ln_std(n_1)
            ln_out(n_1, res1, "ln1_g", "ln1_b", ACT.Identity, lambda k: res1[:, k * T:(k + 1) * T], ahi)

            stage_u = PLAN["ffn_up"]

            def up_unit(i, s, slot):
                for m in range(2):
                    k = 2 * i + (s + m * FT)
                    hold(act, flo_ok, 2 * i, "act")
                    nc.scalar.activation(fg[s][m][:, :], bank(2 * slot + m), ACT.Identity, bias=col("ffn_b", k),
                                         scale=col("ffn_w", 3 * k + 2)).then_inc(fa_ok, 1)
                hold(act, ft_ok, 2 * i + (s + 1), "act")
                nc.scalar.activation(fg[s][0][:, :], fg[s][0][:, :], ACT.Silu).then_inc(fs_ok, 1)
                hold(act, ff_ok, 2 * i + (s + 1), "act")
                nc.scalar.activation(cut(fhi, 2 * T * i + s * T, T), fg[s][1][:, :], ACT.Copy).then_inc(fhi_ok, 1)

            evacuate(stage_u, up_unit)
            stage_d = PLAN["ffn_down"]
            act.wait_ge(flo_ok, FT)
            evacuate(stage_d, lambda i, s, slot: None)
            act.dma_start(hres[:, :].rearrange("p (k t) -> p k t", k=KD)[:, :, 0:META], metaT).then_inc(meta_in, 16)
            act.wait_ge(meta_in, 16)
            hview = [hres[:, k * L + META:(k + 1) * L] for k in range(KD)]
            ln_squares(n_2, res2)
            ln_std(n_2)
            ln_out(n_2, res2, "ln2_g", "ln2_b", ACT.Identity, lambda k: hview[k], None)

            for l, y in enumerate(layers):
                if l:
                    for k in range(KD):
                        after(act, layers[l - 1]["n_mpost"]["dve"], k + 1)
                        fold(y["n_pre"], f"mix_pre_{l}", k)
                after(act, y["pad_ok"], 1)
                act.dma_start(const2[:, :], const2_d).then_inc(const2_in, 16)
                stage = PLAN[f"in_{l}"]
                near, far = stage.slot(1) * 4, stage.slot(0) * 4
                span, n0 = span_of(l), first_step(l)

                for u in range(3):
                    slot = stage.slot(u % 2)
                    act.wait_ge(unit_done, stage.u0 + u + 1)
                    for m in range(2):
                        j = 2 * u + m
                        dst = qraw[:, j * L:(j + 1) * L] if j < 5 else vch[:, WIN + LEAD:KPAD]
                        o = nc.scalar.activation(split2(dst), wide(slot * 4 + 2 * m), ACT.Copy)
                    o.then_inc(psum_free[slot], 1)
                    split_next(stage, u // 2, u % 2)
                    if u == 1:
                        root(y["n_pre"], KD, far + 2)
                split_next(stage, 1, 1)
                after(act, y["v_ps"], 1)
                nc.scalar.activation(vtok[:, P:KPAD], PS[:, (far + 2) * 512:(far + 2) * 512 + NB * P], ACT.Copy
                                     ).then_inc(y["v_ok"].sem, 1)

                def exps(n):
                    z = n % 2
                    after(act, y["neg_ok"], n - n0 + 1)
                    for j in range(4):
                        p = sc[z][:, j * 256 + WIN * keys(n // 2)[0]:(j + 1) * 256]
                        nc.scalar.activation(p, p, ACT.Exp, bias=small[:, 8 * z + j:8 * z + j + 1],
                                             accum_out=small[:, 16 + 8 * z + j:17 + 8 * z + j])
                    nc.scalar.activation(small[:, 32 + 8 * z:36 + 8 * z], small[:, 32 + 8 * z:36 + 8 * z], ACT.Exp)
                    drain().then_inc(y["p_ok"].sem, 1)

                def turned_p(n):
                    after(act, y["pt_ps"], n - n0 + 1)
                    if n >= n0 + 2:
                        after(act, y["o_ps"], n - n0 - 1)
                    k0 = 512 * keys(n // 2)[0]
                    nc.scalar.activation(pT[n % 2][:, k0:1024], PS[:, (far + 2) * 512 + k0:(far + 4) * 512], ACT.Copy
                                         ).then_inc(y["pt_ok"].sem, 1)

                def token_rms(b):
                    after(act, y["o_ok"], 2 * b + 2 - n0)
                    nc.scalar.activation(nv[0][:, 0:512], y_tok[:, b * 512:(b + 1) * 512], ACT.Square,
                                         accum_out=small[:, 48 + b:49 + b])
                    drain()
                    nc.scalar.activation(small[:, 48 + b:49 + b], small[:, 48 + b:49 + b], ACT.Sqrt, bias=col("eps6", 0),
                                         scale=1.0 / 512).then_inc(y["astd_ok"].sem, 1)

                def turned_y(b):
                    after(act, y["yt_ps"], b - n0 // 2 + 1)
                    t0_, skip = max(b * WIN - LEAD, 0), LEAD if b == 0 else 0
                    for j in range(4):
                        o = nc.scalar.activation(ya[:, j * L + t0_:j * L + t0_ + WIN - skip],
                                                 bank(far + 3, WIN - skip, j * P + skip), ACT.Copy,
                                                 scale=col(f"attn_g_{l}", j))
                    o.then_inc(y["ya_ok"].sem, 1)

                def conv_square(j):
                    after(act, y["yc_ok"], j + 1)
                    square(y["n_conv"], j, yconv[:, j * L:(j + 1) * L])

                for n in range(STEPS):
                    if n > n0:
                        turned_p(n - 1)
                    if n >= n0:
                        exps(n)
                    if n >= n0 + 2 and n % 2 == 0:
                        token_rms(n // 2 - 1)
                    if n >= n0 + 3 and n % 2:
                        turned_y((n - 3) // 2)
                    if n == STEPS - 2:
                        conv_square(0)
                        conv_square(1)
                    if n % 2:
                        split_next(stage, (4 + n // 2) // 2, n // 2 % 2)
                conv_square(2)
                turned_p(STEPS - 1)
                conv_square(3)
                token_rms(NB - 1)
                root(y["n_conv"], 4, near)
                turned_y(NB - 1)
                drain()
                for k in range(4):
                    nc.scalar.activation(span.of(ahi, k), span.of(ya, k), ACT.Copy
                                         ).then_inc(y["n_attn"]["hi"].sem, 1)
                for k in range(4):
                    after(act, y["n_conv"]["dve"], k + 1)
                    nc.scalar.activation(ahi[:, (4 + k) * L:(5 + k) * L], nv[k % 2][:, :], ACT.Copy
                                         ).then_inc(y["n_conv"]["hi"].sem, 1)

                stage = PLAN[f"out_{l}"]

                def out_unit(i, s, slot):
                    for m in range(2):
                        k = 2 * (2 * i + s) + m
                        square(y["n_post"], k, span.tile(slot, m), span)
                        o = nc.scalar.activation(span.fit(span.of(zres, k)), span.tile(slot, m), ACT.Copy)
                    o.then_inc(psum_free[slot], 1)

                for u in range(stage.n - 1):
                    split_next(stage, u // 2, u % 2)
                    out_unit(u // 2, u % 2, stage.slot(u % 2))
                u = stage.n - 1
                act.wait_ge(unit_done, stage.u0 + u + 1)
                out_unit(u // 2, u % 2, stage.slot(u % 2))
                split_next(stage, u // 2, u % 2)
                root(y["n_post"], KD, 0, span)
                for k in range(KD):
                    after(act, y["n_post"]["dve"], k + 1)
                    fold(y["n_mpre"], f"mlp_pre_{l}", k, span)

                W = span.n
                for h in range(2):
                    stage = PLAN[f"up{h}_{l}"]
                    rl_ok, f_ok, f2hi_ok, f2lo_ok = (y[f"{a}{h}"] for a in ("rl_ok", "f_ok", "f2hi_ok", "f2lo_ok"))

                    def relus(i, s, slot):
                        for m in range(2):
                            hold(act, f2lo_ok, 4 * i, "act")
                            nc.scalar.activation(span.fit(rl[2 * s + m][:, 0:W]), span.tile(slot, m), ACT.Relu
                                                 ).then_inc(rl_ok.sem, 1)
                        drain().then_inc(psum_free[slot], 1)

                    def highs(i, s):
                        for m in range(2):
                            hold(act, f_ok, 4 * i + (2 * s + m + 1), "act")
                            nc.scalar.activation(cut(f2hi, 4 * W * i + (2 * s + m) * W, W), rl[2 * s + m][:, 0:W], ACT.Copy
                                                 ).then_inc(f2hi_ok.sem, 1)

                    for s in range(2):
                        split_next(stage, 0, s)
                        relus(0, s, stage.slot(s))
                    if h == 0:
                        root(y["n_mpre"], KD, (stage.slot(0) * 2 + 1) * span.parts, span)
                    for s in range(2):
                        highs(0, s)
                    with act.Fori(1, stage.n // 2) as i:
                        for s in range(2):
                            split_next(stage, i, s)
                            relus(i, s, stage.slot(s))
                            highs(i, s)
                    stage = PLAN[f"down{h}_{l}"]
                    if h == 0:
                        def copy_unit(i, s, slot):
                            nc.scalar.activation(span.fit(cut(zres, 2 * L * i + (s * L + span.first), W)), span.tile(slot, 0),
                                                 ACT.Copy
                                                 ).then_inc(psum_free[slot], 1)

                        evacuate(stage, copy_unit)
                        drain().then_inc(y["zc_ok"].sem, 1)
                    else:
                        for u in range(stage.n):
                            if u < stage.n - 1:
                                split_next(stage, u // 2, u % 2)
                            after(act, y["dn_ok1"], u + 1)
                            square(y["n_mpost"], u, span.of(zres, u), span)
                        split_next(stage, (stage.n - 1) // 2, (stage.n - 1) % 2)
                root(y["n_mpost"], KD, 0, span)

        @block.vector
        def _(dve):
            drain = nc.vector.drain
            v = nc.vector

            def tap(acc, ps, w, sh, n=T):
                return v.scalar_tensor_tensor(acc[:, sh:n], ps[:, 0:n - sh], w, acc[:, sh:n], ALU.mult, ALU.add)

            def layer_norm(n, src, hi, lo, each=None, pe_odd=True):
                after(dve, n["pe"], 1)
                for k in range(KD + 1):
                    if k < KD:
                        t = src[:, k * T:(k + 1) * T]
                        v.scalar_tensor_tensor(t, bank(4), -1.0 / D, t, ALU.mult, ALU.add).then_inc(n["dve"].sem, 1)
                    if k == 1:
                        after(dve, n["act"], 1)
                        v.tensor_copy(acc1[:, :], sq1[0][:, :]).then_inc(n["dve"].sem, 1)
                    elif k > 1 and (k % 2 or not pe_odd):
                        after(dve, n["act"], k)
                        drain()
                        v.tensor_tensor(acc1[:, :], acc1[:, :], sq1[(k - 1) % 2][:, :], ALU.add).then_inc(n["dve"].sem, 1)
                after(dve, n["act"], KD + 1)
                v.reciprocal(rstd[:, 0:T], std[:, 0:T])
                drain()

                def low(k):
                    after(dve, n["hi"], k + 1)
                    c = slice(k * T, (k + 1) * T)
                    v.tensor_tensor(lo[:, c], src[:, c], hi[:, c].bitcast(F32), ALU.subtract).then_inc(n["lo"].sem, 1)

                for k in range(KD):
                    t = src[:, k * T:(k + 1) * T]
                    v.tensor_tensor(t, t, rstd[:, 0:T], ALU.mult).then_inc(n["dve"].sem, 1)
                    if each is not None:
                        each(k)
                    if hi is not None and k >= 2:
                        low(k - 2)
                if hi is not None:
                    low(KD - 2)
                    low(KD - 1)

            def add_up(tile, done):
                drain()
                v.tensor_tensor(acc1[:, :], acc1[:, :], tile, ALU.add).then_inc(done, 1)

            def lows(n, k, src, first, span=every):
                after(dve, n["hi"], k + 1)
                v.tensor_tensor(span.of(alo, first + k), src, span.of(ahi, first + k).bitcast(F32), ALU.subtract
                                ).then_inc(n["lo"].sem, 1)

            def add_square(n, k, span=every):
                after(dve, n["sq"], k + 1)
                drain()
                a, q = acc2[:, 0:span.n], sq3[k % 2][:, 0:span.n]
                if k == 0:
                    v.tensor_copy(a, q).then_inc(n["acc"].sem, 1)
                else:
                    v.tensor_tensor(a, a, q, ALU.add).then_inc(n["acc"].sem, 1)

            def fold(n, g, k, span):
                after(dve, n["hi"], k + 1)
                v.scalar_tensor_tensor(span.of(alo, k), span.of(hres, k), col(g, k), span.of(ahi, k).bitcast(F32),
                                       ALU.mult, ALU.subtract).then_inc(n["lo"].sem, 1)

            def row_scale(n, span=every):
                after(dve, n["std"], 1)
                v.reciprocal(rstd[:, 0:span.n], std[:, 0:span.n])
                drain()

            def residual(n, g, span, each):
                row_scale(n, span)
                for k in range(KD):
                    t, h = span.of(zres, k), span.of(hres, k)
                    v.scalar_tensor_tensor(t, t, col(g, k), rstd[:, 0:span.n], ALU.mult, ALU.mult)
                    drain()
                    v.tensor_tensor(h, h, t, ALU.add).then_inc(n["dve"].sem, 1)
                    each(k)

            def folding(n, g, span=every):
                def each(k):
                    if k:
                        fold(n, g, k - 1, span)
                    if k == KD - 1:
                        fold(n, g, k, span)
                return each

            v.memset(acc1[:, :], 0.0)
            for k in range(KD):
                dve.wait_ge(x_in_s[k * X_PARTS // KD], 16)
                add_up(x_in[:, k * T:(k + 1) * T], xin_ok)
            layer_norm(n_in, x_in, ahi, alo)

            stage = PLAN["xbc"]

            def xbc_unit(i, s):
                slot = stage.slot(s)
                for m in range(2):
                    k = 4 * i + (2 * s + m)
                    hold(dve, conv4_acc, 4 * i + (2 * s + m + 1), "dve")
                    c = 2048 * i + (2 * s + m) * T
                    for w in (2, 1, 0):
                        sh = 3 - w
                        o = v.scalar_tensor_tensor(cut(xbc, c + sh, T - sh), bank(2 * slot + m, T - sh),
                                                   col("ssm_w", 4 * k + w), cut(xbc, c + sh, T - sh),
                                                   ALU.mult, ALU.add)
                        if w:
                            drain()
                    o.then_inc(conv4_tap if m == 0 else psum_free[slot], 1)

            x_, e_, r_, s_, s2, q_, acs, dt_ = dtt[0], dtt[2], dtt[3], dtt[4], dtt[1], dtt[7], dtt[6], dtt[5]

            def dt_ratio():
                dve.wait_ge(dt_exp, 1)
                v.tensor_scalar(r_[:, :], e_[:, :], 2.0, None, ALU.add)
                drain()
                v.reciprocal(s_[:, :], r_[:, :])
                drain()
                v.tensor_tensor(s_[:, :], s_[:, :], e_[:, :], ALU.mult)
                drain()
                v.tensor_tensor(s2[:, :], s_[:, :], s_[:, :], ALU.mult)
                drain()
                v.tensor_scalar(q_[:, :], s2[:, :], 1.0 / 15, None, ALU.mult)

            def dt_series():
                for d in (13, 11, 9, 7, 5, 3):
                    drain()
                    v.scalar_tensor_tensor(q_[:, :], q_[:, :], 1.0 / d, s2[:, :], ALU.add, ALU.mult)

            def dt_sums():
                drain()
                v.scalar_tensor_tensor(q_[:, :], q_[:, :], 1.0, s_[:, :], ALU.add, ALU.mult)
                v.tensor_scalar(x_[:, :], x_[:, :], 0.0, None, ALU.max)
                drain()
                v.scalar_tensor_tensor(dt_[:, :], q_[:, :], 2.0, x_[:, :], ALU.mult, ALU.add).then_inc(dt_ready, 1)
                drain()
                v.tensor_scalar(r_[:, :], dt_[:, :], heads[:, 2:3], -1.0, ALU.mult, ALU.mult)
                drain()
                for c in range(CHUNKS):
                    cs = slice(c * CHUNK, (c + 1) * CHUNK)
                    o = v.tensor_tensor_scan(acs[:, cs], const1[0:32, 128:256], r_[:, cs], 0.0, ALU.mult, ALU.add)
                o.then_inc(dt_ready, 1)

            unit_loop(dve, stage, xbc_unit, 0, 2)
            dt_ratio()
            xbc_unit(1, 0)
            dt_series()
            xbc_unit(1, 1)
            dt_sums()
            unit_loop(dve, stage, xbc_unit, 4, DT_AT + 2)
            dve.wait_ge(end_ps, 1)
            v.scalar_tensor_tensor(ends[:, 0:128], tok[:, 0:128], -1.0, bank(5, 128), ALU.mult, ALU.add
                                   ).then_inc(end_in, 1)
            unit_loop(dve, stage, xbc_unit, DT_AT + 2)

            dve.wait_ge(ends_ok, 1)
            dve.wait_ge(conv4_out, XBCT)
            dve.wait_ge(scratch_in, 32)
            v3 = vpad[:, :].rearrange("p (k t) -> p k t", k=KD)
            v.memset(v3[:, :, 0:TAPS - 1], 0.0)
            stage = PLAN["z_glu"]

            odd = [u for u in range(1, KD, 2) if u != POOL_TILE]

            def long_taps(tiles, a, b, start=None):
                for w in range(a, b) if start is None else [start + k for k in range(a, b)]:
                    drain()
                    for u in tiles:
                        src, acc = cut(vpad, u * VW + w, T), cut(vout, u * T, T)
                        wc = col("conv_w", u * TAPS + w)
                        if isinstance(w, int) and w == 0:
                            v.tensor_scalar(acc, src, wc, col("conv_b", u), ALU.mult, ALU.add)
                        else:
                            v.scalar_tensor_tensor(acc, src, wc, acc, ALU.mult, ALU.add)

            with dve.Fori(0, GROUPS) as g:
                def y_out(j):
                    hold(dve, y_mm, g * GH + 2 * (j + 1), "dve")
                    t = cut(xbc, g * (GP * T) + j * T, T)
                    v.scalar_tensor_tensor(t, t, col("ssm_d", g * GP + j), bank(j % 2), ALU.mult, ALU.add
                                           ).then_inc(y_ok, 1)

                def glu(h):
                    slot = stage.slot(h)
                    hold(dve, sig_ok, 2 * g + (h + 1), "dve")
                    v.tensor_tensor(cut(vpad, 2 * VW * g + (h * VW + TAPS - 1), T), bank(4 + 2 * slot), sig[h][:, 0:T],
                                    ALU.mult).then_inc(psum_free[slot], 1)
                    drain().then_inc(v_ok, 1)

                xdt3 = xdt[:, :].rearrange("p (c n) -> p c n", c=CHUNKS)
                for j in range(GP):
                    hold(dve, xt_ps, g * GP + (j + 1), "dve")
                    for hh in range(2):
                        o = v.tensor_tensor(
                            xdt3[:, :, j * P + hh * 64:j * P + (hh + 1) * 64],
                            bank(j % 2).rearrange("p (c n) -> p c n", c=CHUNKS)[:, :, hh * 64:(hh + 1) * 64],
                            tok[:, 128:256].rearrange("p (c h) -> p c h", c=CHUNKS)[:, :, bass.ds(g * GH + (2 * j + hh), 1)]
                            .to_broadcast([P, CHUNKS, HEAD_P]), ALU.mult)
                    o.then_inc(xdt_ok, 1)
                drain()
                for c in range(CHUNKS - 1):
                    o = v.tensor_tensor(xds[:, c * T:(c + 1) * T].rearrange("p (h n) -> p h n", h=GH),
                                        xdt[:, c * T:(c + 1) * T].rearrange("p (h n) -> p h n", h=GH),
                                        ends[:, bass.ds(g * GH + c * 32, GH)].unsqueeze(2).to_broadcast([P, GH, HEAD_P]),
                                        ALU.mult)
                o.then_inc(xds_ok, 1)
                hold(dve, cb_ps, g + 1, "dve")
                v.tensor_tensor(cbm[:, :].rearrange("p (c t) -> p c t", c=CHUNKS),
                                bank(3).rearrange("p (c t) -> p c t", c=CHUNKS),
                                causal.unsqueeze(1).to_broadcast([P, CHUNKS, P]), ALU.mult).then_inc(cbm_ok, 1)
                glu(0)
                long_taps([2 * g], *TAPS_AT[0:2])
                hold(dve, st_ps, g + 1, "dve")
                v.tensor_copy(st[:, 0:T], bank(0))
                for c in range(1, CHUNKS - 1):
                    drain()
                    v.tensor_tensor(st[:, c * T:(c + 1) * T].rearrange("p (h n) -> p h n", h=GH),
                                    st[:, (c - 1) * T:c * T].rearrange("p (h n) -> p h n", h=GH),
                                    ends[:, bass.ds(g * GH + (128 + c * 32), GH)].unsqueeze(2)
                                    .to_broadcast([P, GH, HEAD_P]), ALU.mult)
                    drain()
                    o = v.tensor_tensor(st[:, c * T:(c + 1) * T], st[:, c * T:(c + 1) * T], bank(c), ALU.add)
                o.then_inc(st_ok, 1)

                for q in range(GH):
                    s = q % 2
                    hold(dve, exp_ok, g * GH + (q + 1), "dve")
                    v.tensor_tensor(c_slot[s][:, :], c_slot[s][:, :], cut(xbc, g * T + CT0 * T, T), ALU.mult)
                    v.tensor_tensor(m_slot[s][:, :], m_slot[s][:, :], cbm[:, :], ALU.mult).then_inc(mc_ok, 1)
                    if q % 2 and q > 1:
                        y_out(q // 2 - 1)
                    long_taps([2 * g], *TAPS_AT[q + 1:q + 3])
                y_out(GP - 1)
                long_taps([2 * g], TAPS_AT[-1], TAPS)
                glu(1)

            for s in range(2):
                dve.wait_ge(acs_in[s], 16 * (HEADS // 2 + 1))

            with dve.Fori(0, GROUPS) as g:
                acc = cut(sumsq, T * g, T)
                for j in range(GP):
                    hold(dve, ysq_ok, GP * g + (j + 1), "dve")
                    if j == 0:
                        v.tensor_copy(acc, ysq[0][:, :]).then_inc(ysq_sum, 1)
                    else:
                        drain()
                        v.tensor_tensor(acc, acc, ysq[j % 2][:, :], ALU.add).then_inc(ysq_sum, 1)

            long_taps(odd, 0, TAPS_GATE)

            def y_low(k):
                dve.wait_ge(yhi_ok, k + 1)
                c = slice(k * T, (k + 1) * T)
                v.tensor_tensor(yn_lo[:, c], xbc[:, c], yn_hi[:, c].bitcast(F32), ALU.subtract).then_inc(ylo_ok, 1)

            for k in range(XT):
                c = slice(k * T, (k + 1) * T)
                if k % GP == 0:
                    g = slice(k // GP * T, (k // GP + 1) * T)
                    dve.wait_ge(ss_std, k // GP + 1)
                    v.reciprocal(rst4[:, g], rst4[:, g])
                    drain()
                v.scalar_tensor_tensor(xbc[:, c], xbc[:, c], col("ssm_norm", k), rst4[:, k // GP * T:(k // GP + 1) * T],
                                       ALU.mult, ALU.mult).then_inc(y_normed, 1)
                if k >= 2:
                    y_low(k - 2)
            y_low(XT - 2)
            y_low(XT - 1)

            v.memset(acc1[:, :], 0.0)
            for u in range(0, KD, 2):
                add_up(vout[:, u * T:(u + 1) * T], vout_ok)
            n = (TAPS - TAPS_GATE) // 4
            assert 4 * n + TAPS_GATE == TAPS
            with dve.Fori(0, KD // 2) as i:
                long_taps(odd, 0, n, n * i + TAPS_GATE)
                for s in range(2):
                    hold(dve, ring_ok, 2 * i + (s + 1), "dve")
                    t = cut(gb, 2 * T * i + s * T, T)
                    v.tensor_tensor(t, t, ring[s][:, :], ALU.mult).then_inc(ring_used, 1)
            drain()
            for u in odd:
                add_up(vout[:, u * T:(u + 1) * T], vout_ok)
            dve.wait_ge(prod_used, POOL_TURNS * POOL_TAPS)
            long_taps([POOL_TILE], POOL_ENDS, TAPS)
            add_up(vout[:, POOL_TILE * T:(POOL_TILE + 1) * T], vout_ok)
            layer_norm(n_conv, vout, chi, clo, pe_odd=False)

            stage_c = PLAN["conv_out"]

            def mix_unit(i, s):
                slot = stage_c.slot(s)
                g = stage_c.u0 + s + 1
                for m in range(2):
                    c = 2048 * i + (2 * s + m) * T
                    if m == 0:
                        hold(dve, tile0_done, 2 * i + (stage_c.z0 + s + 1), "dve")
                    else:
                        hold(dve, unit_done, 2 * i + g, "dve")
                    o = v.tensor_tensor(cut(ga, c, T), cut(ga, c, T), bank(2 * slot + m), ALU.mult)
                    if m == 1:
                        o.then_inc(psum_free[slot], 1)
                    drain()
                    v.tensor_tensor(cut(gb, c, T), cut(gb, c, T), cut(ga, c, T), ALU.add).then_inc(mix_ok, 1)
                for m in range(2):
                    c = 2048 * i + (2 * s + m) * T
                    hold(dve, mixhi_ok, 4 * i + (2 * s + m + 1), "dve")
                    v.tensor_tensor(cut(mixlo, c, T), cut(gb, c, T), cut(mixhi, c, T).bitcast(F32), ALU.subtract
                                    ).then_inc(mixlo_ok, 1)

            unit_loop(dve, stage_c, mix_unit)

            stage_w = PLAN["w_o"]

            def w_o_unit(i, s):
                slot = stage_w.slot(s)
                for m in range(2):
                    c = 2048 * i + (2 * s + m) * T
                    if m == 0:
                        hold(dve, tile0_done, 2 * i + (stage_w.z0 + s + 1), "dve")
                    else:
                        hold(dve, unit_done, 2 * i + (stage_w.u0 + s + 1), "dve")
                    o = v.scalar_tensor_tensor(cut(res1, c, T), cut(ahi, c, T).bitcast(F32), ALPHA,
                                               bank(2 * slot + m), ALU.mult, ALU.add)
                    if m == 1:
                        o.then_inc(psum_free[slot], 1)
                    drain()
                    v.scalar_tensor_tensor(cut(res1, c, T), cut(alo, c, T).bitcast(F32), ALPHA, cut(res1, c, T),
                                           ALU.mult, ALU.add)
                    add_up(cut(res1, c, T), r1_ok)

            v.memset(acc1[:, :], 0.0)
            unit_loop(dve, stage_w, w_o_unit)
            layer_norm(n_1, res1, ahi, alo)

            stage_u = PLAN["ffn_up"]

            def up_unit(i, s):
                slot = stage_u.slot(s)
                for m in range(2):
                    k = 2 * i + (s + m * FT)
                    hold(dve, fa_ok, 4 * i + (2 * s + m + 1), "dve")
                    tap(fg[s][m], bank(2 * slot + m), col("ffn_w", 3 * k + 1), 1)
                    drain()
                    tap(fg[s][m], bank(2 * slot + m), col("ffn_w", 3 * k), 2).then_inc(
                        ft_ok if m == 0 else psum_free[slot], 1)
                drain()
                hold(dve, fs_ok, 2 * i + (s + 1), "dve")
                v.tensor_tensor(fg[s][1][:, :], fg[s][1][:, :], fg[s][0][:, :], ALU.mult).then_inc(ff_ok, 1)
                hold(dve, fhi_ok, 2 * i + (s + 1), "dve")
                c = 2 * T * i + s * T
                v.tensor_tensor(cut(flo, c, T), fg[s][1][:, :], cut(fhi, c, T).bitcast(F32), ALU.subtract
                                ).then_inc(flo_ok, 1)

            unit_loop(dve, stage_u, up_unit)
            stage_d = PLAN["ffn_down"]
            v.memset(acc1[:, :], 0.0)
            with dve.Fori(0, KD // 2) as i:
                for t in range(2):
                    c = 2 * T * i + t * T
                    hold(dve, unit_done, 4 * i + (stage_d.u0 + 2 * t + 2), "dve")
                    v.scalar_tensor_tensor(cut(res2, c, T), cut(ahi, c, T).bitcast(F32), ALPHA, bank(4 + 2 * t),
                                           ALU.mult, ALU.add).then_inc(psum_free[0], 1)
                    drain().then_inc(psum_free[1], 1)
                    v.scalar_tensor_tensor(cut(res2, c, T), cut(alo, c, T).bitcast(F32), ALPHA, cut(res2, c, T),
                                           ALU.mult, ALU.add)
                    add_up(cut(res2, c, T), r2_ok)
            layer_norm(n_2, res2, None, None, folding(layers[0]["n_pre"], "mix_pre_0"))

            for l, y in enumerate(layers):
                v.memset(qpad[:, :].rearrange("p (j t) -> p j t", j=4)[:, :, 0:LEAD], 0.0)
                v.memset(kpad[:, 0:WIN + LEAD], 0.0)
                v.memset(vch[:, 0:WIN + LEAD], 0.0)
                v.memset(vtok[:, 0:P], 0.0)
                for s in range(2):
                    v.memset(upad[s][:, 0:2], 0.0)
                drain().then_inc(y["pad_ok"].sem, 1)
                stage = PLAN[f"in_{l}"]
                near, far = stage.slot(1) * 4, stage.slot(0) * 4
                span, n0 = span_of(l), first_step(l)
                w2 = f"conv2_w_{l}"
                row_scale(y["n_pre"])
                v.tensor_tensor(rstd_sq[:, :], rstd[:, :], rstd[:, :], ALU.mult)
                dve.wait_ge(const2_in, 16 * (l + 1))
                cos, sin = (const2[:, CONST2[a]:CONST2[a] + L] for a in ("cos", "sin"))
                for t in (cos, sin):
                    v.tensor_tensor(t, t, rstd[:, :], ALU.mult)

                def rope(j):
                    after(dve, y["swap_ps"], j + 1)
                    raw_t = qraw[:, j * L:(j + 1) * L]
                    dst = qpad[:, j * QPAD + LEAD:(j + 1) * QPAD] if j < 4 else kpad[:, WIN + LEAD:KPAD]
                    drain()
                    v.tensor_tensor(split2(rot[:, 0:L]), split2(sin), wide(far + 2 * (j % 2)), ALU.mult)
                    v.tensor_tensor(rot[:, L:2 * L], raw_t, cos, ALU.mult)
                    drain()
                    v.tensor_tensor(dst, rot[:, 0:L], rot[:, L:2 * L], ALU.add).then_inc(y["rope_ok"].sem, 1)

                def c_gate(j):
                    dve.wait_ge(tile0_done, stage.z0 + 4 + j)
                    drain()
                    v.tensor_tensor(split2(cgate[j % 2][:, :]), wide(near), split2(rstd_sq[:, :]), ALU.mult)

                def gated(j):
                    dve.wait_ge(unit_done, stage.u0 + 4 + j)
                    drain()
                    v.tensor_tensor(split2(upad[j % 2][:, 2:2 + L]), wide(near + 2), split2(cgate[j % 2][:, :]), ALU.mult
                                    ).then_inc(psum_free[stage.slot((3 + j) % 2)], 1)

                def conv(j):
                    acc, up_ = yconv[:, j * L:(j + 1) * L], upad[j % 2]
                    drain()
                    v.tensor_scalar(acc, up_[:, 0:L], col(w2, 3 * j), None, ALU.mult)
                    for w in (1, 2):
                        drain()
                        v.scalar_tensor_tensor(acc, up_[:, w:w + L], col(w2, 3 * j + w), acc, ALU.mult, ALU.add)
                    drain()
                    v.tensor_tensor(acc, acc, rstd[:, :], ALU.mult)

                def b_gate(j):
                    u, m = 7 + j // 2, j % 2
                    if m == 0:
                        dve.wait_ge(tile0_done, stage.z0 + u + 1)
                    else:
                        dve.wait_ge(unit_done, stage.u0 + u + 1)
                    acc = split2(yconv[:, j * L:(j + 1) * L])
                    drain()
                    v.tensor_tensor(acc, acc, wide(near + 2 * m), ALU.mult).then_inc(y["yc_ok"].sem, 1)
                    if m:
                        drain().then_inc(psum_free[stage.slot(u % 2)], 1)

                dve.wait_ge(psum_free[stage.slot(0)], stage.used(1, 0) + 1)
                vt = vch[:, WIN + LEAD:KPAD]
                v.tensor_tensor(vt, vt, rstd[:, :], ALU.mult).then_inc(y["vch_ok"].sem, 1)
                rope(0)
                rope(1)
                c_gate(0)
                rope(2)
                rope(3)
                gated(0)
                rope(4)
                conv(0)

                sinks = f"sinks_{l}"

                def softmax(n):
                    b, z = n // 2, n % 2
                    after(dve, y["sc_ps"], n - n0 + 1)
                    if n >= n0 + 2:
                        after(dve, y["pt_ps"], n - n0 - 1)
                    drain()
                    k0 = WIN * keys(b)[0]
                    s3 = sc[z][:, :].rearrange("p (j k) -> p j k", j=4)[:, :, k0:256]
                    mask = const2[:, CONST2["mask"] + b * 256 + k0:CONST2["mask"] + (b + 1) * 256]
                    v.scalar_tensor_tensor(s3, PS[:, far * 512:(far + 2) * 512].rearrange("p (j k) -> p j k", j=4)[:, :, k0:256],
                                           0.125, mask.unsqueeze(1).to_broadcast([P, 4, 256 - k0]), ALU.mult, ALU.add
                                           ).then_inc(y["sc_ok"].sem, 1)
                    drain()
                    m_, se = small[:, 8 * z:8 * z + 4], small[:, 32 + 8 * z:36 + 8 * z]
                    sink = cols[:, COLS[sinks][0] + 4 * z:COLS[sinks][0] + 4 * z + 4]
                    v.tensor_reduce(m_, s3, AX_X, ALU.max)
                    drain()
                    v.tensor_tensor(m_, m_, sink, ALU.max)
                    drain()
                    v.tensor_tensor(se, sink, m_, ALU.subtract)
                    v.tensor_scalar(m_, m_, -1.0, None, ALU.mult)
                    drain().then_inc(y["neg_ok"].sem, 1)

                def output(n):
                    b, z = n // 2, n % 2
                    den = small[:, 16 + 8 * z:20 + 8 * z]
                    after(dve, y["p_ok"], n - n0 + 1)
                    v.tensor_tensor(den, den, small[:, 32 + 8 * z:36 + 8 * z], ALU.add)
                    drain()
                    v.reciprocal(den, den)
                    after(dve, y["o_ps"], n - n0 + 1)
                    drain()
                    o3 = y_tok[:, b * 512:(b + 1) * 512].rearrange("p (j n) -> p j n", j=4)[:, :, 64 * z:64 * z + 64]
                    v.tensor_tensor(o3, bank(far + 2, 256).rearrange("p (j n) -> p j n", j=4),
                                    den.unsqueeze(2).to_broadcast([P, 4, 64]), ALU.mult).then_inc(y["o_ok"].sem, 1)

                def token_scale(b):
                    after(dve, y["astd_ok"], b - n0 // 2 + 1)
                    if b >= n0 // 2 + 2:
                        after(dve, y["yt_ps"], b - n0 // 2 - 1)
                    v.reciprocal(small[:, 56 + b:57 + b], small[:, 48 + b:49 + b])
                    drain()
                    v.tensor_scalar(diag[b % 2][:, :], ident, small[:, 56 + b:57 + b], None, ALU.mult
                                    ).then_inc(y["dg_ok"].sem, 1)

                for n in range(STEPS):
                    u, m = 4 + n // 2, n % 2
                    if n >= n0:
                        softmax(n)
                    if n > n0:
                        output(n - 1)
                    if n and m == 0 and u <= 7:
                        conv(u - 4)
                    if n >= n0 + 3 and m:
                        token_scale((n - 3) // 2)
                    if u >= 7:
                        b_gate(2 * (u - 7) + m)
                    elif m == 0:
                        c_gate(u - 3)
                    else:
                        gated(u - 3)
                    if n == STEPS - 2:
                        add_square(y["n_conv"], 0)
                        add_square(y["n_conv"], 1)
                add_square(y["n_conv"], 2)
                add_square(y["n_conv"], 3)
                output(STEPS - 1)
                token_scale(NB - 1)
                row_scale(y["n_conv"])

                def conv_normed(k):
                    v.scalar_tensor_tensor(nv[k % 2][:, :], yconv[:, k * L:(k + 1) * L], col(f"conv_g_{l}", k), rstd[:, :],
                                           ALU.mult, ALU.mult).then_inc(y["n_conv"]["dve"].sem, 1)

                conv_normed(0)
                conv_normed(1)
                for k in range(4):
                    lows(y["n_attn"], k, span.of(ya, k), 0, span)
                for k in range(4):
                    lows(y["n_conv"], k, nv[k % 2][:, :], 4)
                    if k < 2:
                        drain()
                        conv_normed(k + 2)

                for k in range(KD):
                    add_square(y["n_post"], k, span)
                residual(y["n_post"], f"mix_post_{l}", span, folding(y["n_mpre"], f"mlp_pre_{l}", span))
                row_scale(y["n_mpre"], span)
                W = span.n
                for h in range(2):
                    stage = PLAN[f"up{h}_{l}"]
                    rl_ok, f_ok, f2hi_ok, f2lo_ok = (y[f"{a}{h}"] for a in ("rl_ok", "f_ok", "f2hi_ok", "f2lo_ok"))

                    def up_body(i, s):
                        for m in range(2):
                            hold(dve, rl_ok, 4 * i + (2 * s + m + 1), "dve")
                            r = rl[2 * s + m][:, 0:W]
                            v.tensor_tensor(r, r, rstd[:, 0:W], ALU.mult)
                            drain()
                            v.tensor_tensor(r, r, r, ALU.mult).then_inc(f_ok.sem, 1)
                        for m in range(2):
                            c = 4 * W * i + (2 * s + m) * W
                            hold(dve, f2hi_ok, 4 * i + (2 * s + m + 1), "dve")
                            v.tensor_tensor(cut(f2lo, c, W), rl[2 * s + m][:, 0:W], cut(f2hi, c, W).bitcast(F32),
                                            ALU.subtract).then_inc(f2lo_ok.sem, 1)

                    unit_loop(dve, stage, up_body)
                stage = PLAN[f"down1_{l}"]
                after(dve, y["zc_ok"], 1)
                for u in range(stage.n):
                    slot = stage.slot(u % 2)
                    dve.wait_ge(unit_done, stage.u0 + u + 1)
                    t = span.fit(span.of(zres, u))
                    v.tensor_tensor(t, t, span.tile(slot, 0), ALU.add).then_inc(psum_free[slot], 1)
                    drain().then_inc(y["dn_ok1"].sem, 1)
                    if u:
                        add_square(y["n_mpost"], u - 1, span)
                add_square(y["n_mpost"], KD - 1, span)
                if l + 1 < LAYERS:
                    residual(y["n_mpost"], f"mlp_post_{l}", span, folding(layers[l + 1]["n_pre"], f"mix_pre_{l + 1}"))
                else:
                    residual(y["n_mpost"], f"mlp_post_{l}", span, lambda k: None)


def _tiles(v):
    return np.asarray(v, np.float32).reshape(-1, P).T


def _blocks(w):
    k, n = w.shape
    return w.reshape(k // P, P, n // P, P).transpose(0, 2, 1, 3)


def _stream(i):
    s = np.zeros((UNITS, P, 16, P), np.float32)

    def put(stage, u, tiles):
        for n, b in enumerate(tiles):
            s[PLAN[stage].u0 + u, :, n, :] = b

    w_in = i["w_in"][0]
    o = np.cumsum([0, 2 * D, SSM, XBC, HEADS, D, D])
    glu, z, xbc = (_blocks(w_in[:, o[j]:o[j + 1]]) for j in range(3))
    gate_a, gate_b = (_blocks(w_in[:, o[j]:o[j + 1]]) for j in (4, 5))
    dt = np.zeros((D, P), np.float32)
    dt[:, 0:HEADS] = w_in[:, o[3]:o[4]]
    put("dt", 0, _blocks(dt)[:, 0])

    def pairs(stage, b, order=None):
        order = list(range(b.shape[1])) if order is None else order
        for u in range(len(order) // 2):
            put(stage, u, [b[k, m] for m in order[2 * u:2 * u + 2] for k in range(b.shape[0])])

    def singles(stage, b):
        for m in range(b.shape[1]):
            put(stage, m, [b[k, m] for k in range(b.shape[0])])

    pairs("xbc", xbc)
    for g in range(GROUPS):
        for h in range(2):
            j = 2 * g + h
            tiles = [glu[k, m] for m in (j, KD + j) for k in range(KD)], [z[k, m] for m in (2 * j, 2 * j + 1)
                                                                          for k in range(KD)]
            put("z_glu", 2 * j, tiles[h])
            put("z_glu", 2 * j + 1, tiles[1 - h])
    pairs("gate_b", gate_b)
    singles("ssm_out", _blocks(i["w_ssm_out"][0]))
    pairs("gate_a", gate_a)
    pairs("conv_out", _blocks(i["w_conv_out"][0]))
    pairs("w_o", _blocks(i["w_o"][0]))
    pairs("ffn_up", _blocks(i["w_ffn_up"][0]), [t for j in range(FT) for t in (j, FT + j)])
    down = _blocks(i["w_ffn_down"][0])
    for m in range(KD):
        for h in range(2):
            put("ffn_down", 2 * m + h, [down[h * (FT // 2) + k, m] for k in range(FT // 2)])
    for l in range(LAYERS):
        w = i["w_in_2"][l]
        q = w[:, 0:512].reshape(D, 2, 4, 64).transpose(0, 2, 1, 3).reshape(D, 512)
        w = _blocks(np.concatenate([q, w[:, 512:]], axis=1))
        pairs(f"in_{l}", w, [0, 1, 2, 3, 4, 5] + [t for j in range(4) for t in (10 + j, 14 + j)] + [6, 7, 8, 9])
        w = i["w_out_2"][l]
        a = w[0:512].reshape(2, 4, 64, D).transpose(1, 0, 2, 3).reshape(512, D)
        pairs(f"out_{l}", _blocks(np.concatenate([a, w[512:]], axis=0)))
        up, down = _blocks(i["w_up_2"][l]), _blocks(i["w_down_2"][l])
        for h in range(2):
            pairs(f"up{h}_{l}", up[:, h * FFH:(h + 1) * FFH])
            singles(f"down{h}_{l}", down[h * FFH:(h + 1) * FFH])
    return s.reshape(UNITS, P, UNIT)


def _columns(i):
    def taps(w):
        k, c = w.shape
        return w.reshape(k, c // P, P).transpose(2, 1, 0).reshape(P, -1)

    c = {
        "ln_in_g": _tiles(i["ln_in_g"]), "ln_in_b": _tiles(i["ln_in_b"]), "conv_w": taps(i["conv_dw_w"][0]),
        "conv_b": _tiles(i["conv_dw_b"][0]), "conv_ln_g": _tiles(i["conv_ln_g"][0]),
        "conv_ln_b": _tiles(i["conv_ln_b"][0]), "ssm_w": taps(i["ssm_conv_w"][0]), "ssm_b": _tiles(i["ssm_conv_b"][0]),
        "ssm_d": _tiles(np.repeat(i["ssm_d"][0], HEAD_P)), "ssm_norm": _tiles(i["ssm_norm_w"][0]),
        "ln1_g": _tiles(i["ln1_g"][0]), "ln1_b": _tiles(i["ln1_b"][0]), "ffn_w": taps(i["ffn_dw_w"][0]),
        "ffn_b": _tiles(i["ffn_dw_b"][0]), "ln2_g": _tiles(i["ln2_g"][0]), "ln2_b": _tiles(i["ln2_b"][0]),
        "eps5": np.full((P, 1), 1e-5, np.float32), "eps6": np.full((P, 1), 1e-6, np.float32),
    }
    for l in range(LAYERS):
        c[f"mix_pre_{l}"] = _tiles(i["mix_pre_g_2"][l])
        c[f"conv2_w_{l}"] = taps(i["conv_w_2"][l])
        c[f"attn_g_{l}"] = _tiles(i["attn_out_g_2"][l].reshape(2, 4, 64).transpose(1, 0, 2).reshape(512))
        c[f"conv_g_{l}"] = _tiles(i["conv_out_g_2"][l])
        c[f"mix_post_{l}"] = _tiles(i["mix_post_g_2"][l])
        c[f"mlp_pre_{l}"] = _tiles(i["mlp_pre_g_2"][l])
        c[f"mlp_post_{l}"] = _tiles(i["mlp_post_g_2"][l])
        c[f"sinks_{l}"] = np.broadcast_to(i["sinks_2"][l].reshape(1, QH), (P, QH))
    return np.ascontiguousarray(np.concatenate([c[n] for n in COLS], axis=1))


def _constants():
    c1 = np.zeros((P, N1), np.float32)
    c1[:, 0:128] = np.eye(P)
    c1[:, 128:256] = 1.0
    s, t = np.arange(P)[:, None], np.arange(P)[None, :]
    c1[:, 256:384] = t >= s
    c1[P - 1, 384:512] = 1.0
    c2 = np.zeros((P, N2), np.float32)
    cos, sin = np.ones((P, L), np.float32), np.zeros((P, L), np.float32)
    half = ROT // 2
    inv = np.power(np.float32(THETA), -np.arange(0, ROT, 2, dtype=np.float32) / np.float32(ROT)).astype(np.float32)
    ang = (np.arange(L, dtype=np.float32)[:, None] * inv[None, :]).astype(np.float32)
    for h in range(2):
        for r in range(half):
            a, b = 64 * h + r, 64 * h + half + r
            c2[b, a] = -1.0
            c2[a, b] = 1.0
            cos[a] = cos[b] = np.cos(ang[:, r])
            sin[a] = sin[b] = np.sin(ang[:, r])
    c2[:, CONST2["cos"]:CONST2["cos"] + L] = cos
    c2[:, CONST2["sin"]:CONST2["sin"] + L] = sin
    kk = np.arange(2 * WIN)[None, :]
    for b in range(NB):
        key = b * WIN + kk
        ok = (kk <= s + WIN) & (kk > s) & (key >= WIN + LEAD)
        c2[:, CONST2["mask"] + b * 256:CONST2["mask"] + (b + 1) * 256] = np.where(ok, 0.0, NEG)
    return c1, c2


def kernel(**inputs):
    import concourse.bacc as _bacc
    from concourse.bass_utils import run_bass_kernel_spmd as _run

    i = {k: np.asarray(v) for k, v in inputs.items()}
    nc = _bacc.Bacc("TRN2", target_bir_lowering=False, num_devices=1, dynamic_dma_scratch_size=1024)
    c1, c2 = _constants()
    arrays = {
        "x_t": np.ascontiguousarray(i["x"][0].T.reshape(KD, P, T).transpose(1, 0, 2)),
        "meta_t": np.ascontiguousarray(i["meta_tokens_2"].T.reshape(KD, P, META).transpose(1, 0, 2)),
        "weights": _stream(i),
        "columns": _columns(i),
        "head_params": np.ascontiguousarray(np.stack([i["ssm_dt_bias"][0], i["ssm_a_log"][0]], axis=1)),
        "const1": c1,
        "const2": c2,
    }
    d = {n: nc.dram_tensor(n, a.shape, F32, kind="ExternalInput").ap() for n, a in arrays.items()}
    acs = nc.dram_tensor("acs_rows", (HEADS + 2, T), F32, kind="Internal").ap()
    out = nc.dram_tensor("out_t", (P, KD, T), F32, kind="ExternalOutput").ap()
    build(nc, d["x_t"].rearrange("p k t -> p (k t)"), d["meta_t"], d["weights"], d["columns"], d["head_params"],
          d["const1"], d["const2"], acs, out)
    r = _run(nc, [arrays], core_ids=[0])
    o = np.asarray(r.results[0]["out_t"])
    return np.ascontiguousarray(o.transpose(2, 1, 0).reshape(1, T, D))
```
